# Optimizing a Trainium2 kernel written in Bass

```python
import math
import jax, jax.numpy as jnp
from jax import lax
import numpy as np

D_MODEL = 1024
BATCH = 1
SEQ = 512
DEPTH = 1

MIX_WIDTH = D_MODEL
ATTN_WIDTH = D_MODEL // 2
HGRN_WIDTH = MIX_WIDTH - ATTN_WIDTH
DIFF_HEADS = 4
DIFF_VDIM = ATTN_WIDTH // DIFF_HEADS
DIFF_QK = DIFF_VDIM // 2
Q_BLOCK = 128
HGRN_HEADS = 4
HGRN_DIM = HGRN_WIDTH // HGRN_HEADS
HGRN_CHUNK = 64
PEER_HEADS = 8
N_KEYS = 128
N_EXPERTS = N_KEYS * N_KEYS
PEER_TOPK = 16
PEER_QDIM = 256
PEER_QHALF = PEER_QDIM // 2
PEER_TOKEN_BLOCK = 128
N_MOD = 6
EPS = 1e-6
SPLIT_SIZES = [DIFF_HEADS * 2 * DIFF_QK, DIFF_HEADS * 2 * DIFF_QK, ATTN_WIDTH,
               HGRN_WIDTH, HGRN_WIDTH, HGRN_WIDTH, HGRN_WIDTH]
IN_COLS = sum(SPLIT_SIZES)
SPLIT_POINTS = [int(v) for v in np.cumsum(SPLIT_SIZES)[:-1]]

kernel_name = "hybrid_diffattn_hgrn2_peer_block"

def rmsnorm(x, g):
    xf = x.astype(jnp.float32)
    y = xf * lax.rsqrt(jnp.mean(xf * xf, axis=-1, keepdims=True) + EPS)
    return (y * g.astype(jnp.float32)).astype(x.dtype)

def diff_attention(q, k, v, lam):
    B, H, _, S, d = q.shape
    nblk = S // Q_BLOCK
    scale = 1.0 / math.sqrt(d)
    qb = q.reshape(B, H, 2, nblk, Q_BLOCK, d).transpose(3, 0, 1, 2, 4, 5)
    kpos = jnp.arange(S)
    vf = v.astype(jnp.float32)

    def one_block(args):
        qi, i = args
        s = jnp.einsum('bhjqd,bhjkd->bhjqk', qi, k).astype(jnp.float32) * scale
        qpos = i * Q_BLOCK + jnp.arange(Q_BLOCK)
        mask = kpos[None, :] <= qpos[:, None]
        s = jnp.where(mask, s, -jnp.inf)
        p = jax.nn.softmax(s, axis=-1)
        a = p[:, :, 0] - lam * p[:, :, 1]
        return jnp.einsum('bhqk,bhkv->bhqv', a, vf)

    out = lax.map(one_block, (qb, jnp.arange(nblk)))
    return out.transpose(1, 2, 0, 3, 4).reshape(B, H, S, v.shape[-1])

def hgrn2_chunkwise(q, k, v, logf):
    B, H, S, dk = q.shape
    dv = v.shape[-1]
    C = HGRN_CHUNK
    n = S // C

    def to_chunks(t):
        return t.reshape(B, H, n, C, t.shape[-1]).transpose(2, 0, 1, 3, 4)

    qc, kc, vc, gc = to_chunks(q), to_chunks(k), to_chunks(v.astype(jnp.float32)), to_chunks(logf)
    bc = jnp.cumsum(gc, axis=-2)
    causal = jnp.tril(jnp.ones((C, C), dtype=bool))[..., None]

    def step(state, inp):
        q_, k_, v_, b_ = inp
        diff = b_[..., :, None, :] - b_[..., None, :, :]
        decay = jnp.exp(jnp.where(causal, diff, -jnp.inf))
        attn = jnp.einsum('bhtk,bhtsk,bhsk->bhts', q_, decay, k_)
        o_intra = jnp.einsum('bhts,bhsv->bhtv', attn, v_)
        o_inter = jnp.einsum('bhtk,bhkv->bhtv', q_ * jnp.exp(b_), state)
        b_last = b_[..., -1:, :]
        new_state = (jnp.exp(b_last[..., 0, :])[..., None] * state
                     + jnp.einsum('bhsk,bhsv->bhkv', k_ * jnp.exp(b_last - b_), v_))
        return new_state, o_intra + o_inter

    state0 = jnp.zeros((B, H, dk, dv), jnp.float32)
    _, ys = lax.scan(step, state0, (qc, kc, vc, bc))
    return ys.transpose(1, 2, 0, 3, 4).reshape(B, H, S, dv)

def hybrid_mixer(h, w_in, lam_qk, g_diff_sub, lb, g_hgrn_out, w_out, lam_init):
    B, S, _ = h.shape
    proj = h @ w_in
    aq, ak, av, hq, hf, hi, hg = jnp.split(proj, SPLIT_POINTS, axis=-1)

    aq = aq.reshape(B, S, DIFF_HEADS, 2, DIFF_QK).transpose(0, 2, 3, 1, 4)
    ak = ak.reshape(B, S, DIFF_HEADS, 2, DIFF_QK).transpose(0, 2, 3, 1, 4)
    av = av.reshape(B, S, DIFF_HEADS, DIFF_VDIM).transpose(0, 2, 1, 3)
    lq = lam_qk.astype(jnp.float32)
    lam = jnp.exp(jnp.sum(lq[0] * lq[1])) - jnp.exp(jnp.sum(lq[2] * lq[3])) + lam_init
    ao = diff_attention(aq, ak, av, lam)
    ao = rmsnorm(ao, g_diff_sub) * (1.0 - lam_init)
    ao = ao.transpose(0, 2, 1, 3).reshape(B, S, ATTN_WIDTH)

    def heads(t):
        return t.reshape(B, S, HGRN_HEADS, HGRN_DIM).transpose(0, 2, 1, 3)
    lbf = lb.astype(jnp.float32)
    f = lbf + (1.0 - lbf) * jax.nn.sigmoid(hf.astype(jnp.float32))
    logf = jnp.log(f)
    kk = 1.0 - f
    qh = jax.nn.silu(hq.astype(jnp.float32))
    ho = hgrn2_chunkwise(heads(qh), heads(kk), heads(hi), heads(logf))
    ho = rmsnorm(ho, g_hgrn_out).transpose(0, 2, 1, 3).reshape(B, S, HGRN_WIDTH)
    ho = ho * jax.nn.silu(hg.astype(jnp.float32))

    cat = jnp.concatenate([ao.astype(jnp.float32), ho], axis=-1).astype(h.dtype)
    return cat @ w_out

def peer(h, w_pq, sub_keys, expert_u, expert_v):
    B, S, D = h.shape
    q = (h @ w_pq).reshape(B, S, PEER_HEADS, 2, PEER_QHALF)
    s = jnp.einsum('bshjd,hjnd->bshjn', q, sub_keys).astype(jnp.float32)
    v1, i1 = lax.top_k(s[..., 0, :], PEER_TOPK)
    v2, i2 = lax.top_k(s[..., 1, :], PEER_TOPK)
    cand = (v1[..., :, None] + v2[..., None, :]).reshape(B, S, PEER_HEADS, PEER_TOPK * PEER_TOPK)
    cidx = (i1[..., :, None] * N_KEYS + i2[..., None, :]).reshape(B, S, PEER_HEADS, PEER_TOPK * PEER_TOPK)
    top_s, pos = lax.top_k(cand, PEER_TOPK)
    idx = jnp.take_along_axis(cidx, pos, axis=-1)
    gate = jax.nn.softmax(top_s, axis=-1)

    T = B * S
    nb = T // PEER_TOKEN_BLOCK
    hb_all = h.reshape(nb, PEER_TOKEN_BLOCK, D)
    ib_all = idx.reshape(nb, PEER_TOKEN_BLOCK, PEER_HEADS * PEER_TOPK)
    gb_all = gate.reshape(nb, PEER_TOKEN_BLOCK, PEER_HEADS * PEER_TOPK)

    def one_block(args):
        hb, ib, gb = args
        u = jnp.take(expert_u, ib, axis=0)
        a = jnp.einsum('tkd,td->tk', u, hb).astype(jnp.float32)
        w = gb * jax.nn.gelu(a, approximate=False)
        vsel = jnp.take(expert_v, ib, axis=0)
        return jnp.einsum('tk,tkd->td', w.astype(vsel.dtype), vsel)

    out = lax.map(one_block, (hb_all, ib_all, gb_all))
    return out.reshape(B, S, D)

def setup_inputs(seed: int = 0) -> dict:
    key = jax.random.key(seed)
    ks = jax.random.split(key, 20)
    f32 = jnp.float32
    D = D_MODEL
    nrm = lambda k, shp, s: jax.random.normal(k, shp, f32) * s
    gain = lambda k, shp: 1.0 + 0.02 * jax.random.normal(k, shp, f32)
    return {
        "x": nrm(ks[0], (BATCH, SEQ, D), 1.0),
        "c": nrm(ks[1], (BATCH, D), 1.0),
        "w_ada": nrm(ks[2], (DEPTH, D, N_MOD * D), 0.5 * D ** -0.5),
        "b_ada": nrm(ks[3], (DEPTH, N_MOD * D), 0.02),
        "g_pre_mix": gain(ks[4], (DEPTH, D)),
        "g_post_mix": gain(ks[5], (DEPTH, D)),
        "g_pre_ffn": gain(ks[6], (DEPTH, D)),
        "g_post_ffn": gain(ks[7], (DEPTH, D)),
        "w_in": nrm(ks[8], (DEPTH, D, IN_COLS), D ** -0.5),
        "lam_qk": nrm(ks[9], (DEPTH, 4, DIFF_QK), 0.1),
        "g_diff_sub": gain(ks[10], (DEPTH, DIFF_VDIM)),
        "lb_theta": nrm(ks[11], (DEPTH + 1, HGRN_WIDTH), 0.1),
        "g_hgrn_out": gain(ks[12], (DEPTH, HGRN_DIM)),
        "w_out": nrm(ks[13], (DEPTH, MIX_WIDTH, D), MIX_WIDTH ** -0.5),
        "w_pq": nrm(ks[14], (DEPTH, D, PEER_HEADS * PEER_QDIM), D ** -0.5),
        "sub_keys": nrm(ks[15], (DEPTH, PEER_HEADS, 2, N_KEYS, PEER_QHALF), PEER_QHALF ** -0.5),
        "expert_u": nrm(ks[16], (DEPTH, N_EXPERTS, D), D ** -0.5),
        "expert_v": nrm(ks[17], (DEPTH, N_EXPERTS, D), D ** -0.5),
    }

def reference(x, c, w_ada, b_ada, g_pre_mix, g_post_mix, g_pre_ffn, g_post_ffn, w_in, lam_qk,
              g_diff_sub, lb_theta, g_hgrn_out, w_out, w_pq, sub_keys, expert_u, expert_v):
    lb_all = jnp.cumsum(jax.nn.softmax(lb_theta.astype(jnp.float32), axis=0), axis=0)
    c_act = jax.nn.silu(c)
    for l in range(DEPTH):
        lam_init = 0.8 - 0.6 * math.exp(-0.3 * l)
        mod = (c_act @ w_ada[l] + b_ada[l])[:, None, :]
        sh1, sc1, gt1, sh2, sc2, gt2 = jnp.split(mod, N_MOD, axis=-1)
        h = rmsnorm(x, g_pre_mix[l]) * (1.0 + sc1) + sh1
        y = hybrid_mixer(h, w_in[l], lam_qk[l], g_diff_sub[l], lb_all[l], g_hgrn_out[l], w_out[l], lam_init)
        x = x + gt1 * rmsnorm(y, g_post_mix[l])
        h = rmsnorm(x, g_pre_ffn[l]) * (1.0 + sc2) + sh2
        y = peer(h, w_pq[l], sub_keys[l], expert_u[l], expert_v[l])
        x = x + gt2 * rmsnorm(y, g_post_ffn[l])
    return x


_drawn_inputs = setup_inputs


def setup_inputs(seed=0):
    import zlib

    import numpy as np

    out = dict(_drawn_inputs(seed))
    spreads = {}
    factors = {'g_post_ffn': 8.0, 'lam_qk': 3.484, 'lb_theta': 4.566, 'g_hgrn_out': 3.08}
    for name, (base, spread) in spreads.items():
        noise = np.random.default_rng([zlib.crc32(name.encode()), seed]).standard_normal(out[name].shape)
        drawn = base * np.exp(spread * noise) if base else spread * noise
        out[name] = __import__('jax').numpy.asarray(drawn.astype(out[name].dtype))
    for name, factor in factors.items():
        out[name] = (out[name] * factor).astype(out[name].dtype)
    return out
```

```python
from contextlib import ExitStack

import concourse.bass as bass
from concourse import mybir

F32 = mybir.dt.float32
F32R = mybir.dt.float32r
BF16 = mybir.dt.bfloat16
U32 = mybir.dt.uint32
ALU = mybir.AluOpType
ACT = mybir.ActivationFunctionType
AX_X = mybir.AxisListType.X

P = 128
D = 1024
S = 512
TT = S // P
KC = D // P
HEADS = 4
HD = 128
QK = 64
W4 = HEADS * S
PH = 8
TOPK = 16
NKEY = 128
HJ = 2 * PH
LAM_INIT = 0.2
EPS = 1e-6
NEG = -1e30
LOWEST = -3.0e38

RAW = 4
SPLIT = 2
UNIT = 1024

JG = 4
GROUPS = NKEY // JG
TB = 32
NTB = S // TB


class Steps:

    def __init__(self, sem):
        self.sem = sem
        self.n = 0

    def then(self, eng, ins):
        self.n += 1
        ins.then_inc(self.sem, 1)
        eng.wait_ge(self.sem, self.n)


class LoopSteps:

    def __init__(self, sem, i, each):
        self.sem, self.i, self.each = sem, i, each
        self.n = 0

    def then(self, eng, ins):
        self.n += 1
        ins.then_inc(self.sem, 1)
        eng.wait_ge(self.sem, self.i * self.each + self.n)

    def done(self):
        assert self.n == self.each, self.n


class Memory:
    pass


def build(nc, a):
    with ExitStack() as outer:
        m = Memory()

        def sb(name, shape, dt=F32, stack=outer):
            return stack.enter_context(nc.sbuf_tensor(name, shape, dt))

        def sem(name):
            return outer.enter_context(nc.semaphore(name))

        m.sb, m.sem = sb, sem
        m.psum = [outer.enter_context(nc.psum_tensor(f"bank{i}", [P, 512], F32)) for i in range(8)]
        m.dve = Steps(sem("dve_step"))
        m.act = Steps(sem("act_step"))
        m.pool = Steps(sem("pool_step"))

        m.ident = sb("ident", [P, P])
        m.ident_bf = sb("ident_bf", [P, P], BF16)
        m.ones = sb("ones", [P, P])
        m.eps = sb("eps", [P, 1])
        m.zero = sb("zero", [P, 1])
        m.mod = sb("mod", [P, 48])
        m.bada = sb("bada", [P, 48])
        m.gains = sb("gains", [P, 4, KC])
        m.cact = sb("cact", [P, KC])
        m.scale = sb("norm_scale", [P, KC])
        m.rowg = sb("rowg", [P, 2, D])
        m.ss = sb("sumsq", [P, TT])
        m.rstd = sb("rstd", [P, TT])
        m.rows = sb("rows", [P, TT, D])

        m.unit_landed = [sem(f"unit_landed{i}") for i in range(RAW)]
        m.unit_hi = sem("unit_hi")
        m.unit_lo = sem("unit_lo")
        m.unit_used = sem("unit_used")
        m.unit_evac = sem("unit_evac")
        m.units = 0
        m.evacs = 0

        stage_project(nc, a, m)
        stage_mix(nc, a, m)
        m.actT = sb("actT", [P, 2, KC, S], F32R)
        with ExitStack() as m.keep:
            m.scores = m.sb("scores_all", [P, TT, HJ * NKEY], F32, m.keep)
            stage_join(nc, a, m)
            stage_scores(nc, a, m)
            stage_choose(nc, a, m)
        stage_experts(nc, a, m)



def units_load(nc, sp, m, src, raw, n0, count):
    def body(i, first):
        for u in range(RAW):
            if not (first and n0 == 0):
                sp.wait_ge(m.unit_lo, i + (n0 - RAW + 1 + u))
            sp.dma_start(raw[:, u, :], src[bass.ds(i + u, 1), :, :].rearrange("a p f -> p (a f)")
                         ).then_inc(m.unit_landed[u], 16)
    body(0, True)
    with sp.Fori(1, count // RAW) as k:
        body(k * RAW, False)


def units_hi(nc, act, m, raw, hl, n0, count):
    def body(i, k, first):
        for u in range(RAW):
            act.wait_ge(m.unit_landed[u], k * 16 + (n0 // RAW + 1) * 16)
            if not (first and n0 == 0 and u < SPLIT):
                act.wait_ge(m.unit_used, i + (n0 - SPLIT + 1 + u))
            nc.scalar.activation(hl[:, 0, u % SPLIT, :], raw[:, u, :], ACT.Copy).then_inc(m.unit_hi, 1)
    body(0, 0, True)
    with act.Fori(1, count // RAW) as k:
        body(k * RAW, k, False)


def unit_lo(nc, dve, m, raw, hl, u, n):
    dve.wait_ge(m.unit_hi, n + 1)
    nc.vector.tensor_tensor(hl[:, 1, u % SPLIT, :], raw[:, u, :], hl[:, 0, u % SPLIT, :].bitcast(F32),
                            ALU.subtract).then_inc(m.unit_lo, 1)


PASSES = ((0, 0), (0, 1), (1, 0))


def column_units_pe(nc, pe, m, hl, n0, e0, count):
    def body(i, first):
        for u in range(RAW):
            pe.wait_ge(m.unit_lo, i + (n0 + 1 + u))
            if not (first and e0 == 0 and u < 2):
                pe.wait_ge(m.unit_evac, i + (e0 - 1 + u))
            bank = m.psum[u % 2]
            for kc in range(KC):
                for j, (a, b) in enumerate(PASSES):
                    last = nc.tensor.matmul(bank[:], hl[:, a, u % SPLIT, kc * P:(kc + 1) * P],
                                            m.actT[:, b, kc, :], start=(kc == 0 and j == 0),
                                            stop=(kc == KC - 1 and j == 2))
            last.then_inc(m.unit_used, 1)
    body(0, True)
    with pe.Fori(1, count // RAW) as k:
        body(k * RAW, False)


def column_units_dve(nc, dve, m, raw, hl, dst, n0, e0, count):
    unit_lo(nc, dve, m, raw, hl, 0, n0)

    def body(i, last):
        for u in range(RAW):
            if not (last and u == RAW - 1):
                unit_lo(nc, dve, m, raw, hl, (u + 1) % RAW, i + (n0 + u + 1))
            dve.wait_ge(m.unit_used, i + (n0 + u + 1))
            nc.vector.tensor_copy(dst[:, bass.ds(i * S + u * S, S)], m.psum[u % 2][:]).then_inc(m.unit_evac, 1)
    with dve.Fori(0, count // RAW - 1) as k:
        body(k * RAW, False)
    body(count - RAW, True)


def row_units_pe(nc, pe, m, hl, n0, e0, groups):
    def body(g, parity, first):
        for u in range(RAW):
            pe.wait_ge(m.unit_lo, g * RAW + (n0 + 1 + u))
            for t in range(TT):
                if u == 0 and not first:
                    pe.wait_ge(m.unit_evac, g * TT + (e0 - TT + t + 1))
                for c in range(2):
                    kc = 2 * u + c
                    for j, (a, b) in enumerate(PASSES):
                        last = nc.tensor.matmul(m.psum[4 + t][:], m.actT[:, a, kc, t * P:(t + 1) * P],
                                                hl[:, b, u % SPLIT, c * S:(c + 1) * S],
                                                start=(kc == 0 and j == 0), stop=(kc == KC - 1 and j == 2))
            last.then_inc(m.unit_used, 1)
    body(0, 0, True)
    with pe.Fori(1, groups) as g:
        body(g, 0, False)


def row_units_dve(nc, dve, m, raw, hl, dst, n0, e0, groups):
    unit_lo(nc, dve, m, raw, hl, 0, n0)

    def body(g, last):
        for u in range(RAW):
            if not (last and u == RAW - 1):
                unit_lo(nc, dve, m, raw, hl, (u + 1) % RAW, g * RAW + (n0 + u + 1))
        dve.wait_ge(m.unit_used, g * RAW + (n0 + RAW))
        for t in range(TT):
            nc.vector.tensor_copy(dst[:, bass.ds(g * TT * S + t * S, S)], m.psum[4 + t][:]).then_inc(m.unit_evac, 1)
    if groups > 1:
        with dve.Fori(0, groups - 1) as g:
            body(g, False)
    body(groups - 1, True)



ADA = 2


def ada_pe(nc, pe, m, wada, ada_landed, ada_used, c, first):
    pe.wait_ge(ada_landed[c % 2], 16 * (c // 2 + 1))
    for n in range(ADA):
        col = c * ADA + n
        for kc in range(KC):
            last = nc.tensor.matmul(m.psum[7][:, col:col + 1], wada[:, c % 2, n, kc, :], m.cact[:, kc:kc + 1],
                                    start=(kc == 0), stop=(kc == KC - 1))
    last.then_inc(ada_used, 1)



def norm_stats(nc, act, m, x, scratch, rows_ready, out_sem):
    for t in range(TT):
        rows_ready(act, t)
        m.act.then(act, nc.scalar.activation(scratch, x[:, t, :], ACT.Square, accum_out=m.ss[:, t:t + 1]))
    nc.scalar.activation(m.rstd[:], m.ss[:], ACT.Sqrt, bias=m.eps[:, 0:1], scale=1.0 / D).then_inc(out_sem, 1)


def norm_rows_dve(nc, dve, m, x, xn, stats, stats_n, xn_ready):
    dve.wait_ge(stats, stats_n)
    m.dve.then(dve, nc.vector.reciprocal(m.rstd[:], m.rstd[:]))
    for t in range(TT):
        nc.vector.tensor_scalar(xn[:, t, :], x[:, t, :], m.rstd[:, t:t + 1], None, ALU.mult).then_inc(xn_ready, 1)


def transpose_pe(nc, pe, m, xn, banks, xn_ready, bank_free, transposed):
    for dc in range(KC):
        if dc >= 2:
            pe.wait_ge(bank_free, dc - 1)
        for t in range(TT):
            if dc == 0 and xn_ready is not None:
                pe.wait_ge(xn_ready, t + 1)
            last = nc.tensor.transpose(m.psum[banks + dc % 2][:, t * P:(t + 1) * P],
                                       xn[:, t, dc * P:(dc + 1) * P], m.ident[:])
        last.then_inc(transposed, 1)


def split_act(nc, act, m, actT, banks, piece, transposed, bank_free, piece_lo, hi_ready, modulated, sh):
    for dc in range(KC):
        act.wait_ge(transposed, dc + 1)
        if dc >= 2:
            act.wait_ge(piece_lo, dc - 1)
        if modulated:
            ins = nc.scalar.activation(piece[:, dc % 2, :], m.psum[banks + dc % 2][:], ACT.Identity,
                                       scale=m.scale[:, dc:dc + 1], bias=m.mod[:, sh + dc:sh + dc + 1])
        else:
            ins = nc.scalar.activation(piece[:, dc % 2, :], m.psum[banks + dc % 2][:], ACT.Copy)
        ins.then_inc(bank_free, 1)
        act.wait_ge(bank_free, dc + 1)
        nc.scalar.activation(actT[:, 0, dc, :], piece[:, dc % 2, :], ACT.Copy).then_inc(hi_ready, 1)


def split_dve(nc, dve, actT, piece, hi_ready, piece_lo):
    for dc in range(KC):
        dve.wait_ge(hi_ready, dc + 1)
        nc.vector.tensor_tensor(actT[:, 1, dc, :], piece[:, dc % 2, :], actT[:, 0, dc, :].bitcast(F32),
                                ALU.subtract).then_inc(piece_lo, 1)



def stage_project(nc, a, m):
    m.keep = ExitStack()
    m.projT = m.sb("projT", [P, 4 * W4], F32, m.keep)
    m.projN = m.sb("projN", [P, 3 * TT * S], F32, m.keep)
    m.wada = m.sb("wada", [P, 2, ADA, KC, P], F32, m.keep)
    m.ada_landed = [m.sem("ada_landed0"), m.sem("ada_landed1")]
    m.ada_used = m.sem("ada_used")
    with ExitStack() as own:
        x = m.rows
        m.actT = m.sb("actT1", [P, 2, KC, S], F32R, own)
        xn = m.projN[:, 0:TT * D].rearrange("p (t d) -> p t d", t=TT)
        raw = m.sb("raw1", [P, RAW, UNIT], F32, own)
        hl = m.sb("hl1", [P, 2, SPLIT, UNIT], F32R, own)
        piece = m.sb("piece1", [P, 2, S], F32, own)
        scratch = m.sb("scratch1", [P, D], F32, own)
        x_landed = [m.sem(f"x_tile{t}_landed") for t in range(TT)]
        small = m.sem("small_landed")
        ident_ready = m.sem("ident_ready")
        const_ready = m.sem("const_ready")
        c_ready = m.sem("c_ready")
        stats = m.sem("stats1")
        xn_ready = m.sem("xn_ready1")
        transposed = m.sem("transposed1")
        bank_free = m.sem("bank_free1")
        hi_ready = m.sem("hi_ready1")
        piece_lo = m.sem("piece_lo1")
        scale_ready = m.sem("scale_ready1")
        first_chunks = 16 // ADA
        block = own.enter_context(nc.Block())

        @block.sync
        def _(sp):
            for t in range(TT):
                sp.dma_start(x[:, t, :], a.x[t * P:(t + 1) * P, :]).then_inc(x_landed[t], 16)
                if t == 0:
                    sp.dma_start(m.cact[:], a.c).then_inc(small, 16)
                    sp.dma_start(m.bada[:], a.b_ada).then_inc(small, 16)
                    sp.dma_start(m.gains[:], a.gains).then_inc(small, 16)
            for c in range(first_chunks):
                if c >= 2:
                    sp.wait_ge(m.ada_used, c - 1)
                sp.dma_start(m.wada[:, c % 2], a.w_ada[c]).then_inc(m.ada_landed[c % 2], 16)
            units_load(nc, sp, m, a.w_cols, raw, 0, 16)
            units_load(nc, sp, m, a.w_rows, raw, 16, 12)

        @block.gpsimd
        def _(pool):
            m.pool.then(pool, nc.gpsimd.memset(m.ident[:], 0.0))
            m.pool.then(pool, nc.gpsimd.affine_select(
                out=m.ident[:], in_=m.ident[:], compare_op=ALU.not_equal, fill=1.0, base=0,
                pattern=[[-1, P]], channel_multiplier=1))
            nc.gpsimd.tensor_copy(m.ident_bf[:], m.ident[:]).then_inc(ident_ready, 1)
            nc.gpsimd.memset(m.ones[:], 1.0).then_inc(const_ready, 1)
            nc.gpsimd.memset(m.eps[:], EPS).then_inc(const_ready, 1)
            nc.gpsimd.memset(m.zero[:], 0.0).then_inc(const_ready, 1)

        @block.scalar
        def _(act):
            act.wait_ge(const_ready, 3)
            act.wait_ge(small, 48)
            nc.scalar.activation(m.cact[:], m.cact[:], ACT.Silu).then_inc(c_ready, 1)
            norm_stats(nc, act, m, x, scratch[:], lambda e, t: e.wait_ge(x_landed[t], 16), stats)
            act.wait_ge(scale_ready, 1)
            split_act(nc, act, m, m.actT, 0, piece, transposed, bank_free, piece_lo, hi_ready, True, 0)
            units_hi(nc, act, m, raw, hl, 0, 16)
            units_hi(nc, act, m, raw, hl, 16, 12)

        @block.vector
        def _(dve):
            norm_rows_dve(nc, dve, m, x, xn, stats, 1, xn_ready)
            dve.wait_ge(m.ada_used, first_chunks)
            m.dve.then(dve, nc.vector.tensor_tensor(m.mod[:, 0:16], m.psum[7][:, 0:16], m.bada[:, 0:16], ALU.add))
            nc.vector.scalar_tensor_tensor(m.scale[:], m.mod[:, 8:16], 1.0, m.gains[:, 0, :],
                                           ALU.add, ALU.mult).then_inc(scale_ready, 1)
            split_dve(nc, dve, m.actT, piece, hi_ready, piece_lo)
            column_units_dve(nc, dve, m, raw, hl, m.projT, 0, 0, 16)
            row_units_dve(nc, dve, m, raw, hl, m.projN, 16, 16, 3)

        @block.tensor
        def _(pe):
            pe.wait_ge(ident_ready, 1)
            pe.wait_ge(c_ready, 1)
            for c in range(first_chunks):
                ada_pe(nc, pe, m, m.wada, m.ada_landed, m.ada_used, c, c == 0)
            transpose_pe(nc, pe, m, xn, 0, xn_ready, bank_free, transposed)
            pe.wait_ge(piece_lo, KC)
            column_units_pe(nc, pe, m, hl, 0, 0, 16)
            row_units_pe(nc, pe, m, hl, 16, 16, 3)
    m.units, m.evacs = 28, 28



LEVELS = ("own", 8, 16, 32, 64)
OWN = 8
OWN_REF = 3
CHUNK = P
NCH = S // CHUNK
STEPS_A = HEADS * TT
ADA_CHUNKS = 32 // ADA
LEVEL_AT = 8
ITEMS = {1: 0, 3: 1, 5: 2, 7: 3, 9: 4, 11: "kb"}
SLOT_E = (0, 0, 1, 0, 1)
SLOT_F = ((0, 1), (2, 2), (3, 3), (0, 0), (1, 1))


def stage_mix(nc, a, m):
    with ExitStack() as own:
        def sb(name, shape, dt=F32):
            return m.sb(name, shape, dt, own)

        cat = m.rows
        q = m.projT[:, 2 * W4:3 * W4]
        f = m.projT[:, 3 * W4:4 * W4]
        av = m.projN[:, 0:TT * S].rearrange("p (t n) -> p t n", t=TT)
        hi = m.projN[:, TT * S:2 * TT * S].rearrange("p (t n) -> p t n", t=TT)
        hg = m.projN[:, 2 * TT * S:3 * TT * S]
        kk = sb("kk", [P, W4])
        b = sb("b", [P, W4])
        E = sb("E", [P, 2, W4])
        F = sb("F", [P, 4, W4])
        attnT = sb("attnT", [P, HEADS, S])
        kbT = sb("kbT", [P, NCH - 1, HEADS * HD])
        state = sb("state", [P, NCH - 1, HEADS * HD])
        prob = sb("prob", [P, 2, S])
        mixed = sb("mixed", [P, 2, S])
        mixedT = sb("mixedT", [P, 2, S])
        masks = sb("masks", [P, len(LEVELS), P])
        negmask = sb("negmask", [P, P], BF16)
        small = sb("small2", [P, 2 * 2 * QK + 2 * HEADS + 2 * HD])
        restart = sb("restart", [P, W4], BF16)
        decay = sb("decay", [P, HEADS * NCH])
        lamp = sb("lamp", [P, 2 * QK])
        lams = sb("lams", [P, 4])
        lb = sb("lb", [P, 2, HEADS])
        nbias = sb("nbias", [P, 2, 2])
        Z = sb("Z", [P, 2, 2])
        rz = sb("rz", [P, 2, 2])
        ss = sb("ss2", [P, TT, 2 * HEADS])
        lam = small[:, 0:4 * QK]
        theta = small[:, 4 * QK:4 * QK + 2 * HEADS]
        g_diff = small[:, 4 * QK + 2 * HEADS:4 * QK + 2 * HEADS + HD]
        g_hgrn = small[:, 4 * QK + 2 * HEADS + HD:]

        small_landed = m.sem("small_landed2")
        masks_ready = m.sem("masks_ready")
        sig_ready = m.sem("sig_ready")
        gate_ready = m.sem("gate_ready")
        log_ready = m.sem("log_ready")
        hg_ready = m.sem("hg_ready")
        lam_sums = m.sem("lam_sums")
        lam_exps = m.sem("lam_exps")
        theta_diff = m.sem("theta_diff")
        scores = m.sem("scores")
        bias_ready = m.sem("bias_ready")
        probs_ready = m.sem("probs_ready")
        mixed_ready = m.sem("mixed_ready")
        mixed_tr = m.sem("mixed_tr")
        mixedT_ready = m.sem("mixedT_ready")
        attn_out = m.sem("attn_out")
        attn_read = m.sem("attn_read")
        diff_ready = m.sem("diff_ready")
        exp_ready = m.sem("exp_ready")
        f_ready = m.sem("f_ready")
        level_done = m.sem("level_done")
        level_copied = m.sem("level_copied")
        mod_read = m.sem("mod_read2")
        kb_tr = m.sem("kb_tr")
        kbT_ready = m.sem("kbT_ready")
        kv_done = m.sem("kv_done")
        state_ready = m.sem("state_ready")
        hgrn_out = m.sem("hgrn_out")
        hgrn_read = m.sem("hgrn_read")
        squares = m.sem("squares")
        sums = m.sem("sums")
        roots = m.sem("roots")

        block = own.enter_context(nc.Block())
        b_k = b[:].rearrange("p (n c) -> p n c", c=CHUNK)
        last_b = b_k[:, :, CHUNK - 1:CHUNK]

        @block.sync
        def _(sp):
            sp.dma_start(small[:], a.small).then_inc(small_landed, 16)
            for c in range(16 // ADA, 48 // ADA):
                sp.wait_ge(m.ada_used, c - 1)
                sp.dma_start(m.wada[:, c % 2], a.w_ada[c]).then_inc(m.ada_landed[c % 2], 16)

        @block.gpsimd
        def _(pool):
            g = nc.gpsimd
            m.pool.then(pool, g.memset(restart[:], 1.0))
            g.memset(restart[:].rearrange("p (n c) -> p n c", c=CHUNK)[:, :, 0:1], 0.0).then_inc(masks_ready, 1)
            m.pool.then(pool, g.memset(negmask[:], 0.0))
            g.affine_select(out=negmask[:], in_=negmask[:], compare_op=ALU.is_ge, fill=NEG, base=0,
                            pattern=[[-1, P]], channel_multiplier=1).then_inc(masks_ready, 1)
            m.pool.then(pool, g.memset(masks[:], 0.0))
            own_mask = masks[:, 0, :].rearrange("p (n c) -> p n c", c=OWN)
            m.pool.then(pool, g.memset(masks[:, 0, :], 1.0))
            m.pool.then(pool, g.affine_select(out=own_mask, in_=own_mask, compare_op=ALU.is_ge, fill=0.0, base=0,
                                              pattern=[[-OWN, P // OWN], [0, OWN]], channel_multiplier=1))
            m.pool.then(pool, g.affine_select(out=own_mask, in_=own_mask, compare_op=ALU.is_ge, fill=0.0, base=0,
                                              pattern=[[OWN, P // OWN], [1, OWN]], channel_multiplier=-1))
            for level in range(1, len(LEVELS)):
                h = LEVELS[level]
                right = masks[:, level, :].rearrange("p (n c) -> p n c", c=2 * h)[:, :, h:2 * h]
                m.pool.then(pool, g.memset(right, 1.0))
                m.pool.then(pool, g.affine_select(out=right, in_=right, compare_op=ALU.is_ge, fill=0.0, base=0,
                                                  pattern=[[-2 * h, P // (2 * h)], [0, h]], channel_multiplier=1))
                m.pool.then(pool, g.affine_select(out=right, in_=right, compare_op=ALU.is_ge, fill=0.0, base=h - 1,
                                                  pattern=[[2 * h, P // (2 * h)], [0, h]], channel_multiplier=-1))
            g.memset(attnT[:], 0.0).then_inc(masks_ready, 1)
            pool.wait_ge(log_ready, 1)
            pool.wait_ge(exp_ready, 1)
            g.tensor_tensor(F[:, 0, :], E[:, 0, :], kk[:], ALU.mult).then_inc(f_ready, 1)
            g.tensor_tensor(F[:, 1, :], E[:, 1, :], q, ALU.mult).then_inc(f_ready, 1)
            for level in range(1, len(LEVELS)):
                h = LEVELS[level]
                pool.wait_ge(exp_ready, level + 1)
                if level == 3:
                    pool.wait_ge(level_done, HEADS)
                out = F[:, SLOT_F[level][0], :].rearrange("p (n c) -> p n c", c=2 * h)
                e = E[:, SLOT_E[level], :].rearrange("p (n c) -> p n c", c=2 * h)
                kv = kk[:].rearrange("p (n c) -> p n c", c=2 * h)
                qv = q.rearrange("p (n c) -> p n c", c=2 * h)
                g.tensor_tensor(out[:, :, 0:h], e[:, :, 0:h], kv[:, :, 0:h], ALU.mult).then_inc(f_ready, 1)
                g.tensor_tensor(out[:, :, h:], e[:, :, h:], qv[:, :, h:], ALU.mult).then_inc(f_ready, 1)
            pool.wait_ge(exp_ready, len(LEVELS) + 1)
            pool.wait_ge(level_done, 3 * HEADS)
            g.tensor_tensor(F[:, 2, :], E[:, 0, :], q, ALU.mult).then_inc(f_ready, 1)
            g.tensor_tensor(F[:, 3, :], E[:, 1, :], kk[:], ALU.mult).then_inc(f_ready, 1)
            pool.wait_ge(hg_ready, 1)
            g.tensor_tensor(hg.rearrange("p (n c) -> p n c", c=HD), hg.rearrange("p (n c) -> p n c", c=HD),
                            g_hgrn.unsqueeze(1).to_broadcast([P, TT * HEADS, HD]), ALU.mult).then_inc(hg_ready, 1)

        @block.scalar
        def _(act):
            A = nc.scalar.activation
            act.wait_ge(theta_diff, 1)
            A(lb[:, 0, :], theta[:, 0:HEADS], ACT.Sigmoid).then_inc(sig_ready, 1)
            A(f, f, ACT.Sigmoid).then_inc(sig_ready, 1)
            A(q, q, ACT.Silu).then_inc(sig_ready, 1)
            A(hg, hg, ACT.Silu).then_inc(hg_ready, 1)
            act.wait_ge(gate_ready, 1)
            act.wait_ge(sig_ready, 3)
            A(f, f, ACT.Ln).then_inc(log_ready, 1)
            act.wait_ge(lam_sums, 1)
            A(lams[:, 2:4], lams[:, 0:2], ACT.Exp).then_inc(lam_exps, 1)
            for n in range(STEPS_A + 1):
                if n < STEPS_A:
                    k = (n % TT + 1) * P
                    act.wait_ge(bias_ready, n + 1)
                    if n >= 1:
                        act.wait_ge(mixed_ready, n)
                    for j in range(2):
                        A(prob[:, j, 0:k], m.psum[2 * (n % 2) + j][:, 0:k], ACT.Exp, bias=nbias[:, n % 2, j:j + 1],
                          scale=QK ** -0.5, accum_out=Z[:, n % 2, j:j + 1]).then_inc(probs_ready, 1)
                if n >= 1:
                    k = ((n - 1) % TT + 1) * P
                    act.wait_ge(mixed_tr, n)
                    if n >= 3:
                        act.wait_ge(attn_out, n - 2)
                    A(mixedT[:, (n - 1) % 2, 0:k], m.psum[4][:, 0:k], ACT.Copy).then_inc(mixedT_ready, 1)
                item = ITEMS.get(n)
                if item == 0:
                    act.wait_ge(diff_ready, 1)
                    m.act.then(act, A(E[:, 1, :], E[:, 0, :], ACT.Exp))
                    A(E[:, 0, :], E[:, 0, :], ACT.Exp, scale=-1.0).then_inc(exp_ready, 1)
                elif item == "kb":
                    act.wait_ge(diff_ready, len(LEVELS) + 1)
                    m.act.then(act, A(decay[:].rearrange("p (n o) -> p n o", o=1), last_b, ACT.Exp))
                    m.act.then(act, A(E[:, 0, :], b[:], ACT.Exp))
                    A(E[:, 1, :], E[:, 1, :], ACT.Exp).then_inc(exp_ready, 1)
                elif item is not None:
                    h = LEVELS[item]
                    act.wait_ge(diff_ready, item + 1)
                    e = E[:, SLOT_E[item], :].rearrange("p (n c) -> p n c", c=2 * h)
                    m.act.then(act, A(e[:, :, 0:h], e[:, :, 0:h], ACT.Exp, scale=-1.0))
                    A(e[:, :, h:], e[:, :, h:], ACT.Exp).then_inc(exp_ready, 1)
            for n in range(NCH - 1):
                act.wait_ge(kb_tr, n + 1)
                A(kbT[:, n, :], m.psum[n % 2][:], ACT.Copy).then_inc(kbT_ready, 1)
            for t in range(TT):
                act.wait_ge(hgrn_read, t + 1)
                if t >= 2:
                    act.wait_ge(sums, t - 1)
                A(E[:, t % 2, 0:D], cat[:, t, :], ACT.Square).then_inc(squares, 1)
            act.wait_ge(sums, TT)
            A(ss[:], ss[:], ACT.Sqrt, bias=m.eps[:, 0:1], scale=1.0 / HD).then_inc(roots, 1)

        @block.vector
        def _(dve):
            V = nc.vector
            dve.wait_ge(small_landed, 16)
            V.tensor_tensor(theta[:, 0:HEADS], theta[:, 0:HEADS], theta[:, HEADS:2 * HEADS],
                            ALU.subtract).then_inc(theta_diff, 1)
            lv = lam.rearrange("p (a b) -> p a b", b=2 * QK)
            m.dve.then(dve, V.tensor_tensor(lamp[:].rearrange("p (a b) -> p a b", b=QK), lv[:, :, 0:QK],
                                            lv[:, :, QK:2 * QK], ALU.mult))
            V.tensor_reduce(lams[:, 0:2], lamp[:].rearrange("p (a b) -> p a b", b=QK), AX_X, ALU.add
                            ).then_inc(lam_sums, 1)
            m.dve.then(dve, V.tensor_scalar(g_diff, g_diff, 1.0 - LAM_INIT, None, ALU.mult))
            dve.wait_ge(sig_ready, 2)
            m.dve.then(dve, V.tensor_scalar(lb[:, 1, :], lb[:, 0, :], -1.0, 1.0, ALU.mult, ALU.add))
            for h in range(HEADS):
                fh = f[:, h * S:(h + 1) * S]
                m.dve.then(dve, V.tensor_scalar(fh, fh, lb[:, 1, h:h + 1], lb[:, 0, h:h + 1], ALU.mult, ALU.add))
            V.tensor_scalar(kk[:], f, -1.0, 1.0, ALU.mult, ALU.add).then_inc(gate_ready, 1)
            dve.wait_ge(lam_exps, 1)
            m.dve.then(dve, V.tensor_tensor(lams[:, 0:1], lams[:, 3:4], lams[:, 2:3], ALU.subtract))
            m.dve.then(dve, V.tensor_scalar(lams[:, 0:1], lams[:, 0:1], -LAM_INIT, None, ALU.add))
            dve.wait_ge(log_ready, 1)
            dve.wait_ge(masks_ready, 3)
            m.dve.then(dve, V.tensor_tensor_scan(b[:], restart[:], f, 0.0, ALU.mult, ALU.add))

            def level_copies(n):
                for u in range(2 * (n - LEVEL_AT), 2 * (n - LEVEL_AT) + 2):
                    level, h = divmod(u, HEADS)
                    dve.wait_ge(level_done, u + 1)
                    V.copy_predicated(attnT[:, h, :].rearrange("p (n c) -> p n c", c=P),
                                      masks[:, level, :].bitcast(U32).unsqueeze(1).to_broadcast([P, NCH, P]),
                                      m.psum[6 + u % 2][:].rearrange("p (n c) -> p n c", c=P)
                                      ).then_inc(level_copied, 1)

            for n in range(STEPS_A + 2):
                if n < STEPS_A:
                    k = (n % TT + 1) * P
                    dve.wait_ge(scores, n + 1)
                    for j in range(2):
                        m.dve.then(dve, V.tensor_reduce(nbias[:, n % 2, j:j + 1], m.psum[2 * (n % 2) + j][:, 0:k],
                                                        AX_X, ALU.max))
                    V.tensor_scalar(nbias[:, n % 2, :], nbias[:, n % 2, :], -QK ** -0.5, None, ALU.mult
                                    ).then_inc(bias_ready, 1)
                if 1 <= n <= STEPS_A:
                    o = n - 1
                    k = (o % TT + 1) * P
                    dve.wait_ge(probs_ready, 2 * n)
                    if o >= 2:
                        dve.wait_ge(mixed_tr, o - 1)
                    m.dve.then(dve, V.reciprocal(rz[:, o % 2, :], Z[:, o % 2, :]))
                    m.dve.then(dve, V.tensor_scalar(rz[:, o % 2, 1:2], rz[:, o % 2, 1:2], lams[:, 0:1], None, ALU.mult))
                    m.dve.then(dve, V.tensor_scalar(mixed[:, o % 2, 0:k], prob[:, 0, 0:k], rz[:, o % 2, 0:1], None,
                                                    ALU.mult))
                    V.scalar_tensor_tensor(mixed[:, o % 2, 0:k], prob[:, 1, 0:k], rz[:, o % 2, 1:2],
                                           mixed[:, o % 2, 0:k], ALU.mult, ALU.add).then_inc(mixed_ready, 1)
                item = ITEMS.get(n)
                if item is not None:
                    if item == 0:
                        bv = b[:].rearrange("p (n c) -> p n c", c=OWN)
                        e = E[:, 0, :].rearrange("p (n c) -> p n c", c=OWN)
                        ref = bv[:, :, OWN_REF:OWN_REF + 1].to_broadcast([P, W4 // OWN, OWN])
                        V.tensor_tensor(e, bv, ref, ALU.subtract).then_inc(diff_ready, 1)
                    elif item == "kb":
                        dve.wait_ge(f_ready, 2 * len(LEVELS))
                        e = E[:, 1, :].rearrange("p (n c) -> p n c", c=CHUNK)
                        V.tensor_tensor(e, last_b.to_broadcast([P, HEADS * NCH, CHUNK]), b_k, ALU.subtract
                                        ).then_inc(diff_ready, 1)
                    else:
                        dve.wait_ge(f_ready, 2 if item <= 2 else 2 * (item - 1))
                        h = LEVELS[item]
                        bv = b[:].rearrange("p (n c) -> p n c", c=2 * h)
                        e = E[:, SLOT_E[item], :].rearrange("p (n c) -> p n c", c=2 * h)
                        ref = bv[:, :, h - 1:h].to_broadcast([P, W4 // (2 * h), 2 * h])
                        V.tensor_tensor(e, bv, ref, ALU.subtract).then_inc(diff_ready, 1)
                if n >= 2:
                    o = n - 2
                    h, t = divmod(o, TT)
                    dve.wait_ge(attn_out, o + 1)
                    V.tensor_copy(cat[:, t, h * HD:(h + 1) * HD], m.psum[5][:, 0:HD]).then_inc(attn_read, 1)
                if n == LEVEL_AT - 1:
                    dve.wait_ge(m.ada_used, 48 // ADA)
                    V.tensor_tensor(m.mod[:, 16:48], m.psum[7][:, 16:48], m.bada[:, 16:48], ALU.add
                                    ).then_inc(mod_read, 1)
                if n >= LEVEL_AT:
                    level_copies(n)
            for n in range(NCH - 1):
                dve.wait_ge(kv_done, n + 1)
                st = state[:, n, :].rearrange("p (h v) -> p h v", h=HEADS)
                kv = m.psum[2 + n % 2][:].rearrange("p (h v) -> p h v", h=HEADS)
                if n == 0:
                    V.tensor_copy(st, kv).then_inc(state_ready, 1)
                else:
                    dve.wait_ge(state_ready, n)
                    before = state[:, n - 1, :].rearrange("p (h v) -> p h v", h=HEADS)
                    dec = decay[:].rearrange("p (h n) -> p h n", h=HEADS)[:, :, n:n + 1].to_broadcast([P, HEADS, HD])
                    m.dve.then(dve, V.tensor_tensor(st, before, dec, ALU.mult))
                    V.tensor_tensor(st, st, kv, ALU.add).then_inc(state_ready, 1)
            for t in range(TT):
                dve.wait_ge(hgrn_out, t + 1)
                V.tensor_copy(cat[:, t, HEADS * HD:], m.psum[4 + t][:]).then_inc(hgrn_read, 1)
            for t in range(TT):
                dve.wait_ge(squares, t + 1)
                V.tensor_reduce(ss[:, t, :], E[:, t % 2, 0:D].rearrange("p (h v) -> p h v", v=HD), AX_X, ALU.add
                                ).then_inc(sums, 1)
            dve.wait_ge(roots, 1)
            m.dve.then(dve, V.reciprocal(ss[:], ss[:]))
            dve.wait_ge(hg_ready, 2)
            hgv = hg.rearrange("p (t n) -> p t n", t=TT)
            for t in range(TT):
                cv = cat[:, t, :].rearrange("p (h v) -> p h v", v=HD)
                m.dve.then(dve, V.tensor_tensor(cv, cv, ss[:, t, :].unsqueeze(2).to_broadcast([P, 2 * HEADS, HD]),
                                                ALU.mult))
                m.dve.then(dve, V.tensor_tensor(cv[:, 0:HEADS], cv[:, 0:HEADS],
                                                g_diff.unsqueeze(1).to_broadcast([P, HEADS, HD]), ALU.mult))
                m.dve.then(dve, V.tensor_tensor(cat[:, t, HEADS * HD:], cat[:, t, HEADS * HD:], hgv[:, t, :], ALU.mult))

        @block.tensor
        def _(pe):
            T = nc.tensor
            aq, ak = m.projT[:, 0:W4], m.projT[:, W4:2 * W4]
            pe.wait_ge(masks_ready, 3)

            def level_matmuls(n):
                if n == LEVEL_AT:
                    pe.wait_ge(mod_read, 1)
                for u in range(2 * (n - LEVEL_AT), 2 * (n - LEVEL_AT) + 2):
                    level, h = divmod(u, HEADS)
                    pe.wait_ge(f_ready, 2 * level + 2)
                    if u >= 2:
                        pe.wait_ge(level_copied, u - 1)
                    for c in range(NCH):
                        at = slice(h * S + c * CHUNK, h * S + (c + 1) * CHUNK)
                        last = T.matmul(m.psum[6 + u % 2][:, c * CHUNK:(c + 1) * CHUNK], F[:, SLOT_F[level][0], at],
                                        F[:, SLOT_F[level][1], at], start=True, stop=True)
                    last.then_inc(level_done, 1)

            for n in range(STEPS_A + 2):
                if n < STEPS_A:
                    h, t = divmod(n, TT)
                    k = (t + 1) * P
                    if n >= 2:
                        pe.wait_ge(probs_ready, 2 * (n - 1))
                    for j in range(2):
                        part = slice(j * QK, (j + 1) * QK)
                        bank = m.psum[2 * (n % 2) + j]
                        T.matmul(bank[:, 0:k], aq[part, h * S + t * P:h * S + (t + 1) * P],
                                 ak[part, h * S:h * S + k], start=True, stop=False)
                        last = T.matmul(bank[:, t * P:k], m.ident_bf[:], negmask[:], start=False, stop=True)
                    last.then_inc(scores, 1)
                if 1 <= n <= STEPS_A:
                    o = n - 1
                    pe.wait_ge(mixed_ready, o + 1)
                    if o >= 1:
                        pe.wait_ge(mixedT_ready, o)
                    for kb in range(o % TT + 1):
                        last = T.transpose(m.psum[4][:, kb * P:(kb + 1) * P], mixed[:, o % 2, kb * P:(kb + 1) * P],
                                           m.ident[:])
                    last.then_inc(mixed_tr, 1)
                if n >= 2:
                    o = n - 2
                    h, t = divmod(o, TT)
                    pe.wait_ge(mixedT_ready, o + 1)
                    if o >= 1:
                        pe.wait_ge(attn_read, o)
                    for kb in range(t + 1):
                        last = T.matmul(m.psum[5][:, 0:HD], mixedT[:, o % 2, kb * P:(kb + 1) * P],
                                        av[:, kb, h * HD:(h + 1) * HD], start=(kb == 0), stop=(kb == t))
                    last.then_inc(attn_out, 1)
                if n < ADA_CHUNKS // 2:
                    for c in range(16 // ADA + 2 * n, 16 // ADA + 2 * n + 2):
                        ada_pe(nc, pe, m, m.wada, m.ada_landed, m.ada_used, c, False)
                if n >= LEVEL_AT:
                    level_matmuls(n)
            pe.wait_ge(f_ready, 2 * len(LEVELS) + 2)
            for n in range(NCH - 1):
                if n >= 2:
                    pe.wait_ge(kbT_ready, n - 1)
                for h in range(HEADS):
                    last = T.transpose(m.psum[n % 2][:, h * HD:(h + 1) * HD],
                                       F[:, 3, h * S + n * CHUNK:h * S + (n + 1) * CHUNK], m.ident[:])
                last.then_inc(kb_tr, 1)
            for n in range(NCH - 1):
                pe.wait_ge(kbT_ready, n + 1)
                if n >= 2:
                    pe.wait_ge(state_ready, n - 1)
                for h in range(HEADS):
                    last = T.matmul(m.psum[2 + n % 2][:, h * HD:(h + 1) * HD], kbT[:, n, h * HD:(h + 1) * HD],
                                    hi[:, n, h * HD:(h + 1) * HD], start=True, stop=True)
                last.then_inc(kv_done, 1)
            pe.wait_ge(attn_read, STEPS_A)
            pe.wait_ge(level_copied, HEADS * len(LEVELS))
            for t in range(NCH):
                if t >= 1:
                    pe.wait_ge(state_ready, t)
                for h in range(HEADS):
                    at = slice(h * S + t * CHUNK, h * S + (t + 1) * CHUNK)
                    out = m.psum[4 + t][:, h * HD:(h + 1) * HD]
                    last = T.matmul(out, attnT[:, h, t * CHUNK:(t + 1) * CHUNK], hi[:, t, h * HD:(h + 1) * HD],
                                    start=True, stop=(t == 0))
                    if t >= 1:
                        last = T.matmul(out, F[:, 2, at], state[:, t - 1, h * HD:(h + 1) * HD], start=False, stop=True)
                last.then_inc(hgrn_out, 1)
    m.keep.close()



def stage_join(nc, a, m):
    h2T = m.actT
    with ExitStack() as own:
        m.actT = m.sb("catT", [P, 2, KC, S], F32R, own)
        catT = m.actT
        raw = m.sb("raw3", [P, RAW, UNIT], F32, own)
        hl = m.sb("hl3", [P, 2, SPLIT, UNIT], F32R, own)
        x = m.sb("x3", [P, TT, D], F32, own)
        piece = m.sb("piece3", [P, 2, S], F32, own)
        scratch = m.sb("scratch3", [P, D], F32, own)
        gcol = m.sb("gcol", [P, 2, KC], F32, own)
        diag = m.sb("diag", [P, 2 * KC, P], F32, own)
        y = m.rows[:].rearrange("p t d -> p (t d)").rearrange("p (g t n) -> p t g n", g=2, t=TT)
        sem = m.sem
        x_landed = sem("x_again_landed")
        diag_ready, row_ready = sem("diag_ready"), sem("row_ready")
        cat_tr, cat_free, cat_lo, cat_hi = sem("cat_tr"), sem("cat_free"), sem("cat_lo"), sem("cat_hi")
        stats = sem("stats3")
        x2_ready, x2_stored = sem("x2_ready"), sem("x2_stored")
        stats_b, xn_ready = sem("stats3b"), sem("xn_ready3")
        transposed, bank_free, hi_ready, piece_lo = sem("tr3"), sem("free3"), sem("hi3"), sem("lo3")
        n0, e0 = m.units, m.evacs
        block = own.enter_context(nc.Block())

        @block.sync
        def _(sp):
            sp.dma_start(x[:], a.x.rearrange("(t p) d -> p t d", p=P)).then_inc(x_landed, 16)
            units_load(nc, sp, m, a.w_out, raw, n0, 8)
            sp.wait_ge(x2_ready, TT)
            sp.dma_start(a.x2, x[:]).then_inc(x2_stored, 16)
            sp.wait_ge(x2_stored, 16)

        @block.scalar
        def _(act):
            split_act(nc, act, m, catT, 4, piece, cat_tr, cat_free, cat_lo, cat_hi, False, 0)
            units_hi(nc, act, m, raw, hl, n0, 8)
            act.wait_ge(m.unit_evac, e0 + 2 * TT)
            for t in range(TT):
                m.act.then(act, nc.scalar.activation(scratch[:].rearrange("p (g n) -> p g n", g=2), y[:, t],
                                                     ACT.Square, accum_out=m.ss[:, t:t + 1]))
            nc.scalar.activation(m.rstd[:], m.ss[:], ACT.Sqrt, bias=m.eps[:, 0:1], scale=1.0 / D).then_inc(stats, 1)
            norm_stats(nc, act, m, x, scratch[:], lambda e, t: e.wait_ge(x2_ready, t + 1), stats_b)
            split_act(nc, act, m, h2T, 4, piece, transposed, bank_free, piece_lo, hi_ready, True, 24)

        @block.vector
        def _(dve):
            V = nc.vector
            for w, (gate, gain) in enumerate(((16, 1), (40, 3))):
                m.dve.then(dve, V.tensor_tensor(gcol[:, w, :], m.mod[:, gate:gate + KC], m.gains[:, gain, :],
                                                ALU.mult))
            for c in range(2 * KC):
                V.tensor_scalar(diag[:, c, :], m.ident[:], gcol[:, c // KC, c % KC:c % KC + 1], None, ALU.mult
                                ).then_inc(diag_ready, 1)
            m.dve.then(dve, V.scalar_tensor_tensor(m.scale[:], m.mod[:, 32:40], 1.0, m.gains[:, 2, :],
                                                   ALU.add, ALU.mult))
            for c in range(4):
                dve.wait_ge(row_ready, c + 1)
                m.dve.then(dve, V.tensor_copy(m.rowg[:, c // 2, (c % 2) * S:(c % 2 + 1) * S], m.psum[c][:]))
            split_dve(nc, dve, catT, piece, cat_hi, cat_lo)
            row_units_dve(nc, dve, m, raw, hl, m.rows[:].rearrange("p t d -> p (t d)"), n0, e0, 2)
            dve.wait_ge(stats, 1)
            dve.wait_ge(x_landed, 16)
            m.dve.then(dve, V.reciprocal(m.rstd[:], m.rstd[:]))
            for t in range(TT):
                g = m.rowg[:, 0, :].rearrange("p (g n) -> p g n", g=2)
                xt = x[:, t, :].rearrange("p (g n) -> p g n", g=2)
                m.dve.then(dve, V.scalar_tensor_tensor(y[:, t], y[:, t], m.rstd[:, t:t + 1], g, ALU.mult, ALU.mult))
                V.tensor_tensor(xt, xt, y[:, t], ALU.add).then_inc(x2_ready, 1)
            norm_rows_dve(nc, dve, m, x, m.rows, stats_b, 1, xn_ready)
            split_dve(nc, dve, h2T, piece, hi_ready, piece_lo)

        @block.tensor
        def _(pe):
            for c in range(4):
                pe.wait_ge(diag_ready, 4 * c + 4)
                nc.tensor.matmul(m.psum[c][:], m.ones[:], diag[:, 4 * c:4 * c + 4, :].rearrange("p c n -> p (c n)"),
                                 start=True, stop=True).then_inc(row_ready, 1)
            transpose_pe(nc, pe, m, m.rows, 4, None, cat_free, cat_tr)
            pe.wait_ge(cat_lo, KC)
            row_units_pe(nc, pe, m, hl, n0, e0, 2)
            pe.wait_ge(m.unit_evac, e0 + 2 * TT)
            transpose_pe(nc, pe, m, m.rows, 4, xn_ready, bank_free, transposed)
    m.units += 8
    m.evacs += 8
    m.actT = h2T



def stage_scores(nc, a, m):
    with ExitStack() as own:
        qT = m.sb("qT", [P, HJ * S], F32, own)
        keys = m.sb("keys", [P, HJ * NKEY], F32, own)
        raw = m.sb("raw4", [P, RAW, UNIT], F32, own)
        hl = m.sb("hl4", [P, 2, SPLIT, UNIT], F32R, own)
        keys_landed = m.sem("keys_landed")
        scored, scores_read = m.sem("scored"), m.sem("scores_read")
        n0, e0 = m.units, m.evacs
        block = own.enter_context(nc.Block())

        @block.sync
        def _(sp):
            sp.dma_start(keys[:], a.keys).then_inc(keys_landed, 16)
            units_load(nc, sp, m, a.w_pq, raw, n0, 16)

        @block.scalar
        def _(act):
            units_hi(nc, act, m, raw, hl, n0, 16)
            for n in range(TT * HJ // 4):
                t, c = divmod(n, HJ // 4)
                act.wait_ge(scored, n + 1)
                nc.scalar.activation(m.scores[:, t, c * S:(c + 1) * S], m.psum[2 + n % 6][:], ACT.Copy
                                     ).then_inc(scores_read, 1)
            act.wait_ge(scores_read, TT * HJ // 4)

        @block.vector
        def _(dve):
            column_units_dve(nc, dve, m, raw, hl, qT, n0, e0, 16)

        @block.tensor
        def _(pe):
            column_units_pe(nc, pe, m, hl, n0, e0, 16)
            pe.wait_ge(m.unit_evac, e0 + 16)
            pe.wait_ge(keys_landed, 16)
            for n in range(TT * HJ // 4):
                t, c = divmod(n, HJ // 4)
                if n >= 6:
                    pe.wait_ge(scores_read, n - 5)
                for k in range(4):
                    hj = 4 * c + k
                    last = nc.tensor.matmul(m.psum[2 + n % 6][:, k * NKEY:(k + 1) * NKEY],
                                            qT[:, hj * S + t * P:hj * S + (t + 1) * P],
                                            keys[:, hj * NKEY:(hj + 1) * NKEY], start=True, stop=True)
                last.then_inc(scored, 1)
    m.units += 16
    m.evacs += 16



ROWS = [(a, 1 + a, TOPK // (a + 1)) for a in range(5)] + [(5, 8, 2), (8, 16, 1)]
NCAND = sum((a1 - a0) * n for a0, a1, n in ROWS)
RING = 16
PER = 4
DROW = NKEY * S + 1024


def candidate_sums(eng, out, first, second):
    at = 0
    for a0, a1, n in ROWS:
        c = a1 - a0
        o = out[:, :, at:at + c * n].rearrange("p h (a b) -> p h a b", a=c)
        last = eng.tensor_tensor(o, first[:, :, a0:a1].unsqueeze(3).to_broadcast([P, PH, c, n]),
                                 second[:, :, 0:n].unsqueeze(2).to_broadcast([P, PH, c, n]), ALU.add)
        at += c * n
    return last


def stage_choose(nc, a, m):
    with ExitStack() as own:
        def sb(name, shape, dt=F32):
            return m.sb(name, shape, dt, own)

        work = sb("work", [P, HJ, NKEY])
        rest = sb("rest", [P, HJ, NKEY])
        v = sb("v", [P, HJ, TOPK])
        vi = sb("vi", [P, HJ, TOPK], U32)
        vf = sb("vf", [P, HJ, TOPK])
        cand = sb("cand", [P, PH, NCAND])
        cand2 = sb("cand2", [P, PH, NCAND])
        code = sb("code", [P, PH, NCAND])
        top = sb("top", [P, PH, TOPK])
        pos = sb("pos", [P, PH, TOPK], U32)
        posf = sb("posf", [P, PH, TOPK])
        hit = sb("hit", [P, PH * TOPK, NCAND])
        places = sb("places", [P, NCAND])
        slots = sb("slots", [P, 3, PH * TOPK])
        slots_u = sb("slots_u", [P, 3, PH * TOPK], U32)
        total = sb("total", [P, PH])
        slotsT = sb("slotsT", [P, 3, S])
        iota = sb("iota", [P, NKEY])
        second_key = sb("second_key", [P, RING])
        carrier = sb("carrier", [P, 2 + RING // PER])
        onehot1 = sb("onehot1", [P, RING, NKEY])
        onehot2 = sb("onehot2", [P, RING, NKEY])
        gates = sb("gates", [P, 2, NKEY, TB])
        sem = m.sem
        iota_ready, work_ready, work_read = sem("iota_ready"), sem("work_ready"), sem("work_read")
        vf_ready, code_ready = sem("vf_ready"), sem("code_ready")
        hit_ready, hit_coded = sem("hit_ready"), sem("hit_coded")
        shifted, exps = sem("shifted"), sem("exps")
        slots_ready, slots_tr, slots_read = sem("slots_ready"), sem("slots_tr"), sem("slots_read")
        dve_loop = sem("dve_loop")
        first_ready, second_ready = sem("first_ready"), sem("second_ready")
        second_copied = sem("second_copied")
        gated, gates_read = sem("gated"), sem("gates_read")
        stored = [sem("stored0"), sem("stored1")]
        pairs = S // (2 * TB)
        block = own.enter_context(nc.Block())

        def first_rows(dve, i, first):
            for u in range(RING):
                if not first and u % PER == 0:
                    dve.wait_ge(gated, i * (RING // PER) + (u // PER - RING // PER + 1))
                at = bass.ds(i * RING + u, 1)
                nc.vector.tensor_scalar(onehot1[:, u, :], iota[:], slotsT[:, 0, at], slotsT[:, 2, at],
                                        ALU.is_equal, ALU.mult).then_inc(first_ready, 1)

        def second_rows(pool, i, first):
            if not first:
                pool.wait_ge(second_ready, i * RING)
                carry_wait(0)
            nc.gpsimd.tensor_copy(second_key[:], slotsT[:, 1, bass.ds(i * RING, RING)]).then_inc(second_copied, 1)
            pool.wait_ge(second_copied, i + 1)
            carry_wait(1)
            for u in range(RING):
                if not first and u % PER == 0:
                    pool.wait_ge(gated, i * (RING // PER) + (u // PER - RING // PER + 1))
                    carry_wait(2 + u // PER)
                nc.gpsimd.tensor_scalar(onehot2[:, u, :], iota[:], second_key[:, u:u + 1], None,
                                        ALU.is_equal).then_inc(second_ready, 1)

        def carry_wait(c):
            nc.gpsimd.tensor_tensor(carrier[:, c:c + 1], m.zero[:], m.zero[:], ALU.add)

        @block.gpsimd
        def _(pool):
            g = nc.gpsimd
            g.iota(iota[:], [[1, NKEY]], base=0, channel_multiplier=0,
                   allow_small_or_imprecise_dtypes=True).then_inc(iota_ready, 1)
            g.iota(places[:], [[1, NCAND]], base=0, channel_multiplier=0,
                   allow_small_or_imprecise_dtypes=True).then_inc(iota_ready, 1)
            vv = vf[:].rearrange("p (h j) k -> p h j k", j=2)
            with pool.Fori(0, TT) as t:
                pool.wait_ge(vf_ready, t + 1)
                candidate_sums(g, code, vv[:, :, 0, :], vv[:, :, 1, :]).then_inc(code_ready, 1)
                pool.wait_ge(code_ready, t + 1)
                pool.wait_ge(hit_ready, t + 1)
                hv = hit[:].rearrange("p (h k) c -> p h k c", h=PH)
                g.tensor_tensor(hv, hv, code[:].unsqueeze(2).to_broadcast([P, PH, TOPK, NCAND]), ALU.mult
                                ).then_inc(hit_coded, 1)
            pool.wait_ge(iota_ready, 2)
            pool.wait_ge(slots_read, TT)
            second_rows(pool, 0, True)
            with pool.Fori(1, S // RING) as i:
                second_rows(pool, i, False)

        @block.scalar
        def _(act):
            for t in range(TT):
                if t >= 1:
                    act.wait_ge(work_read, t)
                nc.scalar.activation(work[:].rearrange("p h k -> p (h k)"), m.scores[:, t, :], ACT.Copy
                                     ).then_inc(work_ready, 1)
                act.wait_ge(shifted, t + 1)
                nc.scalar.activation(slots[:, 2, :], slots[:, 2, :], ACT.Exp).then_inc(exps, 1)
                act.wait_ge(slots_tr, t + 1)
                nc.scalar.activation(slotsT[:, :, t * P:(t + 1) * P],
                                     m.psum[4][:, 0:3 * P].rearrange("p (w n) -> p w n", w=3), ACT.Copy
                                     ).then_inc(slots_read, 1)
            def read_gates(p, first):
                for k in range(2):
                    if not first:
                        act.wait_ge(stored[k], p * 16)
                    for c in range(TB // PER):
                        act.wait_ge(gated, p * (2 * TB // PER) + (k * (TB // PER) + c + 1))
                        nc.scalar.activation(gates[:, k, :, c * PER:(c + 1) * PER],
                                             m.psum[c % 4][:].rearrange("p (t j) -> p j t", t=PER), ACT.Copy
                                             ).then_inc(gates_read, 1)
            read_gates(0, True)
            with act.Fori(1, pairs) as p:
                read_gates(p, False)

        @block.sync
        def _(sp):
            with sp.Fori(0, pairs) as p:
                for k in range(2):
                    sp.wait_ge(gates_read, p * (2 * TB // PER) + ((k + 1) * (TB // PER)))
                    dst = a.gates[:, 0:NKEY * S].rearrange("p (g n) -> p g n", n=NTB * JG * TB)
                    sp.dma_start(dst[:, 0:GROUPS, bass.ds(p * (2 * JG * TB) + k * JG * TB, JG * TB)],
                                 gates[:, k, :, :].rearrange("p (g j) t -> p g (j t)", j=JG)).then_inc(stored[k], 16)
            for k in range(2):
                sp.wait_ge(stored[k], 16 * pairs)

        @block.vector
        def _(dve):
            V = nc.vector
            dve.wait_ge(iota_ready, 2)
            for t in range(TT):
                st = LoopSteps(dve_loop, t, 17)

                def top16(values, count, replaced, best, where):
                    for r in range(count):
                        last = V.max(best[:, r, 0:8], values[:, r, :])
                    st.then(dve, last)
                    for r in range(count):
                        last = V.match_replace(replaced[:, r, :], best[:, r, 0:8], values[:, r, :], LOWEST)
                    st.then(dve, last)
                    for r in range(count):
                        V.max_index(where[:, r, 0:8], best[:, r, 0:8], values[:, r, :])
                    for r in range(count):
                        last = V.max(best[:, r, 8:16], replaced[:, r, :])
                    st.then(dve, last)
                    for r in range(count):
                        last = V.max_index(where[:, r, 8:16], best[:, r, 8:16], replaced[:, r, :])
                    st.then(dve, last)

                dve.wait_ge(work_ready, t + 1)
                top16(work, HJ, rest, v, vi)
                st.then(dve, V.tensor_copy(vf[:], vi[:]))
                vv = vf[:].rearrange("p (h j) k -> p h j k", j=2)
                V.tensor_scalar(vv[:, :, 0, :], vv[:, :, 0, :], float(NKEY), None, ALU.mult).then_inc(vf_ready, 1)
                v4 = v[:].rearrange("p (h j) k -> p h j k", j=2)
                candidate_sums(V, cand, v4[:, :, 0, :], v4[:, :, 1, :]).then_inc(work_read, 1)
                dve.wait_ge(work_read, t + 1)
                top16(cand, PH, cand2, top, pos)
                st.then(dve, V.tensor_copy(posf[:], pos[:]))
                V.tensor_tensor(hit[:], posf[:].rearrange("p h k -> p (h k)").unsqueeze(2)
                                .to_broadcast([P, PH * TOPK, NCAND]),
                                places[:].unsqueeze(1).to_broadcast([P, PH * TOPK, NCAND]), ALU.is_equal
                                ).then_inc(hit_ready, 1)
                if t >= 1:
                    dve.wait_ge(slots_tr, t)
                gate = slots[:, 2, :].rearrange("p (h k) -> p h k", h=PH)
                V.tensor_tensor(gate, top[:], top[:, :, 0:1].to_broadcast([P, PH, TOPK]), ALU.subtract
                                ).then_inc(shifted, 1)
                dve.wait_ge(exps, t + 1)
                st.then(dve, V.tensor_reduce(total[:], gate, AX_X, ALU.add))
                st.then(dve, V.reciprocal(total[:], total[:]))
                st.then(dve, V.tensor_tensor(gate, gate, total[:].unsqueeze(2).to_broadcast([P, PH, TOPK]), ALU.mult))
                dve.wait_ge(hit_coded, t + 1)
                st.then(dve, V.tensor_reduce(posf[:].rearrange("p h k -> p (h k)"), hit[:], AX_X, ALU.add))
                st.then(dve, V.tensor_copy(slots_u[:, 2, :], posf[:].rearrange("p h k -> p (h k)")))
                st.then(dve, V.tensor_scalar(slots_u[:, 0, :], slots_u[:, 2, :], 7, None, ALU.logical_shift_right))
                st.then(dve, V.tensor_scalar(slots_u[:, 1, :], slots_u[:, 2, :], NKEY - 1, None, ALU.bitwise_and))
                V.tensor_copy(slots[:, 0:2, :], slots_u[:, 0:2, :]).then_inc(slots_ready, 1)
                st.done()
            dve.wait_ge(slots_read, TT)
            first_rows(dve, 0, True)
            with dve.Fori(1, S // RING) as i:
                first_rows(dve, i, False)

        @block.tensor
        def _(pe):
            for t in range(TT):
                pe.wait_ge(slots_ready, t + 1)
                if t >= 1:
                    pe.wait_ge(slots_read, t)
                for w in range(3):
                    last = nc.tensor.transpose(m.psum[4][:, w * P:(w + 1) * P], slots[:, w, :], m.ident[:])
                last.then_inc(slots_tr, 1)

            def body(i, first):
                for c in range(RING // PER):
                    if not first:
                        pe.wait_ge(gates_read, i * (RING // PER) + (c - RING // PER + 1))
                    pe.wait_ge(first_ready, i * RING + (c + 1) * PER)
                    pe.wait_ge(second_ready, i * RING + (c + 1) * PER)
                    for k in range(PER):
                        u = c * PER + k
                        last = nc.tensor.matmul(m.psum[c][:, k * NKEY:(k + 1) * NKEY], onehot1[:, u, :],
                                                onehot2[:, u, :], start=True, stop=True)
                    last.then_inc(gated, 1)
            body(0, True)
            with pe.Fori(1, S // RING) as i:
                body(i, False)



def stage_experts(nc, a, m):
    with ExitStack() as own:
        def sb(name, shape, dt=F32):
            return m.sb(name, shape, dt, own)

        u_raw = sb("u_raw", [P, JG, D])
        v_raw = sb("v_raw", [P, JG, D])
        u = sb("u", [P, 2, JG, D], F32R)
        v = sb("v_parts", [P, 2, JG, D], F32R)
        w = sb("w", [P, 2, JG, S], F32R)
        gates = sb("group_gates", [P, NTB, JG, TB])
        act_out = sb("act_out", [P, 2, S])
        weighed = sb("weighed", [P, 2, S])
        y = m.rows
        sem = m.sem
        u_landed, v_landed, gates_landed = sem("u_landed"), sem("v_landed"), sem("gates_landed")
        u_hi, u_lo, v_hi, v_lo = sem("u_hi"), sem("u_lo"), sem("v_hi"), sem("v_lo")
        a_done, gelus, weighed_done, w_ready = sem("a_done"), sem("gelus"), sem("weighed_done"), sem("w_ready")
        y_done, y_added = sem("y_done"), sem("y_added")
        weigh_step = sem("weigh_step")
        squares, stats, out_ready = sem("squares5"), sem("stats5"), sem("out_ready")
        x2_landed, out_stored = sem("x2_landed"), sem("out_stored")
        pieces = 2 * TT
        block = own.enter_context(nc.Block())

        @block.sync
        def _(sp):
            def load_u(g):
                sp.dma_start(u_raw[:], a.u[bass.ds(g * JG, JG), :, :].rearrange("j p d -> p j d")).then_inc(u_landed, 16)

            def load_v(g):
                sp.dma_start(v_raw[:], a.v[bass.ds(g * JG, JG), :, :].rearrange("j p d -> p j d")).then_inc(v_landed, 16)

            def load_gates(g):
                n = NTB * JG * TB
                sp.dma_start(gates[:].rearrange("p b j t -> p (b j t)"), a.gates[:, bass.ds(g * n, n)]
                             ).then_inc(gates_landed, 16)
            load_u(0)
            load_v(0)
            load_gates(0)
            sp.wait_ge(u_lo, JG)
            load_u(1)
            with sp.Fori(0, GROUPS - 2) as g:
                sp.wait_ge(v_lo, g * JG + JG)
                load_v(g + 1)
                sp.wait_ge(weighed_done, g * JG + JG)
                load_gates(g + 1)
                sp.wait_ge(u_lo, g * JG + 2 * JG)
                load_u(g + 2)
            sp.wait_ge(v_lo, (GROUPS - 1) * JG)
            load_v(GROUPS - 1)
            sp.wait_ge(weighed_done, (GROUPS - 1) * JG)
            load_gates(GROUPS - 1)
            sp.wait_ge(u_lo, GROUPS * JG)
            sp.dma_start(u_raw[:], a.x2).then_inc(x2_landed, 16)
            for t in range(TT):
                sp.wait_ge(out_ready, t + 1)
                sp.dma_start(a.out[t * P:(t + 1) * P, :], u_raw[:, t, :]).then_inc(out_stored, 16)
            sp.wait_ge(out_stored, 16 * TT)

        @block.gpsimd
        def _(pool):
            nc.gpsimd.memset(y[:], 0.0).then_inc(y_added, 1)

        @block.scalar
        def _(act):
            def hi_of_u(g):
                act.wait_ge(u_landed, g * 16 + 16)
                for j in range(JG):
                    nc.scalar.activation(u[:, 0, j, :], u_raw[:, j, :], ACT.Copy).then_inc(u_hi, 1)

            def activations(g):
                act.wait_ge(v_landed, g * 16 + 16)
                act.wait_ge(y_added, g * pieces + 1)
                for j in range(JG):
                    nc.scalar.activation(v[:, 0, j, :], v_raw[:, j, :], ACT.Copy).then_inc(v_hi, 1)
                    act.wait_ge(a_done, g * JG + (j + 1))
                    if j >= 2:
                        act.wait_ge(weighed_done, g * JG + (j - 1))
                    nc.scalar.activation(act_out[:, j % 2, :], m.psum[j % 2][:], ACT.Gelu).then_inc(gelus, 1)
            hi_of_u(0)
            with act.Fori(0, GROUPS - 1) as g:
                activations(g)
                hi_of_u(g + 1)
            activations(GROUPS - 1)
            act.wait_ge(y_added, GROUPS * pieces + 1)
            for t in range(TT):
                m.act.then(act, nc.scalar.activation(v_raw[:, t, :], y[:, t, :], ACT.Square,
                                                     accum_out=m.ss[:, t:t + 1]))
            nc.scalar.activation(m.rstd[:], m.ss[:], ACT.Sqrt, bias=m.eps[:, 0:1], scale=1.0 / D).then_inc(stats, 1)

        @block.vector
        def _(dve):
            V = nc.vector

            def lo_of_u(g):
                for j in range(JG):
                    dve.wait_ge(u_hi, g * JG + (j + 1))
                    V.tensor_tensor(u[:, 1, j, :], u_raw[:, j, :], u[:, 0, j, :].bitcast(F32), ALU.subtract
                                    ).then_inc(u_lo, 1)

            def weigh(g):
                dve.wait_ge(gates_landed, g * 16 + 16)
                for j in range(JG):
                    dve.wait_ge(v_hi, g * JG + (j + 1))
                    V.tensor_tensor(v[:, 1, j, :], v_raw[:, j, :], v[:, 0, j, :].bitcast(F32), ALU.subtract
                                    ).then_inc(v_lo, 1)
                    dve.wait_ge(gelus, g * JG + (j + 1))
                    V.tensor_tensor(weighed[:, j % 2, :].rearrange("p (b t) -> p b t", t=TB),
                                    act_out[:, j % 2, :].rearrange("p (b t) -> p b t", t=TB), gates[:, :, j, :],
                                    ALU.mult).then_inc(weighed_done, 1)
                    dve.wait_ge(weighed_done, g * JG + (j + 1))
                    V.tensor_copy(w[:, 0, j, :], weighed[:, j % 2, :]).then_inc(weigh_step, 1)
                    dve.wait_ge(weigh_step, g * JG + (j + 1))
                    V.tensor_tensor(w[:, 1, j, :], weighed[:, j % 2, :], w[:, 0, j, :].bitcast(F32), ALU.subtract
                                    ).then_inc(w_ready, 1)

            def add(g):
                for p in range(pieces):
                    t, half = p % TT, p // TT
                    dve.wait_ge(y_done, g * pieces + (p + 1))
                    part = y[:, t, half * S:(half + 1) * S]
                    V.tensor_tensor(part, part, m.psum[2 + p % 6][:], ALU.add).then_inc(y_added, 1)
            lo_of_u(0)
            dve.wait_ge(y_added, 1)
            with dve.Fori(0, GROUPS - 1) as g:
                weigh(g)
                lo_of_u(g + 1)
                add(g)
            weigh(GROUPS - 1)
            add(GROUPS - 1)
            dve.wait_ge(stats, 1)
            m.dve.then(dve, V.reciprocal(m.rstd[:], m.rstd[:]))
            dve.wait_ge(x2_landed, 16)
            for t in range(TT):
                m.dve.then(dve, V.scalar_tensor_tensor(y[:, t, :], y[:, t, :], m.rstd[:, t:t + 1], m.rowg[:, 1, :],
                                                       ALU.mult, ALU.mult))
                V.tensor_tensor(u_raw[:, t, :], u_raw[:, t, :], y[:, t, :], ALU.add).then_inc(out_ready, 1)

        @block.tensor
        def _(pe):
            with pe.Fori(0, GROUPS) as g:
                for j in range(JG):
                    pe.wait_ge(u_lo, g * JG + (j + 1))
                    if j >= 2:
                        pe.wait_ge(gelus, g * JG + (j - 1))
                    for kc in range(KC):
                        for i, (p, q) in enumerate(PASSES):
                            last = nc.tensor.matmul(m.psum[j % 2][:], u[:, p, j, kc * P:(kc + 1) * P],
                                                    m.actT[:, q, kc, :], start=(kc == 0 and i == 0),
                                                    stop=(kc == KC - 1 and i == 2))
                    last.then_inc(a_done, 1)

                def piece(p, j):
                    t, half = p % TT, p // TT
                    for i, (x, z) in enumerate(PASSES):
                        last = nc.tensor.matmul(m.psum[2 + p % 6][:], w[:, x, j, t * P:(t + 1) * P],
                                                v[:, z, j, half * S:(half + 1) * S], start=(j == 0 and i == 0),
                                                stop=(j == JG - 1 and i == 2))
                    if j == JG - 1:
                        last.then_inc(y_done, 1)
                pe.wait_ge(y_added, g * pieces + 1)
                for j in range(JG):
                    pe.wait_ge(v_lo, g * JG + (j + 1))
                    pe.wait_ge(w_ready, g * JG + (j + 1))
                    for p in range(TT):
                        piece(p, j)
                for p in range(TT, pieces):
                    if p >= 6:
                        pe.wait_ge(y_added, g * pieces + (p - 4))
                    for j in range(JG):
                        piece(p, j)



def kernel(**inputs):
    import numpy as np
    import concourse.bacc as bacc
    from concourse.bass_utils import run_bass_kernel_spmd

    def get(name):
        return np.asarray(inputs[name])

    def columns(w):
        n = w.shape[1] // P
        return w.reshape(KC, P, n, P).transpose(2, 1, 0, 3).reshape(n, P, KC * P)

    def rows(w):
        n = w.shape[1] // S
        return w.reshape(KC // 2, 2, P, n, S).transpose(3, 0, 2, 1, 4).reshape(n * KC // 2, P, 2 * S)

    def by_partition(vec):
        return vec.reshape(-1, P).T

    w_in, w_ada = get("w_in")[0], get("w_ada")[0]
    parts = [w_in[:, i * S:(i + 1) * S] for i in range(7)]
    theta = get("lb_theta")
    arrays = {
        "x": get("x")[0],
        "c": by_partition(get("c")[0]),
        "w_ada": w_ada.reshape(KC, P, 48 // ADA, ADA, P).transpose(2, 1, 3, 0, 4),
        "b_ada": by_partition(get("b_ada")[0]),
        "gains": np.stack([by_partition(get(n)[0]) for n in ("g_pre_mix", "g_post_mix", "g_pre_ffn", "g_post_ffn")],
                          axis=1),
        "w_cols": np.concatenate([columns(parts[i]) for i in (0, 1, 3, 4)]),
        "w_rows": np.concatenate([rows(parts[i]) for i in (2, 5, 6)]),
        "small": np.concatenate([np.tile(get("lam_qk")[0].reshape(1, -1), (P, 1)), by_partition(theta[0]),
                                 by_partition(theta[1]), np.tile(get("g_diff_sub"), (P, 1)),
                                 np.tile(get("g_hgrn_out"), (P, 1))], axis=1),
        "w_out": rows(get("w_out")[0]),
        "w_pq": columns(get("w_pq")[0]),
        "keys": get("sub_keys")[0].transpose(3, 0, 1, 2).reshape(P, HJ * NKEY),
        "u": get("expert_u")[0].reshape(NKEY, NKEY, KC, P).transpose(1, 3, 2, 0).reshape(NKEY, P, D),
        "v": get("expert_v")[0].reshape(NKEY, NKEY, D).transpose(1, 0, 2),
    }
    nc = bacc.Bacc("TRN2", target_bir_lowering=False, num_devices=1)
    a = Memory()
    for name, value in arrays.items():
        arrays[name] = value = np.ascontiguousarray(value)
        a.__dict__[name] = nc.dram_tensor(f"in_{name}", value.shape, F32, kind="ExternalInput").ap()
    a.x2 = nc.dram_tensor("x2", (P, TT, D), F32).ap()
    a.gates = nc.dram_tensor("expert_gates", (P, DROW), F32).ap()
    a.out = nc.dram_tensor("out", (S, D), F32, kind="ExternalOutput").ap()
    build(nc, a)
    r = run_bass_kernel_spmd(nc, [{f"in_{k}": v for k, v in arrays.items()}], core_ids=[0])
    return r.results[0]["out"].reshape(1, S, D)
```

```python
from contextlib import ExitStack

import concourse.bass as bass
from concourse import mybir

F32 = mybir.dt.float32
F32R = mybir.dt.float32r
BF16 = mybir.dt.bfloat16
U32 = mybir.dt.uint32
ALU = mybir.AluOpType
ACT = mybir.ActivationFunctionType
AX_X = mybir.AxisListType.X

P = 128
D = 1024
S = 512
TT = S // P
KC = D // P
HEADS = 4
HD = 128
QK = 64
W4 = HEADS * S
PH = 8
TOPK = 16
NKEY = 128
HJ = 2 * PH
LAM_INIT = 0.2
EPS = 1e-6
NEG = -1e30
LOWEST = -3.0e38

RAW = 4
SPLIT = 2
UNIT = 1024

JG = 4
GROUPS = NKEY // JG
TB = 32
NTB = S // TB


class Steps:

    def __init__(self, sem):
        self.sem = sem
        self.n = 0

    def then(self, eng, ins):
        self.n += 1
        ins.then_inc(self.sem, 1)
        eng.wait_ge(self.sem, self.n)


class LoopSteps:

    def __init__(self, sem, i, each):
        self.sem, self.i, self.each = sem, i, each
        self.n = 0

    def then(self, eng, ins):
        self.n += 1
        ins.then_inc(self.sem, 1)
        eng.wait_ge(self.sem, self.i * self.each + self.n)

    def done(self):
        assert self.n == self.each, self.n


class Memory:
    pass


def build(nc, a):
    with ExitStack() as outer:
        m = Memory()

        def sb(name, shape, dt=F32, stack=outer):
            return stack.enter_context(nc.sbuf_tensor(name, shape, dt))

        def sem(name):
            return outer.enter_context(nc.semaphore(name))

        m.sb, m.sem = sb, sem
        m.psum = [outer.enter_context(nc.psum_tensor(f"bank{i}", [P, 512], F32)) for i in range(8)]
        m.dve = Steps(sem("dve_step"))
        m.act = Steps(sem("act_step"))
        m.pool = Steps(sem("pool_step"))

        m.ident = sb("ident", [P, P])
        m.ident_bf = sb("ident_bf", [P, P], BF16)
        m.ones = sb("ones", [P, P])
        m.eps = sb("eps", [P, 1])
        m.zero = sb("zero", [P, 1])
        m.mod = sb("mod", [P, 48])
        m.bada = sb("bada", [P, 48])
        m.gains = sb("gains", [P, 4, KC])
        m.cact = sb("cact", [P, KC])
        m.scale = sb("norm_scale", [P, KC])
        m.rowg = sb("rowg", [P, 2, D])
        m.ss = sb("sumsq", [P, TT])
        m.rstd = sb("rstd", [P, TT])
        m.rows = sb("rows", [P, TT, D])

        m.unit_landed = [sem(f"unit_landed{i}") for i in range(RAW)]
        m.unit_hi = sem("unit_hi")
        m.unit_lo = sem("unit_lo")
        m.unit_used = sem("unit_used")
        m.unit_evac = sem("unit_evac")
        m.units = 0
        m.evacs = 0

        stage_project(nc, a, m)
        stage_mix(nc, a, m)
        m.actT = sb("actT", [P, 2, KC, S], F32R)
        stage_join(nc, a, m)
        m.slotsT = sb("slotsT", [P, 3, S])
        stage_select(nc, a, m)
        m.u_raw = sb("u_raw", [P, JG, D])
        m.v_raw = sb("v_raw", [P, JG, D])
        m.early_in = sb("early_in", [P, JG, S])
        m.u_landed = sem("u_landed")
        m.early_landed = [sem(f"early_landed{j}") for j in range(JG)]
        stage_gates(nc, a, m)
        stage_experts(nc, a, m)



def units_load(nc, sp, m, src, raw, n0, count):
    def body(i, first):
        for u in range(RAW):
            if not (first and n0 == 0):
                sp.wait_ge(m.unit_lo, i + (n0 - RAW + 1 + u))
            sp.dma_start(raw[:, u, :], src[bass.ds(i + u, 1), :, :].rearrange("a p f -> p (a f)")
                         ).then_inc(m.unit_landed[u], 16)
    body(0, True)
    with sp.Fori(1, count // RAW) as k:
        body(k * RAW, False)


def units_hi(nc, act, m, raw, hl, n0, count):
    def body(i, k, first):
        for u in range(RAW):
            act.wait_ge(m.unit_landed[u], k * 16 + (n0 // RAW + 1) * 16)
            if not (first and n0 == 0 and u < SPLIT):
                act.wait_ge(m.unit_used, i + (n0 - SPLIT + 1 + u))
            nc.scalar.activation(hl[:, 0, u % SPLIT, :], raw[:, u, :], ACT.Copy).then_inc(m.unit_hi, 1)
    body(0, 0, True)
    with act.Fori(1, count // RAW) as k:
        body(k * RAW, k, False)


def unit_lo(nc, dve, m, raw, hl, u, n):
    dve.wait_ge(m.unit_hi, n + 1)
    nc.vector.tensor_tensor(hl[:, 1, u % SPLIT, :], raw[:, u, :], hl[:, 0, u % SPLIT, :].bitcast(F32),
                            ALU.subtract).then_inc(m.unit_lo, 1)


PASSES = ((0, 0), (0, 1), (1, 0))


def column_units_pe(nc, pe, m, hl, n0, e0, count):
    def body(i, first):
        for u in range(RAW):
            pe.wait_ge(m.unit_lo, i + (n0 + 1 + u))
            if not (first and e0 == 0 and u < 2):
                pe.wait_ge(m.unit_evac, i + (e0 - 1 + u))
            bank = m.psum[u % 2]
            for kc in range(KC):
                for j, (a, b) in enumerate(PASSES):
                    last = nc.tensor.matmul(bank[:], hl[:, a, u % SPLIT, kc * P:(kc + 1) * P],
                                            m.actT[:, b, kc, :], start=(kc == 0 and j == 0),
                                            stop=(kc == KC - 1 and j == 2))
            last.then_inc(m.unit_used, 1)
    body(0, True)
    with pe.Fori(1, count // RAW) as k:
        body(k * RAW, False)


def column_units_dve(nc, dve, m, raw, hl, dst, n0, e0, count):
    unit_lo(nc, dve, m, raw, hl, 0, n0)

    def body(i, last):
        for u in range(RAW):
            if not (last and u == RAW - 1):
                unit_lo(nc, dve, m, raw, hl, (u + 1) % RAW, i + (n0 + u + 1))
            dve.wait_ge(m.unit_used, i + (n0 + u + 1))
            nc.vector.tensor_copy(dst[:, bass.ds(i * S + u * S, S)], m.psum[u % 2][:]).then_inc(m.unit_evac, 1)
    with dve.Fori(0, count // RAW - 1) as k:
        body(k * RAW, False)
    body(count - RAW, True)


def row_units_pe(nc, pe, m, hl, n0, e0, groups):
    def body(g, parity, first):
        for u in range(RAW):
            pe.wait_ge(m.unit_lo, g * RAW + (n0 + 1 + u))
            for t in range(TT):
                if u == 0 and not first:
                    pe.wait_ge(m.unit_evac, g * TT + (e0 - TT + t + 1))
                for c in range(2):
                    kc = 2 * u + c
                    for j, (a, b) in enumerate(PASSES):
                        last = nc.tensor.matmul(m.psum[4 + t][:], m.actT[:, a, kc, t * P:(t + 1) * P],
                                                hl[:, b, u % SPLIT, c * S:(c + 1) * S],
                                                start=(kc == 0 and j == 0), stop=(kc == KC - 1 and j == 2))
            last.then_inc(m.unit_used, 1)
    body(0, 0, True)
    with pe.Fori(1, groups) as g:
        body(g, 0, False)


def row_units_dve(nc, dve, m, raw, hl, dst, n0, e0, groups):
    unit_lo(nc, dve, m, raw, hl, 0, n0)

    def body(g, last):
        for u in range(RAW):
            if not (last and u == RAW - 1):
                unit_lo(nc, dve, m, raw, hl, (u + 1) % RAW, g * RAW + (n0 + u + 1))
        dve.wait_ge(m.unit_used, g * RAW + (n0 + RAW))
        for t in range(TT):
            nc.vector.tensor_copy(dst[:, bass.ds(g * TT * S + t * S, S)], m.psum[4 + t][:]).then_inc(m.unit_evac, 1)
    if groups > 1:
        with dve.Fori(0, groups - 1) as g:
            body(g, False)
    body(groups - 1, True)



ADA = 2


def ada_pe(nc, pe, m, wada, ada_landed, ada_used, c, first):
    pe.wait_ge(ada_landed[c % 2], 16 * (c // 2 + 1))
    for n in range(ADA):
        col = c * ADA + n
        for kc in range(KC):
            last = nc.tensor.matmul(m.psum[7][:, col:col + 1], wada[:, c % 2, n, kc, :], m.cact[:, kc:kc + 1],
                                    start=(kc == 0), stop=(kc == KC - 1))
    last.then_inc(ada_used, 1)



def norm_stats(nc, act, m, x, scratch, rows_ready, out_sem):
    for t in range(TT):
        rows_ready(act, t)
        m.act.then(act, nc.scalar.activation(scratch, x[:, t, :], ACT.Square, accum_out=m.ss[:, t:t + 1]))
    nc.scalar.activation(m.rstd[:], m.ss[:], ACT.Sqrt, bias=m.eps[:, 0:1], scale=1.0 / D).then_inc(out_sem, 1)


def norm_rows_dve(nc, dve, m, x, xn, stats, stats_n, xn_ready):
    dve.wait_ge(stats, stats_n)
    m.dve.then(dve, nc.vector.reciprocal(m.rstd[:], m.rstd[:]))
    for t in range(TT):
        nc.vector.tensor_scalar(xn[:, t, :], x[:, t, :], m.rstd[:, t:t + 1], None, ALU.mult).then_inc(xn_ready, 1)


def transpose_pe(nc, pe, m, xn, banks, xn_ready, bank_free, transposed):
    for dc in range(KC):
        if dc >= 2:
            pe.wait_ge(bank_free, dc - 1)
        for t in range(TT):
            if dc == 0 and xn_ready is not None:
                pe.wait_ge(xn_ready, t + 1)
            last = nc.tensor.transpose(m.psum[banks + dc % 2][:, t * P:(t + 1) * P],
                                       xn[:, t, dc * P:(dc + 1) * P], m.ident[:])
        last.then_inc(transposed, 1)


def split_act(nc, act, m, actT, banks, piece, transposed, bank_free, piece_lo, hi_ready, modulated, sh):
    for dc in range(KC):
        act.wait_ge(transposed, dc + 1)
        if dc >= 2:
            act.wait_ge(piece_lo, dc - 1)
        if modulated:
            ins = nc.scalar.activation(piece[:, dc % 2, :], m.psum[banks + dc % 2][:], ACT.Identity,
                                       scale=m.scale[:, dc:dc + 1], bias=m.mod[:, sh + dc:sh + dc + 1])
        else:
            ins = nc.scalar.activation(piece[:, dc % 2, :], m.psum[banks + dc % 2][:], ACT.Copy)
        ins.then_inc(bank_free, 1)
        act.wait_ge(bank_free, dc + 1)
        nc.scalar.activation(actT[:, 0, dc, :], piece[:, dc % 2, :], ACT.Copy).then_inc(hi_ready, 1)


def split_dve(nc, dve, actT, piece, hi_ready, piece_lo):
    for dc in range(KC):
        dve.wait_ge(hi_ready, dc + 1)
        nc.vector.tensor_tensor(actT[:, 1, dc, :], piece[:, dc % 2, :], actT[:, 0, dc, :].bitcast(F32),
                                ALU.subtract).then_inc(piece_lo, 1)



def stage_project(nc, a, m):
    m.keep = ExitStack()
    m.projT = m.sb("projT", [P, 4 * W4], F32, m.keep)
    m.projN = m.sb("projN", [P, 3 * TT * S], F32, m.keep)
    m.wada = m.sb("wada", [P, 2, ADA, KC, P], F32, m.keep)
    m.ada_landed = [m.sem("ada_landed0"), m.sem("ada_landed1")]
    m.ada_used = m.sem("ada_used")
    with ExitStack() as own:
        x = m.rows
        m.actT = m.sb("actT1", [P, 2, KC, S], F32R, own)
        xn = m.projN[:, 0:TT * D].rearrange("p (t d) -> p t d", t=TT)
        raw = m.sb("raw1", [P, RAW, UNIT], F32, own)
        hl = m.sb("hl1", [P, 2, SPLIT, UNIT], F32R, own)
        piece = m.sb("piece1", [P, 2, S], F32, own)
        scratch = m.sb("scratch1", [P, D], F32, own)
        x_landed = [m.sem(f"x_tile{t}_landed") for t in range(TT)]
        small = m.sem("small_landed")
        ident_ready = m.sem("ident_ready")
        const_ready = m.sem("const_ready")
        c_ready = m.sem("c_ready")
        stats = m.sem("stats1")
        xn_ready = m.sem("xn_ready1")
        transposed = m.sem("transposed1")
        bank_free = m.sem("bank_free1")
        hi_ready = m.sem("hi_ready1")
        piece_lo = m.sem("piece_lo1")
        scale_ready = m.sem("scale_ready1")
        first_chunks = 16 // ADA
        block = own.enter_context(nc.Block())

        @block.sync
        def _(sp):
            for t in range(TT):
                sp.dma_start(x[:, t, :], a.x[t * P:(t + 1) * P, :]).then_inc(x_landed[t], 16)
                if t == 0:
                    sp.dma_start(m.cact[:], a.c).then_inc(small, 16)
                    sp.dma_start(m.bada[:], a.b_ada).then_inc(small, 16)
                    sp.dma_start(m.gains[:], a.gains).then_inc(small, 16)
            for c in range(first_chunks):
                if c >= 2:
                    sp.wait_ge(m.ada_used, c - 1)
                sp.dma_start(m.wada[:, c % 2], a.w_ada[c]).then_inc(m.ada_landed[c % 2], 16)
            units_load(nc, sp, m, a.w_cols, raw, 0, 16)
            units_load(nc, sp, m, a.w_rows, raw, 16, 12)

        @block.gpsimd
        def _(pool):
            m.pool.then(pool, nc.gpsimd.memset(m.ident[:], 0.0))
            m.pool.then(pool, nc.gpsimd.affine_select(
                out=m.ident[:], in_=m.ident[:], compare_op=ALU.not_equal, fill=1.0, base=0,
                pattern=[[-1, P]], channel_multiplier=1))
            nc.gpsimd.tensor_copy(m.ident_bf[:], m.ident[:]).then_inc(ident_ready, 1)
            nc.gpsimd.memset(m.ones[:], 1.0).then_inc(const_ready, 1)
            nc.gpsimd.memset(m.eps[:], EPS).then_inc(const_ready, 1)
            nc.gpsimd.memset(m.zero[:], 0.0).then_inc(const_ready, 1)

        @block.scalar
        def _(act):
            act.wait_ge(const_ready, 3)
            act.wait_ge(small, 48)
            nc.scalar.activation(m.cact[:], m.cact[:], ACT.Silu).then_inc(c_ready, 1)
            norm_stats(nc, act, m, x, scratch[:], lambda e, t: e.wait_ge(x_landed[t], 16), stats)
            act.wait_ge(scale_ready, 1)
            split_act(nc, act, m, m.actT, 0, piece, transposed, bank_free, piece_lo, hi_ready, True, 0)
            units_hi(nc, act, m, raw, hl, 0, 16)
            units_hi(nc, act, m, raw, hl, 16, 12)

        @block.vector
        def _(dve):
            norm_rows_dve(nc, dve, m, x, xn, stats, 1, xn_ready)
            dve.wait_ge(m.ada_used, first_chunks)
            m.dve.then(dve, nc.vector.tensor_tensor(m.mod[:, 0:16], m.psum[7][:, 0:16], m.bada[:, 0:16], ALU.add))
            nc.vector.scalar_tensor_tensor(m.scale[:], m.mod[:, 8:16], 1.0, m.gains[:, 0, :],
                                           ALU.add, ALU.mult).then_inc(scale_ready, 1)
            split_dve(nc, dve, m.actT, piece, hi_ready, piece_lo)
            column_units_dve(nc, dve, m, raw, hl, m.projT, 0, 0, 16)
            row_units_dve(nc, dve, m, raw, hl, m.projN, 16, 16, 3)

        @block.tensor
        def _(pe):
            pe.wait_ge(ident_ready, 1)
            pe.wait_ge(c_ready, 1)
            for c in range(first_chunks):
                ada_pe(nc, pe, m, m.wada, m.ada_landed, m.ada_used, c, c == 0)
            transpose_pe(nc, pe, m, xn, 0, xn_ready, bank_free, transposed)
            pe.wait_ge(piece_lo, KC)
            column_units_pe(nc, pe, m, hl, 0, 0, 16)
            row_units_pe(nc, pe, m, hl, 16, 16, 3)
    m.units, m.evacs = 28, 28



LEVELS = ("own", 8, 16, 32, 64)
OWN = 8
OWN_REF = 3
CHUNK = P
NCH = S // CHUNK
STEPS_A = HEADS * TT
ADA_CHUNKS = 32 // ADA
LEVEL_AT = 8
ITEMS = {1: 0, 3: 1, 5: 2, 7: 3, 9: 4, 11: "kb"}
SLOT_E = (0, 0, 1, 0, 1)
SLOT_F = ((0, 1), (2, 2), (3, 3), (0, 0), (1, 1))


def stage_mix(nc, a, m):
    with ExitStack() as own:
        def sb(name, shape, dt=F32):
            return m.sb(name, shape, dt, own)

        cat = m.rows
        q = m.projT[:, 2 * W4:3 * W4]
        f = m.projT[:, 3 * W4:4 * W4]
        av = m.projN[:, 0:TT * S].rearrange("p (t n) -> p t n", t=TT)
        hi = m.projN[:, TT * S:2 * TT * S].rearrange("p (t n) -> p t n", t=TT)
        hg = m.projN[:, 2 * TT * S:3 * TT * S]
        kk = sb("kk", [P, W4])
        b = sb("b", [P, W4])
        E = sb("E", [P, 2, W4])
        F = sb("F", [P, 4, W4])
        attnT = sb("attnT", [P, HEADS, S])
        kbT = sb("kbT", [P, NCH - 1, HEADS * HD])
        state = sb("state", [P, NCH - 1, HEADS * HD])
        prob = sb("prob", [P, 2, S])
        mixed = sb("mixed", [P, 2, S])
        mixedT = sb("mixedT", [P, 2, S])
        masks = sb("masks", [P, len(LEVELS), P])
        negmask = sb("negmask", [P, P], BF16)
        small = sb("small2", [P, 2 * 2 * QK + 2 * HEADS + 2 * HD])
        restart = sb("restart", [P, W4], BF16)
        decay = sb("decay", [P, HEADS * NCH])
        lamp = sb("lamp", [P, 2 * QK])
        lams = sb("lams", [P, 4])
        lb = sb("lb", [P, 2, HEADS])
        nbias = sb("nbias", [P, 2, 2])
        Z = sb("Z", [P, 2, 2])
        rz = sb("rz", [P, 2, 2])
        ss = sb("ss2", [P, TT, 2 * HEADS])
        lam = small[:, 0:4 * QK]
        theta = small[:, 4 * QK:4 * QK + 2 * HEADS]
        g_diff = small[:, 4 * QK + 2 * HEADS:4 * QK + 2 * HEADS + HD]
        g_hgrn = small[:, 4 * QK + 2 * HEADS + HD:]

        small_landed = m.sem("small_landed2")
        masks_ready = m.sem("masks_ready")
        sig_ready = m.sem("sig_ready")
        gate_ready = m.sem("gate_ready")
        log_ready = m.sem("log_ready")
        hg_ready = m.sem("hg_ready")
        lam_sums = m.sem("lam_sums")
        lam_exps = m.sem("lam_exps")
        theta_diff = m.sem("theta_diff")
        scores = m.sem("scores")
        bias_ready = m.sem("bias_ready")
        probs_ready = m.sem("probs_ready")
        mixed_ready = m.sem("mixed_ready")
        mixed_tr = m.sem("mixed_tr")
        mixedT_ready = m.sem("mixedT_ready")
        attn_out = m.sem("attn_out")
        attn_read = m.sem("attn_read")
        diff_ready = m.sem("diff_ready")
        exp_ready = m.sem("exp_ready")
        f_ready = m.sem("f_ready")
        level_done = m.sem("level_done")
        level_copied = m.sem("level_copied")
        mod_read = m.sem("mod_read2")
        kb_tr = m.sem("kb_tr")
        kbT_ready = m.sem("kbT_ready")
        kv_done = m.sem("kv_done")
        state_ready = m.sem("state_ready")
        hgrn_out = m.sem("hgrn_out")
        hgrn_read = m.sem("hgrn_read")
        squares = m.sem("squares")
        sums = m.sem("sums")
        roots = m.sem("roots")

        block = own.enter_context(nc.Block())
        b_k = b[:].rearrange("p (n c) -> p n c", c=CHUNK)
        last_b = b_k[:, :, CHUNK - 1:CHUNK]

        @block.sync
        def _(sp):
            sp.dma_start(small[:], a.small).then_inc(small_landed, 16)
            for c in range(16 // ADA, 48 // ADA):
                sp.wait_ge(m.ada_used, c - 1)
                sp.dma_start(m.wada[:, c % 2], a.w_ada[c]).then_inc(m.ada_landed[c % 2], 16)

        @block.gpsimd
        def _(pool):
            g = nc.gpsimd
            m.pool.then(pool, g.memset(restart[:], 1.0))
            g.memset(restart[:].rearrange("p (n c) -> p n c", c=CHUNK)[:, :, 0:1], 0.0).then_inc(masks_ready, 1)
            m.pool.then(pool, g.memset(negmask[:], 0.0))
            g.affine_select(out=negmask[:], in_=negmask[:], compare_op=ALU.is_ge, fill=NEG, base=0,
                            pattern=[[-1, P]], channel_multiplier=1).then_inc(masks_ready, 1)
            m.pool.then(pool, g.memset(masks[:], 0.0))
            own_mask = masks[:, 0, :].rearrange("p (n c) -> p n c", c=OWN)
            m.pool.then(pool, g.memset(masks[:, 0, :], 1.0))
            m.pool.then(pool, g.affine_select(out=own_mask, in_=own_mask, compare_op=ALU.is_ge, fill=0.0, base=0,
                                              pattern=[[-OWN, P // OWN], [0, OWN]], channel_multiplier=1))
            m.pool.then(pool, g.affine_select(out=own_mask, in_=own_mask, compare_op=ALU.is_ge, fill=0.0, base=0,
                                              pattern=[[OWN, P // OWN], [1, OWN]], channel_multiplier=-1))
            for level in range(1, len(LEVELS)):
                h = LEVELS[level]
                right = masks[:, level, :].rearrange("p (n c) -> p n c", c=2 * h)[:, :, h:2 * h]
                m.pool.then(pool, g.memset(right, 1.0))
                m.pool.then(pool, g.affine_select(out=right, in_=right, compare_op=ALU.is_ge, fill=0.0, base=0,
                                                  pattern=[[-2 * h, P // (2 * h)], [0, h]], channel_multiplier=1))
                m.pool.then(pool, g.affine_select(out=right, in_=right, compare_op=ALU.is_ge, fill=0.0, base=h - 1,
                                                  pattern=[[2 * h, P // (2 * h)], [0, h]], channel_multiplier=-1))
            g.memset(attnT[:], 0.0).then_inc(masks_ready, 1)
            pool.wait_ge(log_ready, 1)
            pool.wait_ge(exp_ready, 1)
            g.tensor_tensor(F[:, 0, :], E[:, 0, :], kk[:], ALU.mult).then_inc(f_ready, 1)
            g.tensor_tensor(F[:, 1, :], E[:, 1, :], q, ALU.mult).then_inc(f_ready, 1)
            for level in range(1, len(LEVELS)):
                h = LEVELS[level]
                pool.wait_ge(exp_ready, level + 1)
                if level == 3:
                    pool.wait_ge(level_done, HEADS)
                out = F[:, SLOT_F[level][0], :].rearrange("p (n c) -> p n c", c=2 * h)
                e = E[:, SLOT_E[level], :].rearrange("p (n c) -> p n c", c=2 * h)
                kv = kk[:].rearrange("p (n c) -> p n c", c=2 * h)
                qv = q.rearrange("p (n c) -> p n c", c=2 * h)
                g.tensor_tensor(out[:, :, 0:h], e[:, :, 0:h], kv[:, :, 0:h], ALU.mult).then_inc(f_ready, 1)
                g.tensor_tensor(out[:, :, h:], e[:, :, h:], qv[:, :, h:], ALU.mult).then_inc(f_ready, 1)
            pool.wait_ge(exp_ready, len(LEVELS) + 1)
            pool.wait_ge(level_done, 3 * HEADS)
            g.tensor_tensor(F[:, 2, :], E[:, 0, :], q, ALU.mult).then_inc(f_ready, 1)
            g.tensor_tensor(F[:, 3, :], E[:, 1, :], kk[:], ALU.mult).then_inc(f_ready, 1)
            pool.wait_ge(hg_ready, 1)
            g.tensor_tensor(hg.rearrange("p (n c) -> p n c", c=HD), hg.rearrange("p (n c) -> p n c", c=HD),
                            g_hgrn.unsqueeze(1).to_broadcast([P, TT * HEADS, HD]), ALU.mult).then_inc(hg_ready, 1)

        @block.scalar
        def _(act):
            A = nc.scalar.activation
            act.wait_ge(theta_diff, 1)
            A(lb[:, 0, :], theta[:, 0:HEADS], ACT.Sigmoid).then_inc(sig_ready, 1)
            A(f, f, ACT.Sigmoid).then_inc(sig_ready, 1)
            A(q, q, ACT.Silu).then_inc(sig_ready, 1)
            A(hg, hg, ACT.Silu).then_inc(hg_ready, 1)
            act.wait_ge(gate_ready, 1)
            act.wait_ge(sig_ready, 3)
            A(f, f, ACT.Ln).then_inc(log_ready, 1)
            act.wait_ge(lam_sums, 1)
            A(lams[:, 2:4], lams[:, 0:2], ACT.Exp).then_inc(lam_exps, 1)
            for n in range(STEPS_A + 1):
                if n < STEPS_A:
                    k = (n % TT + 1) * P
                    act.wait_ge(bias_ready, n + 1)
                    if n >= 1:
                        act.wait_ge(mixed_ready, n)
                    for j in range(2):
                        A(prob[:, j, 0:k], m.psum[2 * (n % 2) + j][:, 0:k], ACT.Exp, bias=nbias[:, n % 2, j:j + 1],
                          scale=QK ** -0.5, accum_out=Z[:, n % 2, j:j + 1]).then_inc(probs_ready, 1)
                if n >= 1:
                    k = ((n - 1) % TT + 1) * P
                    act.wait_ge(mixed_tr, n)
                    if n >= 3:
                        act.wait_ge(attn_out, n - 2)
                    A(mixedT[:, (n - 1) % 2, 0:k], m.psum[4][:, 0:k], ACT.Copy).then_inc(mixedT_ready, 1)
                item = ITEMS.get(n)
                if item == 0:
                    act.wait_ge(diff_ready, 1)
                    m.act.then(act, A(E[:, 1, :], E[:, 0, :], ACT.Exp))
                    A(E[:, 0, :], E[:, 0, :], ACT.Exp, scale=-1.0).then_inc(exp_ready, 1)
                elif item == "kb":
                    act.wait_ge(diff_ready, len(LEVELS) + 1)
                    m.act.then(act, A(decay[:].rearrange("p (n o) -> p n o", o=1), last_b, ACT.Exp))
                    m.act.then(act, A(E[:, 0, :], b[:], ACT.Exp))
                    A(E[:, 1, :], E[:, 1, :], ACT.Exp).then_inc(exp_ready, 1)
                elif item is not None:
                    h = LEVELS[item]
                    act.wait_ge(diff_ready, item + 1)
                    e = E[:, SLOT_E[item], :].rearrange("p (n c) -> p n c", c=2 * h)
                    m.act.then(act, A(e[:, :, 0:h], e[:, :, 0:h], ACT.Exp, scale=-1.0))
                    A(e[:, :, h:], e[:, :, h:], ACT.Exp).then_inc(exp_ready, 1)
            for n in range(NCH - 1):
                act.wait_ge(kb_tr, n + 1)
                A(kbT[:, n, :], m.psum[n % 2][:], ACT.Copy).then_inc(kbT_ready, 1)
            for t in range(TT):
                act.wait_ge(hgrn_read, t + 1)
                if t >= 2:
                    act.wait_ge(sums, t - 1)
                A(E[:, t % 2, 0:D], cat[:, t, :], ACT.Square).then_inc(squares, 1)
            act.wait_ge(sums, TT)
            A(ss[:], ss[:], ACT.Sqrt, bias=m.eps[:, 0:1], scale=1.0 / HD).then_inc(roots, 1)

        @block.vector
        def _(dve):
            V = nc.vector
            dve.wait_ge(small_landed, 16)
            V.tensor_tensor(theta[:, 0:HEADS], theta[:, 0:HEADS], theta[:, HEADS:2 * HEADS],
                            ALU.subtract).then_inc(theta_diff, 1)
            lv = lam.rearrange("p (a b) -> p a b", b=2 * QK)
            m.dve.then(dve, V.tensor_tensor(lamp[:].rearrange("p (a b) -> p a b", b=QK), lv[:, :, 0:QK],
                                            lv[:, :, QK:2 * QK], ALU.mult))
            V.tensor_reduce(lams[:, 0:2], lamp[:].rearrange("p (a b) -> p a b", b=QK), AX_X, ALU.add
                            ).then_inc(lam_sums, 1)
            m.dve.then(dve, V.tensor_scalar(g_diff, g_diff, 1.0 - LAM_INIT, None, ALU.mult))
            dve.wait_ge(sig_ready, 2)
            m.dve.then(dve, V.tensor_scalar(lb[:, 1, :], lb[:, 0, :], -1.0, 1.0, ALU.mult, ALU.add))
            for h in range(HEADS):
                fh = f[:, h * S:(h + 1) * S]
                m.dve.then(dve, V.tensor_scalar(fh, fh, lb[:, 1, h:h + 1], lb[:, 0, h:h + 1], ALU.mult, ALU.add))
            V.tensor_scalar(kk[:], f, -1.0, 1.0, ALU.mult, ALU.add).then_inc(gate_ready, 1)
            dve.wait_ge(lam_exps, 1)
            m.dve.then(dve, V.tensor_tensor(lams[:, 0:1], lams[:, 3:4], lams[:, 2:3], ALU.subtract))
            m.dve.then(dve, V.tensor_scalar(lams[:, 0:1], lams[:, 0:1], -LAM_INIT, None, ALU.add))
            dve.wait_ge(log_ready, 1)
            dve.wait_ge(masks_ready, 3)
            m.dve.then(dve, V.tensor_tensor_scan(b[:], restart[:], f, 0.0, ALU.mult, ALU.add))

            def level_copies(n):
                for u in range(2 * (n - LEVEL_AT), 2 * (n - LEVEL_AT) + 2):
                    level, h = divmod(u, HEADS)
                    dve.wait_ge(level_done, u + 1)
                    V.copy_predicated(attnT[:, h, :].rearrange("p (n c) -> p n c", c=P),
                                      masks[:, level, :].bitcast(U32).unsqueeze(1).to_broadcast([P, NCH, P]),
                                      m.psum[6 + u % 2][:].rearrange("p (n c) -> p n c", c=P)
                                      ).then_inc(level_copied, 1)

            for n in range(STEPS_A + 2):
                if n < STEPS_A:
                    k = (n % TT + 1) * P
                    dve.wait_ge(scores, n + 1)
                    for j in range(2):
                        m.dve.then(dve, V.tensor_reduce(nbias[:, n % 2, j:j + 1], m.psum[2 * (n % 2) + j][:, 0:k],
                                                        AX_X, ALU.max))
                    V.tensor_scalar(nbias[:, n % 2, :], nbias[:, n % 2, :], -QK ** -0.5, None, ALU.mult
                                    ).then_inc(bias_ready, 1)
                if 1 <= n <= STEPS_A:
                    o = n - 1
                    k = (o % TT + 1) * P
                    dve.wait_ge(probs_ready, 2 * n)
                    if o >= 2:
                        dve.wait_ge(mixed_tr, o - 1)
                    m.dve.then(dve, V.reciprocal(rz[:, o % 2, :], Z[:, o % 2, :]))
                    m.dve.then(dve, V.tensor_scalar(rz[:, o % 2, 1:2], rz[:, o % 2, 1:2], lams[:, 0:1], None, ALU.mult))
                    m.dve.then(dve, V.tensor_scalar(mixed[:, o % 2, 0:k], prob[:, 0, 0:k], rz[:, o % 2, 0:1], None,
                                                    ALU.mult))
                    V.scalar_tensor_tensor(mixed[:, o % 2, 0:k], prob[:, 1, 0:k], rz[:, o % 2, 1:2],
                                           mixed[:, o % 2, 0:k], ALU.mult, ALU.add).then_inc(mixed_ready, 1)
                item = ITEMS.get(n)
                if item is not None:
                    if item == 0:
                        bv = b[:].rearrange("p (n c) -> p n c", c=OWN)
                        e = E[:, 0, :].rearrange("p (n c) -> p n c", c=OWN)
                        ref = bv[:, :, OWN_REF:OWN_REF + 1].to_broadcast([P, W4 // OWN, OWN])
                        V.tensor_tensor(e, bv, ref, ALU.subtract).then_inc(diff_ready, 1)
                    elif item == "kb":
                        dve.wait_ge(f_ready, 2 * len(LEVELS))
                        e = E[:, 1, :].rearrange("p (n c) -> p n c", c=CHUNK)
                        V.tensor_tensor(e, last_b.to_broadcast([P, HEADS * NCH, CHUNK]), b_k, ALU.subtract
                                        ).then_inc(diff_ready, 1)
                    else:
                        dve.wait_ge(f_ready, 2 if item <= 2 else 2 * (item - 1))
                        h = LEVELS[item]
                        bv = b[:].rearrange("p (n c) -> p n c", c=2 * h)
                        e = E[:, SLOT_E[item], :].rearrange("p (n c) -> p n c", c=2 * h)
                        ref = bv[:, :, h - 1:h].to_broadcast([P, W4 // (2 * h), 2 * h])
                        V.tensor_tensor(e, bv, ref, ALU.subtract).then_inc(diff_ready, 1)
                if n >= 2:
                    o = n - 2
                    h, t = divmod(o, TT)
                    dve.wait_ge(attn_out, o + 1)
                    V.tensor_copy(cat[:, t, h * HD:(h + 1) * HD], m.psum[5][:, 0:HD]).then_inc(attn_read, 1)
                if n == LEVEL_AT - 1:
                    dve.wait_ge(m.ada_used, 48 // ADA)
                    V.tensor_tensor(m.mod[:, 16:48], m.psum[7][:, 16:48], m.bada[:, 16:48], ALU.add
                                    ).then_inc(mod_read, 1)
                if n >= LEVEL_AT:
                    level_copies(n)
            for n in range(NCH - 1):
                dve.wait_ge(kv_done, n + 1)
                st = state[:, n, :].rearrange("p (h v) -> p h v", h=HEADS)
                kv = m.psum[2 + n % 2][:].rearrange("p (h v) -> p h v", h=HEADS)
                if n == 0:
                    V.tensor_copy(st, kv).then_inc(state_ready, 1)
                else:
                    dve.wait_ge(state_ready, n)
                    before = state[:, n - 1, :].rearrange("p (h v) -> p h v", h=HEADS)
                    dec = decay[:].rearrange("p (h n) -> p h n", h=HEADS)[:, :, n:n + 1].to_broadcast([P, HEADS, HD])
                    m.dve.then(dve, V.tensor_tensor(st, before, dec, ALU.mult))
                    V.tensor_tensor(st, st, kv, ALU.add).then_inc(state_ready, 1)
            for t in range(TT):
                dve.wait_ge(hgrn_out, t + 1)
                V.tensor_copy(cat[:, t, HEADS * HD:], m.psum[4 + t][:]).then_inc(hgrn_read, 1)
            for t in range(TT):
                dve.wait_ge(squares, t + 1)
                V.tensor_reduce(ss[:, t, :], E[:, t % 2, 0:D].rearrange("p (h v) -> p h v", v=HD), AX_X, ALU.add
                                ).then_inc(sums, 1)
            dve.wait_ge(roots, 1)
            m.dve.then(dve, V.reciprocal(ss[:], ss[:]))
            dve.wait_ge(hg_ready, 2)
            hgv = hg.rearrange("p (t n) -> p t n", t=TT)
            for t in range(TT):
                cv = cat[:, t, :].rearrange("p (h v) -> p h v", v=HD)
                m.dve.then(dve, V.tensor_tensor(cv, cv, ss[:, t, :].unsqueeze(2).to_broadcast([P, 2 * HEADS, HD]),
                                                ALU.mult))
                m.dve.then(dve, V.tensor_tensor(cv[:, 0:HEADS], cv[:, 0:HEADS],
                                                g_diff.unsqueeze(1).to_broadcast([P, HEADS, HD]), ALU.mult))
                m.dve.then(dve, V.tensor_tensor(cat[:, t, HEADS * HD:], cat[:, t, HEADS * HD:], hgv[:, t, :], ALU.mult))

        @block.tensor
        def _(pe):
            T = nc.tensor
            aq, ak = m.projT[:, 0:W4], m.projT[:, W4:2 * W4]
            pe.wait_ge(masks_ready, 3)

            def level_matmuls(n):
                if n == LEVEL_AT:
                    pe.wait_ge(mod_read, 1)
                for u in range(2 * (n - LEVEL_AT), 2 * (n - LEVEL_AT) + 2):
                    level, h = divmod(u, HEADS)
                    pe.wait_ge(f_ready, 2 * level + 2)
                    if u >= 2:
                        pe.wait_ge(level_copied, u - 1)
                    for c in range(NCH):
                        at = slice(h * S + c * CHUNK, h * S + (c + 1) * CHUNK)
                        last = T.matmul(m.psum[6 + u % 2][:, c * CHUNK:(c + 1) * CHUNK], F[:, SLOT_F[level][0], at],
                                        F[:, SLOT_F[level][1], at], start=True, stop=True)
                    last.then_inc(level_done, 1)

            for n in range(STEPS_A + 2):
                if n < STEPS_A:
                    h, t = divmod(n, TT)
                    k = (t + 1) * P
                    if n >= 2:
                        pe.wait_ge(probs_ready, 2 * (n - 1))
                    for j in range(2):
                        part = slice(j * QK, (j + 1) * QK)
                        bank = m.psum[2 * (n % 2) + j]
                        T.matmul(bank[:, 0:k], aq[part, h * S + t * P:h * S + (t + 1) * P],
                                 ak[part, h * S:h * S + k], start=True, stop=False)
                        last = T.matmul(bank[:, t * P:k], m.ident_bf[:], negmask[:], start=False, stop=True)
                    last.then_inc(scores, 1)
                if 1 <= n <= STEPS_A:
                    o = n - 1
                    pe.wait_ge(mixed_ready, o + 1)
                    if o >= 1:
                        pe.wait_ge(mixedT_ready, o)
                    for kb in range(o % TT + 1):
                        last = T.transpose(m.psum[4][:, kb * P:(kb + 1) * P], mixed[:, o % 2, kb * P:(kb + 1) * P],
                                           m.ident[:])
                    last.then_inc(mixed_tr, 1)
                if n >= 2:
                    o = n - 2
                    h, t = divmod(o, TT)
                    pe.wait_ge(mixedT_ready, o + 1)
                    if o >= 1:
                        pe.wait_ge(attn_read, o)
                    for kb in range(t + 1):
                        last = T.matmul(m.psum[5][:, 0:HD], mixedT[:, o % 2, kb * P:(kb + 1) * P],
                                        av[:, kb, h * HD:(h + 1) * HD], start=(kb == 0), stop=(kb == t))
                    last.then_inc(attn_out, 1)
                if n < ADA_CHUNKS // 2:
                    for c in range(16 // ADA + 2 * n, 16 // ADA + 2 * n + 2):
                        ada_pe(nc, pe, m, m.wada, m.ada_landed, m.ada_used, c, False)
                if n >= LEVEL_AT:
                    level_matmuls(n)
            pe.wait_ge(f_ready, 2 * len(LEVELS) + 2)
            for n in range(NCH - 1):
                if n >= 2:
                    pe.wait_ge(kbT_ready, n - 1)
                for h in range(HEADS):
                    last = T.transpose(m.psum[n % 2][:, h * HD:(h + 1) * HD],
                                       F[:, 3, h * S + n * CHUNK:h * S + (n + 1) * CHUNK], m.ident[:])
                last.then_inc(kb_tr, 1)
            for n in range(NCH - 1):
                pe.wait_ge(kbT_ready, n + 1)
                if n >= 2:
                    pe.wait_ge(state_ready, n - 1)
                for h in range(HEADS):
                    last = T.matmul(m.psum[2 + n % 2][:, h * HD:(h + 1) * HD], kbT[:, n, h * HD:(h + 1) * HD],
                                    hi[:, n, h * HD:(h + 1) * HD], start=True, stop=True)
                last.then_inc(kv_done, 1)
            pe.wait_ge(attn_read, STEPS_A)
            pe.wait_ge(level_copied, HEADS * len(LEVELS))
            for t in range(NCH):
                if t >= 1:
                    pe.wait_ge(state_ready, t)
                for h in range(HEADS):
                    at = slice(h * S + t * CHUNK, h * S + (t + 1) * CHUNK)
                    out = m.psum[4 + t][:, h * HD:(h + 1) * HD]
                    last = T.matmul(out, attnT[:, h, t * CHUNK:(t + 1) * CHUNK], hi[:, t, h * HD:(h + 1) * HD],
                                    start=True, stop=(t == 0))
                    if t >= 1:
                        last = T.matmul(out, F[:, 2, at], state[:, t - 1, h * HD:(h + 1) * HD], start=False, stop=True)
                last.then_inc(hgrn_out, 1)
    m.keep.close()



def stage_join(nc, a, m):
    h2T = m.actT
    with ExitStack() as own:
        m.actT = m.sb("catT", [P, 2, KC, S], F32R, own)
        catT = m.actT
        raw = m.sb("raw3", [P, RAW, UNIT], F32, own)
        hl = m.sb("hl3", [P, 2, SPLIT, UNIT], F32R, own)
        x = m.sb("x3", [P, TT, D], F32, own)
        piece = m.sb("piece3", [P, 2, S], F32, own)
        scratch = m.sb("scratch3", [P, D], F32, own)
        gcol = m.sb("gcol", [P, 2, KC], F32, own)
        diag = m.sb("diag", [P, 2 * KC, P], F32, own)
        y = m.rows[:].rearrange("p t d -> p (t d)").rearrange("p (g t n) -> p t g n", g=2, t=TT)
        sem = m.sem
        x_landed = sem("x_again_landed")
        diag_ready, row_ready = sem("diag_ready"), sem("row_ready")
        cat_tr, cat_free, cat_lo, cat_hi = sem("cat_tr"), sem("cat_free"), sem("cat_lo"), sem("cat_hi")
        stats = sem("stats3")
        x2_ready, x2_stored = sem("x2_ready"), sem("x2_stored")
        stats_b, xn_ready = sem("stats3b"), sem("xn_ready3")
        transposed, bank_free, hi_ready, piece_lo = sem("tr3"), sem("free3"), sem("hi3"), sem("lo3")
        n0, e0 = m.units, m.evacs
        block = own.enter_context(nc.Block())

        @block.sync
        def _(sp):
            sp.dma_start(x[:], a.x.rearrange("(t p) d -> p t d", p=P)).then_inc(x_landed, 16)
            units_load(nc, sp, m, a.w_out, raw, n0, 8)
            sp.wait_ge(x2_ready, TT)
            sp.dma_start(a.x2, x[:]).then_inc(x2_stored, 16)
            sp.wait_ge(x2_stored, 16)

        @block.scalar
        def _(act):
            split_act(nc, act, m, catT, 4, piece, cat_tr, cat_free, cat_lo, cat_hi, False, 0)
            units_hi(nc, act, m, raw, hl, n0, 8)
            act.wait_ge(m.unit_evac, e0 + 2 * TT)
            for t in range(TT):
                m.act.then(act, nc.scalar.activation(scratch[:].rearrange("p (g n) -> p g n", g=2), y[:, t],
                                                     ACT.Square, accum_out=m.ss[:, t:t + 1]))
            nc.scalar.activation(m.rstd[:], m.ss[:], ACT.Sqrt, bias=m.eps[:, 0:1], scale=1.0 / D).then_inc(stats, 1)
            norm_stats(nc, act, m, x, scratch[:], lambda e, t: e.wait_ge(x2_ready, t + 1), stats_b)
            split_act(nc, act, m, h2T, 4, piece, transposed, bank_free, piece_lo, hi_ready, True, 24)

        @block.vector
        def _(dve):
            V = nc.vector
            for w, (gate, gain) in enumerate(((16, 1), (40, 3))):
                m.dve.then(dve, V.tensor_tensor(gcol[:, w, :], m.mod[:, gate:gate + KC], m.gains[:, gain, :],
                                                ALU.mult))
            for c in range(2 * KC):
                V.tensor_scalar(diag[:, c, :], m.ident[:], gcol[:, c // KC, c % KC:c % KC + 1], None, ALU.mult
                                ).then_inc(diag_ready, 1)
            m.dve.then(dve, V.scalar_tensor_tensor(m.scale[:], m.mod[:, 32:40], 1.0, m.gains[:, 2, :],
                                                   ALU.add, ALU.mult))
            for c in range(4):
                dve.wait_ge(row_ready, c + 1)
                m.dve.then(dve, V.tensor_copy(m.rowg[:, c // 2, (c % 2) * S:(c % 2 + 1) * S], m.psum[c][:]))
            split_dve(nc, dve, catT, piece, cat_hi, cat_lo)
            row_units_dve(nc, dve, m, raw, hl, m.rows[:].rearrange("p t d -> p (t d)"), n0, e0, 2)
            dve.wait_ge(stats, 1)
            dve.wait_ge(x_landed, 16)
            m.dve.then(dve, V.reciprocal(m.rstd[:], m.rstd[:]))
            for t in range(TT):
                g = m.rowg[:, 0, :].rearrange("p (g n) -> p g n", g=2)
                xt = x[:, t, :].rearrange("p (g n) -> p g n", g=2)
                m.dve.then(dve, V.scalar_tensor_tensor(y[:, t], y[:, t], m.rstd[:, t:t + 1], g, ALU.mult, ALU.mult))
                V.tensor_tensor(xt, xt, y[:, t], ALU.add).then_inc(x2_ready, 1)
            norm_rows_dve(nc, dve, m, x, m.rows, stats_b, 1, xn_ready)
            split_dve(nc, dve, h2T, piece, hi_ready, piece_lo)

        @block.tensor
        def _(pe):
            for c in range(4):
                pe.wait_ge(diag_ready, 4 * c + 4)
                nc.tensor.matmul(m.psum[c][:], m.ones[:], diag[:, 4 * c:4 * c + 4, :].rearrange("p c n -> p (c n)"),
                                 start=True, stop=True).then_inc(row_ready, 1)
            transpose_pe(nc, pe, m, m.rows, 4, None, cat_free, cat_tr)
            pe.wait_ge(cat_lo, KC)
            row_units_pe(nc, pe, m, hl, n0, e0, 2)
            pe.wait_ge(m.unit_evac, e0 + 2 * TT)
            transpose_pe(nc, pe, m, m.rows, 4, xn_ready, bank_free, transposed)
    m.units += 8
    m.evacs += 8
    m.actT = h2T



ROWS = [(a, 1 + a, TOPK // (a + 1)) for a in range(5)] + [(5, 8, 2), (8, 16, 1)]
NCAND = sum((a1 - a0) * n for a0, a1, n in ROWS)
PRE = 5
ROUNDS = (HJ + PRE * JG) // RAW
assert ROUNDS == PH + 1
SPLIT4 = 4


def candidate_sums(eng, out, first, second):
    at = 0
    for a0, a1, n in ROWS:
        c = a1 - a0
        o = out[:, :, at:at + c * n].rearrange("p h (a b) -> p h a b", a=c)
        last = eng.tensor_tensor(o, first[:, :, a0:a1].unsqueeze(3).to_broadcast([P, TT, c, n]),
                                 second[:, :, 0:n].unsqueeze(2).to_broadcast([P, TT, c, n]), ALU.add)
        at += c * n
    return last


def stage_select(nc, a, m):
    with ExitStack() as own:
        def sb(name, shape, dt=F32):
            return m.sb(name, shape, dt, own)

        qT = sb("qT", [P, RAW, S])
        keys = sb("keys", [P, HJ * NKEY])
        raw = sb("raw4", [P, RAW, UNIT])
        hl = sb("hl4", [P, 2, SPLIT4, UNIT], F32R)
        scores = sb("key_scores", [P, HJ, TT * NKEY])
        early = sb("early_acts", [P, 2, S])
        rest = sb("rest", [P, 2 * TT, NKEY])
        v = sb("v", [P, 2 * TT, TOPK])
        vi = sb("vi", [P, 2 * TT, TOPK], U32)
        vf = sb("vf", [P, 2, 2, TT, TOPK])
        cand = sb("cand", [P, TT, NCAND])
        cand2 = sb("cand2", [P, TT, NCAND])
        code = sb("code", [P, 2, TT, NCAND])
        top = sb("top", [P, TT, PH, TOPK])
        best = sb("best", [P, TT, TOPK])
        pos = sb("pos", [P, TT, TOPK], U32)
        posf = sb("posf", [P, TT, TOPK])
        hit = sb("hit", [P, 2, TT * TOPK, NCAND])
        chosen = sb("chosen", [P, TT, PH, TOPK])
        places = sb("places", [P, NCAND])
        room = m.rows[:].rearrange("p t d -> p (t d)")
        n = 3 * TT * PH * TOPK
        slots = room[:, 0:n].rearrange("p (t w n) -> p t w n", t=TT, w=3)
        slots_u = room[:, n:2 * n].bitcast(U32).rearrange("p (w t n) -> p w t n", t=TT, w=3)
        total = sb("total", [P, TT, PH])
        sem = m.sem
        keys_landed = sem("keys_landed")
        scored, scores_read = sem("scored"), sem("scores_read")
        early_stored = [sem("early_stored0"), sem("early_stored1")]
        iota_ready = sem("iota_ready")
        vf_ready, code_ready = sem("vf_ready"), sem("code_ready")
        hit_ready, hit_coded, hit_summed = sem("hit_ready"), sem("hit_coded"), sem("hit_summed")
        shifted, exps = sem("shifted"), sem("exps")
        slots_ready, slots_tr, slots_read = sem("slots_ready"), sem("slots_tr"), sem("slots_read")
        n0, e0 = m.units, m.evacs
        early_units = PRE * JG
        block = own.enter_context(nc.Block())

        @block.sync
        def _(sp):
            sp.dma_start(keys[:], a.keys).then_inc(keys_landed, 16)
            units_load(nc, sp, m, a.w_pq, raw, n0, HJ)

            def body(i, first):
                for u in range(RAW):
                    sp.wait_ge(m.unit_lo, i + (n0 + HJ - RAW + 1 + u))
                    sp.dma_start(raw[:, u, :], a.u[bass.ds(i + u, 1), :, :].rearrange("a p f -> p (a f)")
                                 ).then_inc(m.unit_landed[u], 16)
                    if not (first and u < 2):
                        sp.wait_ge(m.unit_evac, i + (e0 + HJ + u - 1))
                        sp.dma_start(a.early[bass.ds(i + (u - 2), 1), :, :].rearrange("a p f -> p (a f)"),
                                     early[:, u % 2, :]).then_inc(early_stored[u % 2], 16)
            body(0, True)
            with sp.Fori(1, PRE) as k:
                body(k * RAW, False)
            for u in range(2):
                sp.wait_ge(m.unit_evac, e0 + HJ + early_units - 1 + u)
                sp.dma_start(a.early[early_units - 2 + u], early[:, u, :]).then_inc(early_stored[u], 16)
            for u in range(2):
                sp.wait_ge(early_stored[u], 16 * early_units // 2)

        @block.gpsimd
        def _(pool):
            g = nc.gpsimd
            g.iota(places[:], [[1, NCAND]], base=0, channel_multiplier=0,
                   allow_small_or_imprecise_dtypes=True).then_inc(iota_ready, 1)

            def codes(k, b):
                pool.wait_ge(vf_ready, k)
                candidate_sums(g, code[:, b], vf[:, b, 0], vf[:, b, 1]).then_inc(code_ready, 1)
                pool.wait_ge(code_ready, k)
                pool.wait_ge(hit_ready, k)

            def coded(b, half):
                hv = hit[:, b].rearrange("p (t k) c -> p t k c", t=TT)[:, 2 * half:2 * half + 2]
                c = code[:, b, 2 * half:2 * half + 2].unsqueeze(2).to_broadcast([P, 2, TOPK, NCAND])
                g.tensor_tensor(hv, hv, c, ALU.mult).then_inc(hit_coded, 1)

            def low(k, u):
                pool.wait_ge(m.unit_hi, k * RAW + (n0 + u + 1))
                g.tensor_tensor(hl[:, 1, u % SPLIT4, :], raw[:, u, :], hl[:, 0, u % SPLIT4, :].bitcast(F32),
                                ALU.subtract).then_inc(m.unit_lo, 1)
            for u in range(RAW):
                low(0, u)
            with pool.Fori(0, (ROUNDS - 1) // 2) as r:
                for b in range(2):
                    k = r * 2 + (b + 1)
                    for u in range(RAW):
                        if u == 3:
                            codes(k, b)
                            coded(b, 0)
                        low(k, u)
                    coded(b, 1)

        @block.scalar
        def _(act):
            def hi(i, k, u):
                act.wait_ge(m.unit_landed[u], k * 16 + (n0 // RAW + 1) * 16)
                act.wait_ge(m.unit_used, i + (n0 - SPLIT4 + 1 + u))
                nc.scalar.activation(hl[:, 0, u % SPLIT4, :], raw[:, u, :], ACT.Copy).then_inc(m.unit_hi, 1)

            def read_queries(i, u):
                act.wait_ge(m.unit_used, i + (n0 + u + 1))
                nc.scalar.activation(qT[:, u % RAW, :], m.psum[u % 2][:], ACT.Copy).then_inc(m.unit_evac, 1)

            def read_scores(i, u):
                act.wait_ge(scored, i + (u + 1))
                nc.scalar.activation(scores[:, bass.ds(i + u, 1), :].rearrange("p a n -> p (a n)"),
                                     m.psum[2 + u % RAW][:], ACT.Copy).then_inc(scores_read, 1)

            def queries_round(i, k, first):
                for u in range(RAW):
                    hi(i, k, u)
                    if not (first and u < 1):
                        read_queries(i, u - 1)
                    if not (first and u < 2):
                        read_scores(i, u - 2)
            queries_round(0, 0, True)
            with act.Fori(1, HJ // RAW) as k:
                queries_round(k * RAW, k, False)

            def early_round(i, k, first):
                for u in range(RAW):
                    hi(i + HJ, k + HJ // RAW, u)
                    if first and u < 1:
                        read_queries(HJ, -1)
                    elif not first or u >= 1:
                        act.wait_ge(m.unit_used, i + (n0 + HJ + u))
                        if not (first and u < 3):
                            act.wait_ge(early_stored[(u - 1) % 2], k * 32 + 16 * ((u - 1) // 2))
                        nc.scalar.activation(early[:, (u - 1) % 2, :], m.psum[(u - 1) % 2][:], ACT.Gelu
                                             ).then_inc(m.unit_evac, 1)
                    if first and u < 2:
                        read_scores(HJ, u - 2)
            early_round(0, 0, True)
            with act.Fori(1, PRE - 1) as k:
                early_round(k * RAW, k, False)
            act.wait_ge(shifted, 1)
            nc.scalar.activation(top[:], top[:], ACT.Exp).then_inc(exps, 1)
            early_round((PRE - 1) * RAW, PRE - 1, False)
            act.wait_ge(m.unit_used, n0 + HJ + early_units)
            act.wait_ge(early_stored[1], 16 * (early_units // 2 - 1))
            nc.scalar.activation(early[:, 1, :], m.psum[1][:], ACT.Gelu).then_inc(m.unit_evac, 1)
            for t in range(TT):
                act.wait_ge(slots_tr, t + 1)
                nc.scalar.activation(m.slotsT[:, :, t * P:(t + 1) * P],
                                     m.psum[4 + t][:, 0:3 * P].rearrange("p (w n) -> p w n", w=3), ACT.Copy
                                     ).then_inc(slots_read, 1)
            act.wait_ge(slots_read, TT)

        @block.vector
        def _(dve):
            V = nc.vector
            st = m.dve

            def top16(values, count, replaced, largest, where):
                for r in range(count):
                    last = V.max(largest[:, r, 0:8], values[:, r, :])
                st.then(dve, last)
                for r in range(count):
                    last = V.match_replace(replaced[:, r, :], largest[:, r, 0:8], values[:, r, :], LOWEST)
                st.then(dve, last)
                for r in range(count):
                    V.max_index(where[:, r, 0:8], largest[:, r, 0:8], values[:, r, :])
                for r in range(count):
                    last = V.max(largest[:, r, 8:16], replaced[:, r, :])
                st.then(dve, last)
                for r in range(count):
                    last = V.max_index(where[:, r, 8:16], largest[:, r, 8:16], replaced[:, r, :])
                st.then(dve, last)

            def codes(h):
                dve.wait_ge(hit_coded, 2 * h + 2)
                V.tensor_reduce(chosen[:, :, h, :], hit[:, h % 2].rearrange("p (t k) c -> p t k c", t=TT), AX_X, ALU.add
                                ).then_inc(hit_summed, 1)

            dve.wait_ge(iota_ready, 1)
            for h in range(PH):
                dve.wait_ge(scores_read, 2 * h + 2)
                pair = scores[:, 2 * h:2 * h + 2, :].rearrange("p j (t n) -> p (j t) n", t=TT)
                top16(pair, 2 * TT, rest, v, vi)
                if h >= 2:
                    dve.wait_ge(hit_coded, 2 * h - 2)
                V.tensor_scalar(vf[:, h % 2, 0], vi[:, 0:TT], float(NKEY), None, ALU.mult)
                V.tensor_copy(vf[:, h % 2, 1], vi[:, TT:]).then_inc(vf_ready, 1)
                st.then(dve, candidate_sums(V, cand, v[:, 0:TT], v[:, TT:]))
                top16(cand, TT, cand2, best, pos)
                V.tensor_copy(top[:, :, h, :], best[:])
                st.then(dve, V.tensor_copy(posf[:], pos[:]))
                if h >= 2:
                    codes(h - 2)
                    dve.wait_ge(hit_summed, h - 1)
                V.tensor_tensor(hit[:, h % 2], posf[:].rearrange("p t k -> p (t k)").unsqueeze(2)
                                .to_broadcast([P, TT * TOPK, NCAND]),
                                places[:].unsqueeze(1).to_broadcast([P, TT * TOPK, NCAND]), ALU.is_equal
                                ).then_inc(hit_ready, 1)
            tops = top[:].rearrange("p t h k -> p (t h) k")
            st.then(dve, V.tensor_copy(total[:], top[:, :, :, 0]))
            V.tensor_tensor(tops, tops, total[:].rearrange("p t h -> p (t h)").unsqueeze(2)
                            .to_broadcast([P, TT * PH, TOPK]), ALU.subtract).then_inc(shifted, 1)
            dve.wait_ge(exps, 1)
            st.then(dve, V.tensor_reduce(total[:].rearrange("p t h -> p (t h)"), tops, AX_X, ALU.add))
            st.then(dve, V.reciprocal(total[:], total[:]))
            for t in range(TT):
                V.tensor_tensor(slots[:, t, 2, :].rearrange("p (h k) -> p h k", h=PH), top[:, t],
                                total[:, t].unsqueeze(2).to_broadcast([P, PH, TOPK]), ALU.mult)
            codes(PH - 2)
            codes(PH - 1)
            dve.wait_ge(hit_summed, PH)
            st.then(dve, V.tensor_copy(slots_u[:, 2], chosen[:].rearrange("p t h k -> p t (h k)")))
            V.tensor_scalar(slots_u[:, 0], slots_u[:, 2], 7, None, ALU.logical_shift_right)
            st.then(dve, V.tensor_scalar(slots_u[:, 1], slots_u[:, 2], NKEY - 1, None, ALU.bitwise_and))
            for t in range(TT):
                V.tensor_copy(slots[:, t, 0:2, :], slots_u[:, 0:2, t, :]).then_inc(slots_ready, 1)

        @block.tensor
        def _(pe):
            def unit(i, u, first):
                pe.wait_ge(m.unit_lo, i + (n0 + 1 + u))
                if not (first and u < 2):
                    pe.wait_ge(m.unit_evac, i + (e0 - 1 + u))
                bank = m.psum[u % 2]
                for kc in range(KC):
                    for j, (x, z) in enumerate(PASSES):
                        last = nc.tensor.matmul(bank[:], hl[:, x, u % SPLIT4, kc * P:(kc + 1) * P],
                                                m.actT[:, z, kc, :], start=(kc == 0 and j == 0),
                                                stop=(kc == KC - 1 and j == 2))
                last.then_inc(m.unit_used, 1)

            def score(i, u, first):
                pe.wait_ge(m.unit_evac, i + (e0 + 1 + u))
                if not first:
                    pe.wait_ge(scores_read, i + (u + 1 - RAW))
                for t in range(TT):
                    last = nc.tensor.matmul(m.psum[2 + u % RAW][:, t * P:(t + 1) * P],
                                            qT[:, u % RAW, t * P:(t + 1) * P],
                                            keys[:, bass.ds((i + u) * NKEY, NKEY)], start=True, stop=True)
                last.then_inc(scored, 1)

            def queries_round(i, first):
                for u in range(RAW):
                    unit(i, u, first)
                    if not (first and u < 1):
                        score(i, u - 1, first)
            pe.wait_ge(keys_landed, 16)
            queries_round(0, True)
            with pe.Fori(1, HJ // RAW) as k:
                queries_round(k * RAW, False)
            unit(HJ, 0, False)
            score(HJ, -1, False)
            for u in range(1, RAW):
                unit(HJ, u, False)
            with pe.Fori(HJ // RAW + 1, ROUNDS) as k:
                for u in range(RAW):
                    unit(k * RAW, u, False)
            for t in range(TT):
                pe.wait_ge(slots_ready, t + 1)
                for w in range(3):
                    last = nc.tensor.transpose(m.psum[4 + t][:, w * P:(w + 1) * P], slots[:, t, w, :], m.ident[:])
                last.then_inc(slots_tr, 1)
    m.units += HJ + early_units
    m.evacs += HJ + early_units



ROUND = 8
ACT_ROWS = 2
PER = 4
CHUNKS = ROUND // PER
BUFS = 4
DROW = NKEY * S + 1024


def stage_gates(nc, a, m):
    with ExitStack() as own:
        def sb(name, shape, dt=F32):
            return m.sb(name, shape, dt, own)

        slotsT = m.slotsT
        iota = sb("iota", [P, NKEY])
        iota_bf = sb("iota_bf", [P, NKEY, ROUND], BF16)
        first_bf = sb("first_bf", [P, S], BF16)
        hits = sb("first_hits", [P, BUFS, NKEY, ROUND], BF16)
        gate = sb("gate_now", [P, BUFS, ROUND])
        onehot1 = sb("onehot1", [P, BUFS, ROUND, NKEY])
        onehot2 = sb("onehot2", [P, BUFS, ROUND, NKEY])
        gates = sb("gates", [P, 2, NKEY, TB])
        sem = m.sem
        iota_ready = sem("iota_ready5")
        hits_ready, second_ready = sem("hits_ready"), sem("second_ready")
        pool_rows, act_rows = sem("pool_rows"), sem("act_rows")
        gated, gates_read = sem("gated"), sem("gates_read")
        stored = [sem("stored0"), sem("stored1")]
        pairs = S // (2 * TB)
        rounds = 2 * TB // ROUND
        pool_n = ROUND - ACT_ROWS
        block = own.enter_context(nc.Block())

        @block.gpsimd
        def _(pool):
            nc.gpsimd.iota(iota[:], [[1, NKEY]], base=0, channel_multiplier=0,
                           allow_small_or_imprecise_dtypes=True).then_inc(iota_ready, 1)
            nc.gpsimd.iota(iota_bf[:], [[1, NKEY], [0, ROUND]], base=0, channel_multiplier=0,
                           allow_small_or_imprecise_dtypes=True).then_inc(iota_ready, 1)

            def body(i, first):
                for b in range(rounds):
                    pool.wait_ge(hits_ready, i * rounds + (b + 1))
                    if not (first and b < BUFS):
                        pool.wait_ge(gated, i * (rounds * CHUNKS) + (b + 1 - BUFS) * CHUNKS)
                    n = bass.ds(i * (rounds * ROUND) + b * ROUND, pool_n)
                    nc.gpsimd.tensor_tensor(
                        onehot1[:, b % BUFS, 0:pool_n, :].rearrange("p t k -> p k t"), hits[:, b % BUFS, :, 0:pool_n],
                        slotsT[:, 2, n].unsqueeze(1).to_broadcast([P, NKEY, pool_n]), ALU.mult
                        ).then_inc(pool_rows, 1)
            body(0, True)
            with pool.Fori(1, pairs) as i:
                body(i, False)

        @block.scalar
        def _(act):
            def scale_rows(i, b, first):
                act.wait_ge(hits_ready, i * rounds + (b + 1))
                if not (first and b < BUFS):
                    act.wait_ge(gated, i * (rounds * CHUNKS) + (b + 1 - BUFS) * CHUNKS)
                for u in range(pool_n, ROUND):
                    last = nc.scalar.activation(onehot1[:, b % BUFS, u, :], hits[:, b % BUFS, :, u], ACT.Copy,
                                                scale=gate[:, b % BUFS, u:u + 1])
                last.then_inc(act_rows, 1)

            def read_gates(i, b, first):
                k = b * ROUND // TB % 2
                if not first and b * ROUND % TB == 0:
                    act.wait_ge(stored[k], i * 16)
                for c in range(CHUNKS):
                    act.wait_ge(gated, i * (rounds * CHUNKS) + (b * CHUNKS + c + 1))
                    at = (b * ROUND + c * PER) % TB
                    nc.scalar.activation(gates[:, k, :, at:at + PER],
                                         m.psum[CHUNKS * (b % BUFS) + c][:].rearrange("p (t j) -> p j t", t=PER), ACT.Copy
                                         ).then_inc(gates_read, 1)

            def body(i, first):
                for b in range(rounds):
                    scale_rows(i, b, first)
                    if b >= 1:
                        read_gates(i, b - 1, first)
                    elif not first:
                        read_gates(i - 1, rounds - 1, False)
            body(0, True)
            with act.Fori(1, pairs) as i:
                body(i, False)
            read_gates(pairs - 1, rounds - 1, False)

        @block.sync
        def _(sp):
            for j in range(JG):
                sp.dma_start(m.v_raw[:, j, :], a.v[j]).then_inc(m.early_landed[j], 16)
                sp.dma_start(m.early_in[:, j, :], a.early[j]).then_inc(m.early_landed[j], 16)
            sp.dma_start(m.u_raw[:], a.u[PRE * JG:(PRE + 1) * JG].rearrange("j p d -> p j d")
                         ).then_inc(m.u_landed, 16)
            with sp.Fori(0, pairs) as p:
                for k in range(2):
                    sp.wait_ge(gates_read, p * (2 * TB // PER) + ((k + 1) * (TB // PER)))
                    dst = a.gates[:, 0:NKEY * S].rearrange("p (g n) -> p g n", n=NTB * JG * TB)
                    sp.dma_start(dst[:, 0:GROUPS, bass.ds(p * (2 * JG * TB) + k * JG * TB, JG * TB)],
                                 gates[:, k, :, :].rearrange("p (g j) t -> p g (j t)", j=JG)).then_inc(stored[k], 16)
            for k in range(2):
                sp.wait_ge(stored[k], 16 * pairs)

        @block.vector
        def _(dve):
            V = nc.vector
            m.dve.then(dve, V.tensor_copy(first_bf[:], slotsT[:, 0, :]))
            dve.wait_ge(iota_ready, 2)

            def body(i, first):
                for b in range(rounds):
                    if not (first and b < BUFS):
                        dve.wait_ge(gated, i * (rounds * CHUNKS) + (b + 1 - BUFS) * CHUNKS)
                    n = bass.ds(i * (rounds * ROUND) + b * ROUND, ROUND)
                    V.tensor_copy(gate[:, b % BUFS, :], slotsT[:, 2, n])
                    V.tensor_tensor(hits[:, b % BUFS], iota_bf[:],
                                    first_bf[:, n].unsqueeze(1).to_broadcast([P, NKEY, ROUND]), ALU.is_equal
                                    ).then_inc(hits_ready, 1)
                    V.tensor_tensor(onehot2[:, b % BUFS], iota[:].unsqueeze(1).to_broadcast([P, ROUND, NKEY]),
                                    slotsT[:, 1, n].unsqueeze(2).to_broadcast([P, ROUND, NKEY]), ALU.is_equal
                                    ).then_inc(second_ready, 1)
            body(0, True)
            with dve.Fori(1, pairs) as i:
                body(i, False)

        @block.tensor
        def _(pe):
            def body(i, first):
                for b in range(rounds):
                    pe.wait_ge(pool_rows, i * rounds + (b + 1))
                    pe.wait_ge(second_ready, i * rounds + (b + 1))
                    for c in range(CHUNKS):
                        if not (first and b < BUFS):
                            pe.wait_ge(gates_read, i * (rounds * CHUNKS) + ((b - BUFS) * CHUNKS + c + 1))
                        if c == pool_n // PER:
                            pe.wait_ge(act_rows, i * rounds + (b + 1))
                        for k in range(PER):
                            u = c * PER + k
                            last = nc.tensor.matmul(m.psum[CHUNKS * (b % BUFS) + c][:, k * NKEY:(k + 1) * NKEY],
                                                    onehot1[:, b % BUFS, u, :], onehot2[:, b % BUFS, u, :],
                                                    start=True, stop=True)
                        last.then_inc(gated, 1)
            body(0, True)
            with pe.Fori(1, pairs) as i:
                body(i, False)



def stage_experts(nc, a, m):
    with ExitStack() as own:
        def sb(name, shape, dt=F32):
            return m.sb(name, shape, dt, own)

        u_raw, v_raw, early = m.u_raw, m.v_raw, m.early_in
        u = sb("u", [P, 2, JG, D], F32R)
        v = sb("v_parts", [P, 2, JG, D], F32R)
        w = sb("w", [P, 2, JG, S], F32R)
        gates = sb("group_gates", [P, NTB, JG, TB])
        act_out = sb("act_out", [P, 2, S])
        weighed = sb("weighed", [P, 2, S])
        y = m.rows
        sem = m.sem
        u_landed, early_landed = m.u_landed, m.early_landed
        v_landed, gates_landed = sem("v_landed"), sem("gates_landed")
        u_hi, u_lo, v_hi, v_lo = sem("u_hi"), sem("u_lo"), sem("v_hi"), sem("v_lo")
        a_done, gelus, weighed_done, w_ready = sem("a_done"), sem("gelus"), sem("weighed_done"), sem("w_ready")
        y_done, y_added = sem("y_done"), sem("y_added")
        weigh_step = sem("weigh_step")
        early_used = sem("early_used")
        squares, stats, out_ready = sem("squares5"), sem("stats5"), sem("out_ready")
        x2_landed, out_stored = sem("x2_landed"), sem("out_stored")
        pieces = 2 * TT
        block = own.enter_context(nc.Block())

        @block.sync
        def _(sp):
            def load_u(g):
                sp.dma_start(u_raw[:], a.u[bass.ds(g * JG, JG), :, :].rearrange("j p d -> p j d")).then_inc(u_landed, 16)

            def load_v(g):
                sp.dma_start(v_raw[:], a.v[bass.ds(g * JG, JG), :, :].rearrange("j p d -> p j d")).then_inc(v_landed, 16)

            def load_gates(g):
                n = NTB * JG * TB
                sp.dma_start(gates[:].rearrange("p b j t -> p (b j t)"), a.gates[:, bass.ds(g * n, n)]
                             ).then_inc(gates_landed, 16)

            load_gates(0)
            with sp.Fori(1, PRE) as g:
                for j in range(JG):
                    sp.wait_ge(v_lo, g * JG + (j + 1 - JG))
                    sp.dma_start(v_raw[:, j, :], a.v[bass.ds(g * JG + j, 1), :, :].rearrange("a p d -> p (a d)")
                                 ).then_inc(early_landed[j], 16)
                    sp.wait_ge(weighed_done, g * JG + (j + 1 - JG))
                    sp.dma_start(early[:, j, :], a.early[bass.ds(g * JG + j, 1), :, :].rearrange("a p s -> p (a s)")
                                 ).then_inc(early_landed[j], 16)
                load_gates(g)
            sp.wait_ge(v_lo, PRE * JG)
            load_v(PRE)
            sp.wait_ge(weighed_done, PRE * JG)
            load_gates(PRE)
            sp.wait_ge(u_lo, JG)
            load_u(PRE + 1)
            with sp.Fori(PRE, GROUPS - 2) as g:
                sp.wait_ge(v_lo, g * JG + JG)
                load_v(g + 1)
                sp.wait_ge(weighed_done, g * JG + JG)
                load_gates(g + 1)
                sp.wait_ge(u_lo, g * JG + (2 - PRE) * JG)
                load_u(g + 2)
            sp.wait_ge(v_lo, (GROUPS - 1) * JG)
            load_v(GROUPS - 1)
            sp.wait_ge(weighed_done, (GROUPS - 1) * JG)
            load_gates(GROUPS - 1)
            sp.wait_ge(u_lo, (GROUPS - PRE) * JG)
            sp.dma_start(u_raw[:], a.x2).then_inc(x2_landed, 16)
            for t in range(TT):
                sp.wait_ge(out_ready, t + 1)
                sp.dma_start(a.out[t * P:(t + 1) * P, :], u_raw[:, t, :]).then_inc(out_stored, 16)
            sp.wait_ge(out_stored, 16 * TT)

        @block.scalar
        def _(act):
            def hi_of_u(g):
                act.wait_ge(u_landed, (g - PRE) * 16 + 16)
                for j in range(JG):
                    nc.scalar.activation(u[:, 0, j, :], u_raw[:, j, :], ACT.Copy).then_inc(u_hi, 1)

            def activations(g):
                act.wait_ge(v_landed, (g - PRE) * 16 + 16)
                act.wait_ge(y_added, (g - PRE) * pieces + pieces)
                for j in range(JG):
                    nc.scalar.activation(v[:, 0, j, :], v_raw[:, j, :], ACT.Copy).then_inc(v_hi, 1)
                    act.wait_ge(a_done, (g - PRE) * JG + (j + 1))
                    if j >= 2:
                        act.wait_ge(weighed_done, g * JG + (j - 1))
                    nc.scalar.activation(act_out[:, j % 2, :], m.psum[j % 2][:], ACT.Gelu).then_inc(gelus, 1)

            def hi_of_v(g, first):
                for j in range(JG):
                    act.wait_ge(early_landed[j], g * 32 + 32)
                    if not first:
                        act.wait_ge(early_used, g * JG + (j + 1 - JG))
                    nc.scalar.activation(v[:, 0, j, :], v_raw[:, j, :], ACT.Copy).then_inc(v_hi, 1)
            hi_of_v(0, True)
            with act.Fori(1, PRE) as g:
                hi_of_v(g, False)
            hi_of_u(PRE)
            for p in range(0, pieces, 2):
                t, half = p % TT, p // TT
                act.wait_ge(early_used, PRE * JG)
                nc.scalar.activation(y[:, t, half * S:(half + 1) * S], m.psum[p][:], ACT.Copy).then_inc(y_added, 1)
            with act.Fori(PRE, GROUPS - 1) as g:
                activations(g)
                hi_of_u(g + 1)
            activations(GROUPS - 1)
            act.wait_ge(y_added, (GROUPS - PRE + 1) * pieces)
            for t in range(TT):
                m.act.then(act, nc.scalar.activation(v_raw[:, t, :], y[:, t, :], ACT.Square,
                                                     accum_out=m.ss[:, t:t + 1]))
            nc.scalar.activation(m.rstd[:], m.ss[:], ACT.Sqrt, bias=m.eps[:, 0:1], scale=1.0 / D).then_inc(stats, 1)

        @block.vector
        def _(dve):
            V = nc.vector

            def lo_of_u(g):
                for j in range(JG):
                    dve.wait_ge(u_hi, (g - PRE) * JG + (j + 1))
                    V.tensor_tensor(u[:, 1, j, :], u_raw[:, j, :], u[:, 0, j, :].bitcast(F32), ALU.subtract
                                    ).then_inc(u_lo, 1)

            def weigh(g, acts, slots, ready):
                dve.wait_ge(gates_landed, g * 16 + 16)
                for j in range(JG):
                    dve.wait_ge(v_hi, g * JG + (j + 1))
                    V.tensor_tensor(v[:, 1, j, :], v_raw[:, j, :], v[:, 0, j, :].bitcast(F32), ALU.subtract
                                    ).then_inc(v_lo, 1)
                    ready(j)
                    V.tensor_tensor(weighed[:, j % 2, :].rearrange("p (b t) -> p b t", t=TB),
                                    acts[:, j % slots, :].rearrange("p (b t) -> p b t", t=TB), gates[:, :, j, :],
                                    ALU.mult).then_inc(weighed_done, 1)
                    dve.wait_ge(weighed_done, g * JG + (j + 1))
                    V.tensor_copy(w[:, 0, j, :], weighed[:, j % 2, :]).then_inc(weigh_step, 1)
                    dve.wait_ge(weigh_step, g * JG + (j + 1))
                    V.tensor_tensor(w[:, 1, j, :], weighed[:, j % 2, :], w[:, 0, j, :].bitcast(F32), ALU.subtract
                                    ).then_inc(w_ready, 1)

            def weigh_early(g):
                weigh(g, early, JG, lambda j: dve.wait_ge(early_landed[j], g * 32 + 32))

            def weigh_late(g):
                weigh(g, act_out, 2, lambda j: dve.wait_ge(gelus, (g - PRE) * JG + (j + 1)))

            def add(g):
                for p in range(pieces):
                    t, half = p % TT, p // TT
                    dve.wait_ge(y_done, (g - PRE) * pieces + (p + 1))
                    part = y[:, t, half * S:(half + 1) * S]
                    V.tensor_tensor(part, part, m.psum[2 + p % 6][:], ALU.add).then_inc(y_added, 1)
            with dve.Fori(0, PRE) as g:
                weigh_early(g)
            lo_of_u(PRE)
            for p in range(1, pieces, 2):
                t, half = p % TT, p // TT
                dve.wait_ge(early_used, PRE * JG)
                V.tensor_copy(y[:, t, half * S:(half + 1) * S], m.psum[p][:]).then_inc(y_added, 1)
            dve.wait_ge(y_added, pieces)
            with dve.Fori(PRE, GROUPS - 1) as g:
                weigh_late(g)
                lo_of_u(g + 1)
                add(g)
            weigh_late(GROUPS - 1)
            add(GROUPS - 1)
            dve.wait_ge(stats, 1)
            m.dve.then(dve, V.reciprocal(m.rstd[:], m.rstd[:]))
            dve.wait_ge(x2_landed, 16)
            for t in range(TT):
                m.dve.then(dve, V.scalar_tensor_tensor(y[:, t, :], y[:, t, :], m.rstd[:, t:t + 1], m.rowg[:, 1, :],
                                                       ALU.mult, ALU.mult))
                V.tensor_tensor(u_raw[:, t, :], u_raw[:, t, :], y[:, t, :], ALU.add).then_inc(out_ready, 1)

        @block.tensor
        def _(pe):
            def early_units(g, first, final):
                for j in range(JG):
                    pe.wait_ge(v_lo, g * JG + (j + 1))
                    pe.wait_ge(w_ready, g * JG + (j + 1))
                    for p in range(pieces):
                        t, half = p % TT, p // TT
                        for i, (x, z) in enumerate(PASSES):
                            last = nc.tensor.matmul(m.psum[p][:], w[:, x, j, t * P:(t + 1) * P],
                                                    v[:, z, j, half * S:(half + 1) * S],
                                                    start=(first and j == 0 and i == 0),
                                                    stop=(final and j == JG - 1 and i == 2))
                    last.then_inc(early_used, 1)
            early_units(0, True, False)
            with pe.Fori(1, PRE - 1) as g:
                early_units(g, False, False)
            early_units(PRE - 1, False, True)
            pe.wait_ge(y_added, pieces)
            with pe.Fori(PRE, GROUPS) as g:
                for j in range(JG):
                    pe.wait_ge(u_lo, (g - PRE) * JG + (j + 1))
                    if j >= 2:
                        pe.wait_ge(gelus, (g - PRE) * JG + (j - 1))
                    for kc in range(KC):
                        for i, (p, q) in enumerate(PASSES):
                            last = nc.tensor.matmul(m.psum[j % 2][:], u[:, p, j, kc * P:(kc + 1) * P],
                                                    m.actT[:, q, kc, :], start=(kc == 0 and i == 0),
                                                    stop=(kc == KC - 1 and i == 2))
                    last.then_inc(a_done, 1)

                def piece(p, j):
                    t, half = p % TT, p // TT
                    for i, (x, z) in enumerate(PASSES):
                        last = nc.tensor.matmul(m.psum[2 + p % 6][:], w[:, x, j, t * P:(t + 1) * P],
                                                v[:, z, j, half * S:(half + 1) * S], start=(j == 0 and i == 0),
                                                stop=(j == JG - 1 and i == 2))
                    if j == JG - 1:
                        last.then_inc(y_done, 1)
                pe.wait_ge(y_added, (g - PRE) * pieces + pieces)
                for j in range(JG):
                    pe.wait_ge(v_lo, g * JG + (j + 1))
                    pe.wait_ge(w_ready, g * JG + (j + 1))
                    for p in range(TT):
                        piece(p, j)
                for p in range(TT, pieces):
                    if p >= 6:
                        pe.wait_ge(y_added, (g - PRE) * pieces + (pieces + p - 5))
                    for j in range(JG):
                        piece(p, j)



def kernel(**inputs):
    import numpy as np
    import concourse.bacc as bacc
    from concourse.bass_utils import run_bass_kernel_spmd

    def get(name):
        return np.asarray(inputs[name])

    def columns(w):
        n = w.shape[1] // P
        return w.reshape(KC, P, n, P).transpose(2, 1, 0, 3).reshape(n, P, KC * P)

    def rows(w):
        n = w.shape[1] // S
        return w.reshape(KC // 2, 2, P, n, S).transpose(3, 0, 2, 1, 4).reshape(n * KC // 2, P, 2 * S)

    def by_partition(vec):
        return vec.reshape(-1, P).T

    w_in, w_ada = get("w_in")[0], get("w_ada")[0]
    parts = [w_in[:, i * S:(i + 1) * S] for i in range(7)]
    theta = get("lb_theta")
    arrays = {
        "x": get("x")[0],
        "c": by_partition(get("c")[0]),
        "w_ada": w_ada.reshape(KC, P, 48 // ADA, ADA, P).transpose(2, 1, 3, 0, 4),
        "b_ada": by_partition(get("b_ada")[0]),
        "gains": np.stack([by_partition(get(n)[0]) for n in ("g_pre_mix", "g_post_mix", "g_pre_ffn", "g_post_ffn")],
                          axis=1),
        "w_cols": np.concatenate([columns(parts[i]) for i in (0, 1, 3, 4)]),
        "w_rows": np.concatenate([rows(parts[i]) for i in (2, 5, 6)]),
        "small": np.concatenate([np.tile(get("lam_qk")[0].reshape(1, -1), (P, 1)), by_partition(theta[0]),
                                 by_partition(theta[1]), np.tile(get("g_diff_sub"), (P, 1)),
                                 np.tile(get("g_hgrn_out"), (P, 1))], axis=1),
        "w_out": rows(get("w_out")[0]),
        "w_pq": columns(get("w_pq")[0]),
        "keys": get("sub_keys")[0].transpose(3, 0, 1, 2).reshape(P, HJ * NKEY),
        "u": get("expert_u")[0].reshape(NKEY, NKEY, KC, P).transpose(1, 3, 2, 0).reshape(NKEY, P, D),
        "v": get("expert_v")[0].reshape(NKEY, NKEY, D).transpose(1, 0, 2),
    }
    nc = bacc.Bacc("TRN2", target_bir_lowering=False, num_devices=1)
    a = Memory()
    for name, value in arrays.items():
        arrays[name] = value = np.ascontiguousarray(value)
        a.__dict__[name] = nc.dram_tensor(f"in_{name}", value.shape, F32, kind="ExternalInput").ap()
    a.x2 = nc.dram_tensor("x2", (P, TT, D), F32).ap()
    a.early = nc.dram_tensor("early_activations", (PRE * JG, P, S), F32).ap()
    a.gates = nc.dram_tensor("expert_gates", (P, DROW), F32).ap()
    a.out = nc.dram_tensor("out", (S, D), F32, kind="ExternalOutput").ap()
    build(nc, a)
    r = run_bass_kernel_spmd(nc, [{f"in_{k}": v for k, v in arrays.items()}], core_ids=[0])
    return r.results[0]["out"].reshape(1, S, D)
```

```python
from contextlib import ExitStack

import concourse.bass as bass
from concourse import mybir

F32 = mybir.dt.float32
F32R = mybir.dt.float32r
BF16 = mybir.dt.bfloat16
U32 = mybir.dt.uint32
ALU = mybir.AluOpType
ACT = mybir.ActivationFunctionType
AX_X = mybir.AxisListType.X

P = 128
D = 1024
S = 512
TT = S // P
KC = D // P
HEADS = 4
HD = 128
QK = 64
W4 = HEADS * S
PH = 8
TOPK = 16
NKEY = 128
HJ = 2 * PH
LAM_INIT = 0.2
EPS = 1e-6
NEG = -1e30
LOWEST = -3.0e38

RAW = 4
SPLIT = (2, 4)
UNIT = 1024

JG = 4
GROUPS = NKEY // JG
TB = 32
NTB = S // TB


class Steps:

    def __init__(self, sem):
        self.sem = sem
        self.n = 0

    def then(self, eng, ins):
        self.n += 1
        ins.then_inc(self.sem, 1)
        eng.wait_ge(self.sem, self.n)


class LoopSteps:

    def __init__(self, sem, i, each):
        self.sem, self.i, self.each = sem, i, each
        self.n = 0

    def then(self, eng, ins):
        self.n += 1
        ins.then_inc(self.sem, 1)
        eng.wait_ge(self.sem, self.i * self.each + self.n)

    def done(self):
        assert self.n == self.each, self.n


class Memory:
    pass


def build(nc, a):
    with ExitStack() as outer:
        m = Memory()

        def sb(name, shape, dt=F32, stack=outer):
            return stack.enter_context(nc.sbuf_tensor(name, shape, dt))

        def sem(name):
            return outer.enter_context(nc.semaphore(name))

        m.sb, m.sem = sb, sem
        m.psum = [outer.enter_context(nc.psum_tensor(f"bank{i}", [P, 512], F32)) for i in range(8)]
        m.dve = Steps(sem("dve_step"))
        m.act = Steps(sem("act_step"))
        m.pool = Steps(sem("pool_step"))

        m.ident = sb("ident", [P, P])
        m.ident_bf = sb("ident_bf", [P, P], BF16)
        m.ones = sb("ones", [P, P])
        m.eps = sb("eps", [P, 1])
        m.zero = sb("zero", [P, 1])
        m.mod = sb("mod", [P, 48])
        m.bada = sb("bada", [P, 48])
        m.gains = sb("gains", [P, 4, KC])
        m.cact = sb("cact", [P, KC])
        m.scale = sb("norm_scale", [P, KC])
        m.rowg = sb("rowg", [P, 2, D])
        m.ss = sb("sumsq", [P, TT])
        m.rstd = sb("rstd", [P, TT])
        m.rows = sb("rows", [P, TT, D])

        m.unit_landed = [sem(f"unit_landed{i}") for i in range(RAW)]
        m.unit_hi = sem("unit_hi")
        m.unit_lo = sem("unit_lo")
        m.unit_used = sem("unit_used")
        m.unit_evac = sem("unit_evac")
        m.units = 0
        m.evacs = 0

        stage_project(nc, a, m)
        stage_mix(nc, a, m)
        m.actT = sb("actT", [P, 2, KC, S], F32R)
        m.split = SPLIT[1]
        m.slotsT = sb("slotsT", [P, 3, S])
        m.iota = sb("iota", [P, NKEY])
        m.iota_bf = sb("iota_bf", [P, NKEY, ROUND], BF16)
        with ExitStack() as keep:
            m.raw = m.sb("raw3", [P, RAW, UNIT], F32, keep)
            m.hl = m.sb("hl3", [P, 2, SPLIT[1], UNIT], F32R, keep)
            stage_join(nc, a, m)
            stage_select(nc, a, m)
        m.u_raw = sb("u_raw", [P, JG, D])
        m.v_raw = sb("v_raw", [P, JG, D])
        m.early_in = sb("early_in", [P, JG, S])
        m.u_landed = sem("u_landed")
        m.stored = [sem("stored0"), sem("stored1")]
        m.early_landed = [sem(f"early_landed{j}") for j in range(JG)]
        stage_gates(nc, a, m)
        stage_experts(nc, a, m)



def units_load(nc, sp, m, src, raw, n0, count, after=None, done=0):
    def body(i, first):
        for u in range(RAW):
            if first and u < done:
                continue
            if not (first and n0 == 0):
                sp.wait_ge(m.unit_lo, i + (n0 - RAW + 1 + u))
            sp.dma_start(raw[:, u, :], src[bass.ds(i + u, 1), :, :].rearrange("a p f -> p (a f)")
                         ).then_inc(m.unit_landed[u], 16)
    body(0, True)
    if after:
        after(0)
    with sp.Fori(1, count // RAW) as k:
        body(k * RAW, False)
        if after:
            after(k)


def units_hi(nc, act, m, raw, hl, n0, count, done=0):
    def body(i, k, first):
        for u in range(done if first else 0, RAW):
            act.wait_ge(m.unit_landed[u], k * 16 + (n0 // RAW + 1) * 16)
            if not (first and n0 == 0 and u < m.split):
                act.wait_ge(m.unit_used, i + (n0 - m.split + 1 + u))
            nc.scalar.activation(hl[:, 0, u % m.split, :], raw[:, u, :], ACT.Copy).then_inc(m.unit_hi, 1)
    body(0, 0, True)
    if count > RAW:
        with act.Fori(1, count // RAW) as k:
            body(k * RAW, k, False)


def unit_lo(nc, dve, m, raw, hl, u, n):
    dve.wait_ge(m.unit_hi, n + 1)
    nc.vector.tensor_tensor(hl[:, 1, u % m.split, :], raw[:, u, :], hl[:, 0, u % m.split, :].bitcast(F32),
                            ALU.subtract).then_inc(m.unit_lo, 1)


PASSES = ((0, 0), (0, 1), (1, 0))


def column_units_pe(nc, pe, m, hl, n0, e0, count, piece_lo=None):
    def body(i, first):
        for u in range(RAW):
            pe.wait_ge(m.unit_lo, i + (n0 + 1 + u))
            if not (first and e0 == 0 and u < 2):
                pe.wait_ge(m.unit_evac, i + (e0 - 1 + u))
            bank = m.psum[u % 2]
            for kc in range(KC):
                if piece_lo is not None and first and u == 0:
                    pe.wait_ge(piece_lo, kc + 1)
                for j, (a, b) in enumerate(PASSES):
                    last = nc.tensor.matmul(bank[:], hl[:, a, u % m.split, kc * P:(kc + 1) * P],
                                            m.actT[:, b, kc, :], start=(kc == 0 and j == 0),
                                            stop=(kc == KC - 1 and j == 2))
            last.then_inc(m.unit_used, 1)
    body(0, True)
    with pe.Fori(1, count // RAW) as k:
        body(k * RAW, False)


def column_units_dve(nc, dve, m, raw, hl, dst, n0, e0, count):

    def body(i, last):
        for u in range(RAW):
            if not (last and u == RAW - 1):
                unit_lo(nc, dve, m, raw, hl, (u + 1) % RAW, i + (n0 + u + 1))
            dve.wait_ge(m.unit_used, i + (n0 + u + 1))
            nc.vector.tensor_copy(dst[:, bass.ds(i * S + u * S, S)], m.psum[u % 2][:]).then_inc(m.unit_evac, 1)
    with dve.Fori(0, count // RAW - 1) as k:
        body(k * RAW, False)
    body(count - RAW, True)


def row_units_pe(nc, pe, m, hl, n0, e0, groups, piece_lo=None):
    def body(g, parity, first):
        for u in range(RAW):
            pe.wait_ge(m.unit_lo, g * RAW + (n0 + 1 + u))
            if piece_lo is not None and first:
                pe.wait_ge(piece_lo, 2 * u + 2)
            for t in range(TT):
                if u == 0 and not first:
                    pe.wait_ge(m.unit_evac, g * TT + (e0 - TT + t + 1))
                for c in range(2):
                    kc = 2 * u + c
                    for j, (a, b) in enumerate(PASSES):
                        last = nc.tensor.matmul(m.psum[4 + t][:], m.actT[:, a, kc, t * P:(t + 1) * P],
                                                hl[:, b, u % m.split, c * S:(c + 1) * S],
                                                start=(kc == 0 and j == 0), stop=(kc == KC - 1 and j == 2))
            last.then_inc(m.unit_used, 1)
    body(0, 0, True)
    with pe.Fori(1, groups) as g:
        body(g, 0, False)


def row_units_dve(nc, dve, m, raw, hl, dst, n0, e0, groups, after=None, done=0, evac=None):
    if not done:
        unit_lo(nc, dve, m, raw, hl, 0, n0)
    for g in range(groups):
        for u in range(RAW):
            if not (g == groups - 1 and u == RAW - 1) and not (g == 0 and u + 1 < done):
                unit_lo(nc, dve, m, raw, hl, (u + 1) % RAW, g * RAW + (n0 + u + 1))
        dve.wait_ge(m.unit_used, g * RAW + (n0 + RAW))
        for t in range(TT):
            at = g * TT * S + t * S
            if evac:
                evac(g, t, m.psum[4 + t][:]).then_inc(m.unit_evac, 1)
            else:
                nc.vector.tensor_copy(dst[:, at:at + S], m.psum[4 + t][:]).then_inc(m.unit_evac, 1)
        if after:
            after(g)



ADA = 2
ADA_SLOTS = 4
ADA_FIRST = 16 // ADA
ADA_PE = (0, 6)
ADA_DVE = [c for c in range(ADA_FIRST) if c not in ADA_PE]
ADA_POOL = 32 // ADA


def ada_pe(nc, pe, m, c):
    pe.wait_ge(m.ada_landed[c % ADA_SLOTS], 16 * (c // ADA_SLOTS + 1))
    for n in range(ADA):
        col = c * ADA + n
        for kc in range(KC):
            last = nc.tensor.matmul(m.psum[7][:, col:col + 1], m.wada[:, c % ADA_SLOTS, n, kc, :],
                                    m.cact[:, kc:kc + 1], start=(kc == 0), stop=(kc == KC - 1))
    last.then_inc(m.ada_used, 1)


def ada_dve(nc, dve, m, acc, slot, landed, i):
    w = m.wada[:, slot]
    dve.wait_ge(m.ada_landed[slot], landed)
    out = acc[:, i * ADA:(i + 1) * ADA, :]
    m.dve.then(dve, nc.vector.tensor_scalar(out, w[:, :, 0], m.cact[:, 0:1], None, ALU.mult))
    for kc in range(1, KC):
        ins = nc.vector.scalar_tensor_tensor(out, w[:, :, kc], m.cact[:, kc:kc + 1], out, ALU.mult, ALU.add)
        if kc < KC - 1:
            m.dve.then(dve, ins)
    ins.then_inc(m.ada_dved, 1)


def sum_partitions(nc, m, out, rows):
    return nc.tensor.matmul(out, rows, m.ones[:, 0:1], start=True, stop=True)


def ada_pool(nc, pool, m, acc, st, slot, landed, i):
    w = m.wada[:, slot]
    pool.wait_ge(m.ada_landed[slot], landed)
    st.then(pool, nc.gpsimd.tensor_tensor(w, w, m.cact[:].unsqueeze(1).unsqueeze(3).to_broadcast([P, ADA, KC, P]),
                                          ALU.mult))
    st.then(pool, nc.gpsimd.tensor_tensor(w[:, :, 0:4], w[:, :, 0:4], w[:, :, 4:8], ALU.add))
    st.then(pool, nc.gpsimd.tensor_tensor(w[:, :, 0:2], w[:, :, 0:2], w[:, :, 2:4], ALU.add))
    nc.gpsimd.tensor_tensor(acc[:, bass.ds(i * ADA, ADA), :], w[:, :, 0], w[:, :, 1], ALU.add
                            ).then_inc(m.ada_pooled, 1)



def norm_stats(nc, act, m, x, scratch, rows_ready, out_sem):
    for t in range(TT):
        rows_ready(act, t)
        m.act.then(act, nc.scalar.activation(scratch, x[:, t, :], ACT.Square, accum_out=m.ss[:, t:t + 1]))
    nc.scalar.activation(m.rstd[:], m.ss[:], ACT.Sqrt, bias=m.eps[:, 0:1], scale=1.0 / D).then_inc(out_sem, 1)


def norm_rows_dve(nc, dve, m, x, xn, stats, stats_n, xn_ready):
    dve.wait_ge(stats, stats_n)
    m.dve.then(dve, nc.vector.reciprocal(m.rstd[:], m.rstd[:]))
    for t in range(TT):
        nc.vector.tensor_scalar(xn[:, t, :], x[:, t, :], m.rstd[:, t:t + 1], None, ALU.mult).then_inc(xn_ready, 1)


def transpose_pe(nc, pe, m, xn, banks, xn_ready, bank_free, transposed, between=None):
    for dc in range(KC):
        if between and 2 <= dc < 6:
            between(dc - 2)
        if dc >= 2:
            pe.wait_ge(bank_free, dc - 1)
        for t in range(TT):
            if dc == 0 and xn_ready is not None:
                pe.wait_ge(xn_ready, t + 1)
            last = nc.tensor.transpose(m.psum[banks + dc % 2][:, t * P:(t + 1) * P],
                                       xn[:, t, dc * P:(dc + 1) * P], m.ident[:])
        last.then_inc(transposed, 1)


def split_act(nc, act, m, actT, banks, piece, transposed, bank_free, piece_lo, hi_ready, modulated, sh, between=None):
    for dc in range(KC):
        if between and dc == 2:
            between()
        act.wait_ge(transposed, dc + 1)
        if dc >= 2:
            act.wait_ge(piece_lo, dc - 1)
        modulate(nc, m, piece[:, dc % 2, :], m.psum[banks + dc % 2][:], modulated, sh, dc).then_inc(bank_free, 1)
        act.wait_ge(bank_free, dc + 1)
        nc.scalar.activation(actT[:, 0, dc, :], piece[:, dc % 2, :], ACT.Copy).then_inc(hi_ready, 1)


def modulate(nc, m, out, x, modulated, sh, dc):
    if not modulated:
        return nc.scalar.activation(out, x, ACT.Copy)
    return nc.scalar.activation(out, x, ACT.Identity, scale=m.scale[:, dc:dc + 1], bias=m.mod[:, sh + dc:sh + dc + 1])


def split_dve(nc, dve, actT, piece, hi_ready, piece_lo, between=None):
    for dc in range(KC):
        if between and dc == 2:
            between()
        dve.wait_ge(hi_ready, dc + 1)
        nc.vector.tensor_tensor(actT[:, 1, dc, :], piece[:, dc % 2, :], actT[:, 0, dc, :].bitcast(F32),
                                ALU.subtract).then_inc(piece_lo, 1)



def stage_project(nc, a, m):
    m.keep = ExitStack()
    m.projT = m.sb("projT", [P, 4 * W4], F32, m.keep)
    m.projN = m.sb("projN", [P, 3 * TT * S], F32, m.keep)
    m.wada = m.sb("wada", [P, ADA_SLOTS, ADA, KC, P], F32, m.keep)
    m.acc = m.sb("ada_sums", [P, 32, P], F32, m.keep)
    m.small = m.sb("small2", [P, 2 * 2 * QK + 2 * HEADS + 2 * HD], F32, m.keep)
    m.lb = m.sb("lb", [P, 2, HEADS], F32, m.keep)
    m.ada_landed = [m.sem(f"ada_landed{i}") for i in range(ADA_SLOTS)]
    m.ada_used, m.ada_dved, m.ada_pooled = m.sem("ada_used"), m.sem("ada_dved"), m.sem("ada_pooled")
    m.kk = m.wada[:, 2].rearrange("p a k n -> p (a k n)")
    m.restart = m.wada[:, 3].rearrange("p a k n -> p (a k n)")[:, 0:W4 // 2].bitcast(BF16)
    q = m.projT[:, 2 * W4:3 * W4]
    f = m.projT[:, 3 * W4:4 * W4]
    theta = m.small[:, 4 * QK:4 * QK + 2 * HEADS]
    with ExitStack() as own:
        x = m.rows
        m.actT = m.sb("actT1", [P, 2, KC, S], F32R, own)
        xn = m.projN[:, 0:TT * D].rearrange("p (t d) -> p t d", t=TT)
        raw = m.sb("raw1", [P, RAW, UNIT], F32, own)
        hl = m.sb("hl1", [P, 2, SPLIT[0], UNIT], F32R, own)
        m.split = SPLIT[0]
        piece = m.sb("piece1", [P, 2, S], F32, own)
        acc = m.acc
        scratch = acc[:, 32 - KC:].rearrange("p a n -> p (a n)")
        xT = m.projT[:, 0:KC * S].rearrange("p (k s) -> p k s", k=KC)
        x_landed = [m.sem(f"x_tile{t}_landed") for t in range(TT)]
        small = m.sem("small_landed")
        ident_ready = m.sem("ident_ready")
        const_ready = m.sem("const_ready")
        c_ready = m.sem("c_ready")
        stats = m.sem("stats1")
        xn_ready = m.sem("xn_ready1")
        transposed = m.sem("transposed1")
        bank_free = m.sem("bank_free1")
        hi_ready = m.sem("hi_ready1")
        piece_lo = m.sem("piece_lo1")
        scale_ready = m.sem("scale_ready1")
        evened = m.sem("transposed_read1")
        small_landed, theta_diff, sig_ready = m.sem("small_landed2"), m.sem("theta_diff"), m.sem("sig_ready")
        gate_ready, log_ready, restart_ready = m.sem("gate_ready"), m.sem("log_ready"), m.sem("restart_ready")
        ada_step, first_summed = m.sem("ada_step"), m.sem("first_summed")
        block = own.enter_context(nc.Block())

        @block.sync
        def _(sp):
            for t in range(TT):
                sp.dma_start(x[:, t, :], a.x[t * P:(t + 1) * P, :]).then_inc(x_landed[t], 16)
                if t == 0:
                    sp.dma_start(m.cact[:], a.c).then_inc(small, 16)
                    sp.dma_start(m.bada[:], a.b_ada).then_inc(small, 16)
                    sp.dma_start(m.gains[:], a.gains).then_inc(small, 16)
            for c in range(ADA_FIRST):
                before = c - ADA_SLOTS
                if before in ADA_PE:
                    sp.wait_ge(m.ada_used, ADA_PE.index(before) + 1)
                elif before >= 0:
                    sp.wait_ge(m.ada_dved, ADA_DVE.index(before) + 1)
                sp.dma_start(m.wada[:, c % ADA_SLOTS], a.w_ada[c]).then_inc(m.ada_landed[c % ADA_SLOTS], 16)
            sp.dma_start(m.small[:], a.small).then_inc(small_landed, 16)

            def two_chunks(k, done):
                c = ADA_FIRST + 2 * done
                if isinstance(k, int) and k + done == 0:
                    sp.wait_ge(m.ada_used, len(ADA_PE))
                    sp.wait_ge(m.ada_dved, len(ADA_DVE))
                    for n in range(2):
                        sp.dma_start(m.wada[:, 2 + n], a.w_ada[c + n]).then_inc(m.ada_landed[2 + n], 16)
                    c += 2
                else:
                    c += 2
                    sp.wait_ge(m.ada_pooled, k * 2 + (2 * done + 2))
                for n in range(2):
                    sp.dma_start(m.wada[:, n], a.w_ada[bass.ds(k * 2 + (c + n), 1)].rearrange(
                        "o p a k n -> p (o a) k n")).then_inc(m.ada_landed[n], 16)
            units_load(nc, sp, m, a.w_cols, raw, 0, 16, lambda k: two_chunks(k, 0))
            units_load(nc, sp, m, a.w_rows, raw, 16, 12, lambda k: two_chunks(k, 4))

        @block.gpsimd
        def _(pool):
            m.pool.then(pool, nc.gpsimd.memset(m.ident[:], 0.0))
            m.pool.then(pool, nc.gpsimd.affine_select(
                out=m.ident[:], in_=m.ident[:], compare_op=ALU.not_equal, fill=1.0, base=0,
                pattern=[[-1, P]], channel_multiplier=1))
            nc.gpsimd.tensor_copy(m.ident_bf[:], m.ident[:]).then_inc(ident_ready, 1)
            nc.gpsimd.memset(m.ones[:], 1.0).then_inc(const_ready, 1)
            nc.gpsimd.memset(m.eps[:], EPS).then_inc(const_ready, 1)
            nc.gpsimd.memset(m.zero[:], 0.0).then_inc(const_ready, 1)
            pool.wait_ge(c_ready, 1)
            pool.wait_ge(first_summed, 1)
            st = LoopSteps(ada_step, 0, 6)
            for i in range(2):
                ada_pool(nc, pool, m, acc, st, 2 + i, 48, i)
            st.done()
            pool.wait_ge(m.ada_pooled, 2)
            m.pool.then(pool, nc.gpsimd.memset(m.restart, 1.0))
            nc.gpsimd.memset(m.restart.rearrange("p (n c) -> p n c", c=CHUNK)[:, :, 0:1], 0.0
                             ).then_inc(restart_ready, 1)
            last = ADA_POOL // 2 - 1
            with pool.Fori(1, last) as k:
                st = LoopSteps(ada_step, k, 6)
                for i in range(2):
                    ada_pool(nc, pool, m, acc, st, i, k * 16 + 32, k * 2 + i)
                st.done()
            ada_pool(nc, pool, m, acc, LoopSteps(ada_step, last, 6), 0, last * 16 + 32, last * 2)

        @block.scalar
        def _(act):
            act.wait_ge(const_ready, 3)
            act.wait_ge(small, 48)
            nc.scalar.activation(m.cact[:], m.cact[:], ACT.Silu).then_inc(c_ready, 1)
            norm_stats(nc, act, m, x, scratch[:], lambda e, t: e.wait_ge(x_landed[t], 16), stats)
            for dc in range(KC):
                act.wait_ge(transposed, dc + 1)
                nc.scalar.activation(xT[:, dc, :], m.psum[dc % 2][:], ACT.Copy).then_inc(bank_free, 1)
            for u in range(2):
                act.wait_ge(m.unit_landed[u], 16)
                nc.scalar.activation(hl[:, 0, u, :], raw[:, u, :], ACT.Copy).then_inc(m.unit_hi, 1)
            act.wait_ge(bank_free, KC)
            act.wait_ge(scale_ready, 1)
            for dc in range(KC):
                if dc >= 2:
                    act.wait_ge(piece_lo, dc - 1)
                modulate(nc, m, piece[:, dc % 2, :], xT[:, dc, :], True, 0, dc).then_inc(evened, 1)
                act.wait_ge(evened, dc + 1)
                nc.scalar.activation(m.actT[:, 0, dc, :], piece[:, dc % 2, :], ACT.Copy).then_inc(hi_ready, 1)
            units_hi(nc, act, m, raw, hl, 0, 16, 2)
            units_hi(nc, act, m, raw, hl, 16, RAW)
            act.wait_ge(theta_diff, 1)
            nc.scalar.activation(m.lb[:, 0, :], theta[:, 0:HEADS], ACT.Sigmoid).then_inc(sig_ready, 1)
            act.wait_ge(m.unit_evac, 16)
            nc.scalar.activation(f, f, ACT.Sigmoid).then_inc(sig_ready, 1)
            nc.scalar.activation(q, q, ACT.Silu).then_inc(sig_ready, 1)
            units_hi(nc, act, m, raw, hl, 16 + RAW, RAW)
            act.wait_ge(gate_ready, 1)
            nc.scalar.activation(f, f, ACT.Ln).then_inc(log_ready, 1)
            units_hi(nc, act, m, raw, hl, 16 + 2 * RAW, RAW)

        @block.vector
        def _(dve):
            norm_rows_dve(nc, dve, m, x, xn, stats, 1, xn_ready)
            dve.wait_ge(c_ready, 1)
            for i, c in enumerate(ADA_DVE):
                ada_dve(nc, dve, m, acc, c % ADA_SLOTS, 16 * (c // ADA_SLOTS + 1), i)
            unit_lo(nc, dve, m, raw, hl, 0, 0)
            dve.wait_ge(first_summed, 1)
            m.dve.then(dve, nc.vector.tensor_tensor(m.mod[:, 0:16], m.psum[7][:, 0:16], m.bada[:, 0:16], ALU.add))
            nc.vector.scalar_tensor_tensor(m.scale[:], m.mod[:, 8:16], 1.0, m.gains[:, 0, :],
                                           ALU.add, ALU.mult).then_inc(scale_ready, 1)
            split_dve(nc, dve, m.actT, piece, hi_ready, piece_lo)
            column_units_dve(nc, dve, m, raw, hl, m.projT, 0, 0, 16)

            dve.wait_ge(small_landed, 16)
            nc.vector.tensor_tensor(theta[:, 0:HEADS], theta[:, 0:HEADS], theta[:, HEADS:2 * HEADS],
                                    ALU.subtract).then_inc(theta_diff, 1)

            def gates_of_recurrence(g):
                V = nc.vector
                if g == 0:
                    dve.wait_ge(sig_ready, 2)
                    m.dve.then(dve, V.tensor_scalar(m.lb[:, 1, :], m.lb[:, 0, :], -1.0, 1.0, ALU.mult, ALU.add))
                    for h in range(HEADS):
                        fh = f[:, h * S:(h + 1) * S]
                        last = V.tensor_scalar(fh, fh, m.lb[:, 1, h:h + 1], m.lb[:, 0, h:h + 1], ALU.mult, ALU.add)
                    m.dve.then(dve, last)
                    dve.wait_ge(m.ada_pooled, 2)
                    V.tensor_scalar(m.kk, f, -1.0, 1.0, ALU.mult, ALU.add).then_inc(gate_ready, 1)
                elif g == 1:
                    dve.wait_ge(log_ready, 1)
                    dve.wait_ge(restart_ready, 1)
                    m.dve.then(dve, V.tensor_tensor_scan(f, m.restart, f, 0.0, ALU.mult, ALU.add))
            row_units_dve(nc, dve, m, raw, hl, m.projN, 16, 16, 3, gates_of_recurrence)
            ada_dve(nc, dve, m, acc, 1, (ADA_POOL // 2 + 1) * 16, ADA_POOL - 1)
            dve.wait_ge(m.ada_dved, len(ADA_DVE) + 1)

        @block.tensor
        def _(pe):
            pe.wait_ge(ident_ready, 1)
            pe.wait_ge(c_ready, 1)
            ada_pe(nc, pe, m, 0)
            transpose_pe(nc, pe, m, xn, 0, xn_ready, bank_free, transposed)

            def sums_of_dve(some):
                for i in some:
                    pe.wait_ge(m.ada_dved, i + 1)
                    for n in range(ADA):
                        col = ADA_DVE[i] * ADA + n
                        last = sum_partitions(nc, m, m.psum[7][:, col:col + 1], acc[:, i * ADA + n, :])
                return last
            pe.wait_ge(const_ready, 3)
            sums_of_dve(range(3))
            ada_pe(nc, pe, m, 6)
            sums_of_dve(range(3, len(ADA_DVE))).then_inc(first_summed, 1)
            pe.wait_ge(bank_free, KC)
            column_units_pe(nc, pe, m, hl, 0, 0, 16, piece_lo)
            row_units_pe(nc, pe, m, hl, 16, 16, 3)
    m.units, m.evacs = 28, 28



LEVELS = ("own", 8, 16, 32, 64)
OWN = 8
OWN_REF = 3
CHUNK = P
NCH = S // CHUNK
STEPS_A = HEADS * TT
LEVEL_AT = 8
LEVEL_END = LEVEL_AT + HEADS * len(LEVELS) // 2
ITEMS = {1: 0, 3: 1, 5: 2, 7: 3, 9: 4, 11: "kb"}
SLOT_E = (0, 0, 1, 0, 1)
SLOT_F = ((0, 1), (2, 2), (3, 3), (0, 0), (1, 1))


def stage_mix(nc, a, m):
    with ExitStack() as own:
        def sb(name, shape, dt=F32):
            return m.sb(name, shape, dt, own)

        cat = m.rows
        q = m.projT[:, 2 * W4:3 * W4]
        f = m.projT[:, 3 * W4:4 * W4]
        av = m.projN[:, 0:TT * S].rearrange("p (t n) -> p t n", t=TT)
        hi = m.projN[:, TT * S:2 * TT * S].rearrange("p (t n) -> p t n", t=TT)
        hg = m.projN[:, 2 * TT * S:3 * TT * S]
        kk = m.kk
        b = f
        E = m.wada[:, 0:2].rearrange("p s a k n -> p s (a k n)")
        F = sb("F", [P, 4, W4])
        attnT = sb("attnT", [P, HEADS, S])
        kbT = sb("kbT", [P, NCH - 1, HEADS * HD])
        state = sb("state", [P, NCH - 1, HEADS * HD])
        prob = sb("prob", [P, 2, S])
        mixed = sb("mixed", [P, 2, S])
        mixedT = sb("mixedT", [P, 2, S])
        masks = sb("masks", [P, len(LEVELS), P])
        negmask = sb("negmask", [P, P], BF16)
        decay = sb("decay", [P, HEADS * NCH])
        lamp = sb("lamp", [P, 2 * QK])
        lams = sb("lams", [P, 4])
        nbias = sb("nbias", [P, 2, 2])
        Z = sb("Z", [P, 2, 2])
        rz = sb("rz", [P, 2, 2])
        ss = sb("ss2", [P, 2, TT, HEADS])
        small = m.small
        lam = small[:, 0:4 * QK]
        g_diff = small[:, 4 * QK + 2 * HEADS:4 * QK + 2 * HEADS + HD]
        g_hgrn = small[:, 4 * QK + 2 * HEADS + HD:]

        masks_ready = m.sem("masks_ready")
        mod_summed, mod_read = m.sem("mod_summed"), m.sem("mod_read")
        hg_ready = m.sem("hg_ready")
        lam_sums = m.sem("lam_sums")
        lam_exps = m.sem("lam_exps")
        scores = m.sem("scores")
        bias_ready = m.sem("bias_ready")
        probs_ready = m.sem("probs_ready")
        mixed_ready = m.sem("mixed_ready")
        mixed_tr = m.sem("mixed_tr")
        mixedT_ready = m.sem("mixedT_ready")
        attn_out = m.sem("attn_out")
        attn_read = m.sem("attn_read")
        diff_ready = m.sem("diff_ready")
        exp_ready = m.sem("exp_ready")
        f_ready = m.sem("f_ready")
        level_done = m.sem("level_done")
        level_copied = m.sem("level_copied")
        kb_tr = m.sem("kb_tr")
        kbT_ready = m.sem("kbT_ready")
        kv_done = m.sem("kv_done")
        state_ready = m.sem("state_ready")
        hgrn_out = m.sem("hgrn_out")
        hgrn_read = m.sem("hgrn_read")
        squares = m.sem("squares")
        sums = m.sem("sums")
        roots, inverses = m.sem("roots"), m.sem("inverse_norms")

        block = own.enter_context(nc.Block())
        b_k = b.rearrange("p (n c) -> p n c", c=CHUNK)
        last_b = b_k[:, :, CHUNK - 1:CHUNK]

        @block.gpsimd
        def _(pool):
            g = nc.gpsimd
            m.pool.then(pool, g.memset(negmask[:], 0.0))
            g.affine_select(out=negmask[:], in_=negmask[:], compare_op=ALU.is_ge, fill=NEG, base=0,
                            pattern=[[-1, P]], channel_multiplier=1).then_inc(masks_ready, 1)
            m.pool.then(pool, g.memset(masks[:], 0.0))
            own_mask = masks[:, 0, :].rearrange("p (n c) -> p n c", c=OWN)
            m.pool.then(pool, g.memset(masks[:, 0, :], 1.0))
            m.pool.then(pool, g.affine_select(out=own_mask, in_=own_mask, compare_op=ALU.is_ge, fill=0.0, base=0,
                                              pattern=[[-OWN, P // OWN], [0, OWN]], channel_multiplier=1))
            m.pool.then(pool, g.affine_select(out=own_mask, in_=own_mask, compare_op=ALU.is_ge, fill=0.0, base=0,
                                              pattern=[[OWN, P // OWN], [1, OWN]], channel_multiplier=-1))
            for level in range(1, len(LEVELS)):
                h = LEVELS[level]
                right = masks[:, level, :].rearrange("p (n c) -> p n c", c=2 * h)[:, :, h:2 * h]
                m.pool.then(pool, g.memset(right, 1.0))
                m.pool.then(pool, g.affine_select(out=right, in_=right, compare_op=ALU.is_ge, fill=0.0, base=0,
                                                  pattern=[[-2 * h, P // (2 * h)], [0, h]], channel_multiplier=1))
                m.pool.then(pool, g.affine_select(out=right, in_=right, compare_op=ALU.is_ge, fill=0.0, base=h - 1,
                                                  pattern=[[2 * h, P // (2 * h)], [0, h]], channel_multiplier=-1))
            g.memset(attnT[:], 0.0).then_inc(masks_ready, 1)
            pool.wait_ge(exp_ready, 1)
            g.tensor_tensor(F[:, 0, :], E[:, 0, :], kk, ALU.mult).then_inc(f_ready, 1)
            g.tensor_tensor(F[:, 1, :], E[:, 1, :], q, ALU.mult).then_inc(f_ready, 1)
            for level in range(1, len(LEVELS)):
                h = LEVELS[level]
                pool.wait_ge(exp_ready, level + 1)
                if level == 3:
                    pool.wait_ge(level_done, HEADS)
                out = F[:, SLOT_F[level][0], :].rearrange("p (n c) -> p n c", c=2 * h)
                e = E[:, SLOT_E[level], :].rearrange("p (n c) -> p n c", c=2 * h)
                kv = kk.rearrange("p (n c) -> p n c", c=2 * h)
                qv = q.rearrange("p (n c) -> p n c", c=2 * h)
                g.tensor_tensor(out[:, :, 0:h], e[:, :, 0:h], kv[:, :, 0:h], ALU.mult).then_inc(f_ready, 1)
                g.tensor_tensor(out[:, :, h:], e[:, :, h:], qv[:, :, h:], ALU.mult).then_inc(f_ready, 1)
            pool.wait_ge(exp_ready, len(LEVELS) + 1)
            pool.wait_ge(level_done, 3 * HEADS)
            g.tensor_tensor(F[:, 2, :], E[:, 0, :], q, ALU.mult).then_inc(f_ready, 1)
            g.tensor_tensor(F[:, 3, :], E[:, 1, :], kk, ALU.mult).then_inc(f_ready, 1)
            pool.wait_ge(hg_ready, 1)
            g.tensor_tensor(hg.rearrange("p (n c) -> p n c", c=HD), hg.rearrange("p (n c) -> p n c", c=HD),
                            g_hgrn.unsqueeze(1).to_broadcast([P, TT * HEADS, HD]), ALU.mult).then_inc(hg_ready, 1)
            pool.wait_ge(inverses, 1)
            for t in range(TT):
                cv = cat[:, t, 0:HEADS * HD].rearrange("p (h v) -> p h v", v=HD)
                m.pool.then(pool, g.tensor_tensor(cv, cv, ss[:, 0, t, :].unsqueeze(2).to_broadcast([P, HEADS, HD]),
                                                  ALU.mult))
                m.pool.then(pool, g.tensor_tensor(cv, cv, g_diff.unsqueeze(1).to_broadcast([P, HEADS, HD]),
                                                  ALU.mult))

        @block.scalar
        def _(act):
            A = nc.scalar.activation
            A(hg, hg, ACT.Silu).then_inc(hg_ready, 1)
            act.wait_ge(lam_sums, 1)
            A(lams[:, 2:4], lams[:, 0:2], ACT.Exp).then_inc(lam_exps, 1)
            for n in range(STEPS_A + 1):
                if n < STEPS_A:
                    k = (n % TT + 1) * P
                    act.wait_ge(bias_ready, n + 1)
                    if n >= 1:
                        act.wait_ge(mixed_ready, n)
                    for j in range(2):
                        A(prob[:, j, 0:k], m.psum[2 * (n % 2) + j][:, 0:k], ACT.Exp, bias=nbias[:, n % 2, j:j + 1],
                          scale=QK ** -0.5, accum_out=Z[:, n % 2, j:j + 1]).then_inc(probs_ready, 1)
                if n >= 1:
                    k = ((n - 1) % TT + 1) * P
                    act.wait_ge(mixed_tr, n)
                    if n >= 3:
                        act.wait_ge(attn_out, n - 2)
                    A(mixedT[:, (n - 1) % 2, 0:k], m.psum[4][:, 0:k], ACT.Copy).then_inc(mixedT_ready, 1)
                item = ITEMS.get(n)
                if item == 0:
                    act.wait_ge(diff_ready, 1)
                    m.act.then(act, A(E[:, 1, :], E[:, 0, :], ACT.Exp))
                    A(E[:, 0, :], E[:, 0, :], ACT.Exp, scale=-1.0).then_inc(exp_ready, 1)
                elif item == "kb":
                    act.wait_ge(diff_ready, len(LEVELS) + 1)
                    m.act.then(act, A(decay[:].rearrange("p (n o) -> p n o", o=1), last_b, ACT.Exp))
                    m.act.then(act, A(E[:, 0, :], b, ACT.Exp))
                    A(E[:, 1, :], E[:, 1, :], ACT.Exp).then_inc(exp_ready, 1)
                elif item is not None:
                    h = LEVELS[item]
                    act.wait_ge(diff_ready, item + 1)
                    e = E[:, SLOT_E[item], :].rearrange("p (n c) -> p n c", c=2 * h)
                    m.act.then(act, A(e[:, :, 0:h], e[:, :, 0:h], ACT.Exp, scale=-1.0))
                    A(e[:, :, h:], e[:, :, h:], ACT.Exp).then_inc(exp_ready, 1)
            for n in range(NCH - 1):
                act.wait_ge(kb_tr, n + 1)
                A(kbT[:, n, :], m.psum[n % 2][:], ACT.Copy).then_inc(kbT_ready, 1)
            act.wait_ge(f_ready, 2 * len(LEVELS) + 2)
            act.wait_ge(attn_read, STEPS_A)
            for half in range(2):
                for t in range(TT):
                    if half:
                        act.wait_ge(hgrn_read, t + 1)
                    A(E[:, half, t * S:(t + 1) * S], cat[:, t, half * S:(half + 1) * S], ACT.Square
                      ).then_inc(squares, 1)
                act.wait_ge(sums, (half + 1) * TT)
                A(ss[:, half], ss[:, half], ACT.Sqrt, bias=m.eps[:, 0:1], scale=1.0 / HD).then_inc(roots, 1)

        @block.vector
        def _(dve):
            V = nc.vector
            lv = lam.rearrange("p (a b) -> p a b", b=2 * QK)
            m.dve.then(dve, V.tensor_tensor(lamp[:].rearrange("p (a b) -> p a b", b=QK), lv[:, :, 0:QK],
                                            lv[:, :, QK:2 * QK], ALU.mult))
            V.tensor_reduce(lams[:, 0:2], lamp[:].rearrange("p (a b) -> p a b", b=QK), AX_X, ALU.add
                            ).then_inc(lam_sums, 1)
            m.dve.then(dve, V.tensor_scalar(g_diff, g_diff, 1.0 - LAM_INIT, None, ALU.mult))
            dve.wait_ge(lam_exps, 1)
            m.dve.then(dve, V.tensor_tensor(lams[:, 0:1], lams[:, 3:4], lams[:, 2:3], ALU.subtract))
            m.dve.then(dve, V.tensor_scalar(lams[:, 0:1], lams[:, 0:1], -LAM_INIT, None, ALU.add))
            def level_copies(n):
                for u in range(2 * (n - LEVEL_AT), 2 * (n - LEVEL_AT) + 2):
                    level, h = divmod(u, HEADS)
                    dve.wait_ge(level_done, u + 1)
                    V.copy_predicated(attnT[:, h, :].rearrange("p (n c) -> p n c", c=P),
                                      masks[:, level, :].bitcast(U32).unsqueeze(1).to_broadcast([P, NCH, P]),
                                      m.psum[6 + u % 2][:].rearrange("p (n c) -> p n c", c=P)
                                      ).then_inc(level_copied, 1)

            for n in range(STEPS_A + 2):
                if n < STEPS_A:
                    k = (n % TT + 1) * P
                    dve.wait_ge(scores, n + 1)
                    for j in range(2):
                        m.dve.then(dve, V.tensor_reduce(nbias[:, n % 2, j:j + 1], m.psum[2 * (n % 2) + j][:, 0:k],
                                                        AX_X, ALU.max))
                    V.tensor_scalar(nbias[:, n % 2, :], nbias[:, n % 2, :], -QK ** -0.5, None, ALU.mult
                                    ).then_inc(bias_ready, 1)
                if 1 <= n <= STEPS_A:
                    o = n - 1
                    k = (o % TT + 1) * P
                    dve.wait_ge(probs_ready, 2 * n)
                    if o >= 2:
                        dve.wait_ge(mixed_tr, o - 1)
                    m.dve.then(dve, V.reciprocal(rz[:, o % 2, :], Z[:, o % 2, :]))
                    m.dve.then(dve, V.tensor_scalar(rz[:, o % 2, 1:2], rz[:, o % 2, 1:2], lams[:, 0:1], None, ALU.mult))
                    m.dve.then(dve, V.tensor_scalar(mixed[:, o % 2, 0:k], prob[:, 0, 0:k], rz[:, o % 2, 0:1], None,
                                                    ALU.mult))
                    V.scalar_tensor_tensor(mixed[:, o % 2, 0:k], prob[:, 1, 0:k], rz[:, o % 2, 1:2],
                                           mixed[:, o % 2, 0:k], ALU.mult, ALU.add).then_inc(mixed_ready, 1)
                item = ITEMS.get(n)
                if item is not None:
                    if item == 0:
                        bv = b.rearrange("p (n c) -> p n c", c=OWN)
                        e = E[:, 0, :].rearrange("p (n c) -> p n c", c=OWN)
                        ref = bv[:, :, OWN_REF:OWN_REF + 1].to_broadcast([P, W4 // OWN, OWN])
                        V.tensor_tensor(e, bv, ref, ALU.subtract).then_inc(diff_ready, 1)
                    elif item == "kb":
                        dve.wait_ge(f_ready, 2 * len(LEVELS))
                        e = E[:, 1, :].rearrange("p (n c) -> p n c", c=CHUNK)
                        V.tensor_tensor(e, last_b.to_broadcast([P, HEADS * NCH, CHUNK]), b_k, ALU.subtract
                                        ).then_inc(diff_ready, 1)
                    else:
                        dve.wait_ge(f_ready, 2 if item <= 2 else 2 * (item - 1))
                        h = LEVELS[item]
                        bv = b.rearrange("p (n c) -> p n c", c=2 * h)
                        e = E[:, SLOT_E[item], :].rearrange("p (n c) -> p n c", c=2 * h)
                        ref = bv[:, :, h - 1:h].to_broadcast([P, W4 // (2 * h), 2 * h])
                        V.tensor_tensor(e, bv, ref, ALU.subtract).then_inc(diff_ready, 1)
                if n >= 2:
                    o = n - 2
                    h, t = divmod(o, TT)
                    dve.wait_ge(attn_out, o + 1)
                    V.tensor_copy(cat[:, t, h * HD:(h + 1) * HD], m.psum[5][:, 0:HD]).then_inc(attn_read, 1)
                if n == LEVEL_AT - 1:
                    dve.wait_ge(mod_summed, LEVEL_AT)
                    V.tensor_tensor(m.mod[:, 16:48], m.psum[7][:, 0:32], m.bada[:, 16:48], ALU.add
                                    ).then_inc(mod_read, 1)
                if n == LEVEL_AT:
                    dve.wait_ge(masks_ready, 2)
                if LEVEL_AT <= n < LEVEL_END:
                    level_copies(n)
            for n in range(NCH - 1):
                dve.wait_ge(kv_done, n + 1)
                st = state[:, n, :].rearrange("p (h v) -> p h v", h=HEADS)
                kv = m.psum[2 + n % 2][:].rearrange("p (h v) -> p h v", h=HEADS)
                if n == 0:
                    V.tensor_copy(st, kv).then_inc(state_ready, 1)
                else:
                    dve.wait_ge(state_ready, n)
                    before = state[:, n - 1, :].rearrange("p (h v) -> p h v", h=HEADS)
                    dec = decay[:].rearrange("p (h n) -> p h n", h=HEADS)[:, :, n:n + 1].to_broadcast([P, HEADS, HD])
                    m.dve.then(dve, V.tensor_tensor(st, before, dec, ALU.mult))
                    V.tensor_tensor(st, st, kv, ALU.add).then_inc(state_ready, 1)
            def inverse_norms(half):
                dve.wait_ge(roots, half + 1)
                V.reciprocal(ss[:, half], ss[:, half]).then_inc(inverses, 1)
                dve.wait_ge(inverses, half + 1)

            def sum_squares(half, t):
                dve.wait_ge(squares, half * TT + t + 1)
                V.tensor_reduce(ss[:, half, t, :], E[:, half, t * S:(t + 1) * S].rearrange("p (h v) -> p h v", v=HD),
                                AX_X, ALU.add).then_inc(sums, 1)
            for t in range(TT):
                sum_squares(0, t)
                dve.wait_ge(hgrn_out, t + 1)
                V.tensor_copy(cat[:, t, HEADS * HD:], m.psum[4 + t][:]).then_inc(hgrn_read, 1)
            inverse_norms(0)
            for t in range(TT):
                sum_squares(1, t)
            inverse_norms(1)
            dve.wait_ge(hg_ready, 2)
            hgv = hg.rearrange("p (t n) -> p t n", t=TT)
            for t in range(TT):
                cv = cat[:, t, HEADS * HD:].rearrange("p (h v) -> p h v", v=HD)
                m.dve.then(dve, V.tensor_tensor(cv, cv, ss[:, 1, t, :].unsqueeze(2).to_broadcast([P, HEADS, HD]),
                                                ALU.mult))
                m.dve.then(dve, V.tensor_tensor(cat[:, t, HEADS * HD:], cat[:, t, HEADS * HD:], hgv[:, t, :],
                                                ALU.mult))

        @block.tensor
        def _(pe):
            T = nc.tensor
            aq, ak = m.projT[:, 0:W4], m.projT[:, W4:2 * W4]
            pe.wait_ge(masks_ready, 1)

            def level_matmuls(n):
                for u in range(2 * (n - LEVEL_AT), 2 * (n - LEVEL_AT) + 2):
                    level, h = divmod(u, HEADS)
                    pe.wait_ge(f_ready, 2 * level + 2)
                    if u >= 2:
                        pe.wait_ge(level_copied, u - 1)
                    for c in range(NCH):
                        at = slice(h * S + c * CHUNK, h * S + (c + 1) * CHUNK)
                        last = T.matmul(m.psum[6 + u % 2][:, c * CHUNK:(c + 1) * CHUNK], F[:, SLOT_F[level][0], at],
                                        F[:, SLOT_F[level][1], at], start=True, stop=True)
                    last.then_inc(level_done, 1)

            for n in range(STEPS_A + 2):
                if n < STEPS_A:
                    h, t = divmod(n, TT)
                    k = (t + 1) * P
                    if n >= 2:
                        pe.wait_ge(probs_ready, 2 * (n - 1))
                    for j in range(2):
                        part = slice(j * QK, (j + 1) * QK)
                        bank = m.psum[2 * (n % 2) + j]
                        T.matmul(bank[:, 0:k], aq[part, h * S + t * P:h * S + (t + 1) * P],
                                 ak[part, h * S:h * S + k], start=True, stop=False)
                        last = T.matmul(bank[:, t * P:k], m.ident_bf[:], negmask[:], start=False, stop=True)
                    last.then_inc(scores, 1)
                if n >= 2:
                    o = n - 2
                    h, t = divmod(o, TT)
                    pe.wait_ge(mixedT_ready, o + 1)
                    if o >= 1:
                        pe.wait_ge(attn_read, o)
                    for kb in range(t + 1):
                        last = T.matmul(m.psum[5][:, 0:HD], mixedT[:, o % 2, kb * P:(kb + 1) * P],
                                        av[:, kb, h * HD:(h + 1) * HD], start=(kb == 0), stop=(kb == t))
                    last.then_inc(attn_out, 1)
                if n < LEVEL_AT:
                    for c in range(n * 32 // LEVEL_AT, (n + 1) * 32 // LEVEL_AT):
                        last = sum_partitions(nc, m, m.psum[7][:, c:c + 1], m.acc[:, c, :])
                    last.then_inc(mod_summed, 1)
                if LEVEL_AT <= n < LEVEL_END:
                    if n == LEVEL_AT:
                        pe.wait_ge(mod_read, 1)
                    level_matmuls(n)
                if 1 <= n <= STEPS_A:
                    o = n - 1
                    pe.wait_ge(mixed_ready, o + 1)
                    if o >= 1:
                        pe.wait_ge(mixedT_ready, o)
                    for kb in range(o % TT + 1):
                        last = T.transpose(m.psum[4][:, kb * P:(kb + 1) * P], mixed[:, o % 2, kb * P:(kb + 1) * P],
                                           m.ident[:])
                    last.then_inc(mixed_tr, 1)
            pe.wait_ge(f_ready, 2 * len(LEVELS) + 2)
            for n in range(NCH - 1):
                if n >= 2:
                    pe.wait_ge(kbT_ready, n - 1)
                for h in range(HEADS):
                    last = T.transpose(m.psum[n % 2][:, h * HD:(h + 1) * HD],
                                       F[:, 3, h * S + n * CHUNK:h * S + (n + 1) * CHUNK], m.ident[:])
                last.then_inc(kb_tr, 1)
            for n in range(NCH - 1):
                pe.wait_ge(kbT_ready, n + 1)
                if n >= 2:
                    pe.wait_ge(state_ready, n - 1)
                for h in range(HEADS):
                    last = T.matmul(m.psum[2 + n % 2][:, h * HD:(h + 1) * HD], kbT[:, n, h * HD:(h + 1) * HD],
                                    hi[:, n, h * HD:(h + 1) * HD], start=True, stop=True)
                last.then_inc(kv_done, 1)
            pe.wait_ge(attn_read, STEPS_A)
            pe.wait_ge(level_copied, HEADS * len(LEVELS))
            for t in range(NCH):
                if t >= 1:
                    pe.wait_ge(state_ready, t)
                for h in range(HEADS):
                    at = slice(h * S + t * CHUNK, h * S + (t + 1) * CHUNK)
                    out = m.psum[4 + t][:, h * HD:(h + 1) * HD]
                    last = T.matmul(out, attnT[:, h, t * CHUNK:(t + 1) * CHUNK], hi[:, t, h * HD:(h + 1) * HD],
                                    start=True, stop=(t == 0))
                    if t >= 1:
                        last = T.matmul(out, F[:, 2, at], state[:, t - 1, h * HD:(h + 1) * HD], start=False, stop=True)
                last.then_inc(hgrn_out, 1)
    m.keep.close()



def stage_join(nc, a, m):
    h2T = m.actT
    with ExitStack() as own:
        m.actT = m.sb("catT", [P, 2, KC, S], F32R, own)
        catT = m.actT
        raw, hl = m.raw, m.hl
        x = m.sb("x3", [P, TT, D], F32, own)
        piece = m.sb("piece3", [P, 2, S], F32, own)
        scratch = m.sb("scratch3", [P, D], F32, own)
        gcol = m.sb("gcol", [P, 2, KC], F32, own)
        diag = m.sb("diag", [P, 2 * KC, P], F32, own)
        y = m.rows[:].rearrange("p t d -> p (t d)").rearrange("p (g t n) -> p t g n", g=2, t=TT)
        sem = m.sem
        x_landed = sem("x_again_landed")
        diag_ready, row_ready = sem("diag_ready"), sem("row_ready")
        cat_tr, cat_free, cat_lo, cat_hi = sem("cat_tr"), sem("cat_free"), sem("cat_lo"), sem("cat_hi")
        stats = sem("stats3")
        x2_ready, x2_stored = sem("x2_ready"), sem("x2_stored")
        stats_b, xn_ready = sem("stats3b"), sem("xn_ready3")
        transposed, bank_free, hi_ready, piece_lo = sem("tr3"), sem("free3"), sem("hi3"), sem("lo3")
        squared, parts_added = sem("squared3"), sem("parts_added")
        parts = m.sb("sumsq_parts", [P, 2, TT], F32, own)
        n0, e0 = m.units, m.evacs
        block = own.enter_context(nc.Block())

        @block.sync
        def _(sp):
            def residual(k):
                if isinstance(k, int) and k == 0:
                    sp.dma_start(x[:], a.x.rearrange("(t p) d -> p t d", p=P)).then_inc(x_landed, 16)
            units_load(nc, sp, m, a.w_out, raw, n0, 8, residual)
            for u in range(RAW):
                sp.wait_ge(m.unit_lo, n0 + 8 - RAW + 1 + u)
                sp.dma_start(raw[:, u, :], a.w_pq[u]).then_inc(m.unit_landed[u], 16)
            sp.wait_ge(x2_ready, TT)
            sp.dma_start(a.x2, x[:]).then_inc(x2_stored, 16)
            sp.wait_ge(x2_stored, 16)

        @block.gpsimd
        def _(pool):
            for u in range(RAW):
                pool.wait_ge(m.unit_hi, n0 + 8 + u + 1)
                nc.gpsimd.tensor_tensor(hl[:, 1, u, :], raw[:, u, :], hl[:, 0, u, :].bitcast(F32), ALU.subtract
                                        ).then_inc(m.unit_lo, 1)

        @block.scalar
        def _(act):
            A = nc.scalar.activation

            def hi(n, landed):
                u = n % RAW
                act.wait_ge(m.unit_landed[u], landed)
                A(hl[:, 0, u, :], raw[:, u, :], ACT.Copy).then_inc(m.unit_hi, 1)
            rounds = n0 // RAW

            def first_hi():
                for n in range(2):
                    hi(n, (rounds + 1) * 16)
            split_act(nc, act, m, catT, 4, piece, cat_tr, cat_free, cat_lo, cat_hi, False, 0, first_hi)

            def squares(g):
                act.wait_ge(m.unit_used, n0 + (g + 1) * RAW)
                for t in range(TT):
                    A(scratch[:, (t % 2) * S:(t % 2 + 1) * S], m.psum[4 + t][:], ACT.Square,
                      accum_out=parts[:, g, t:t + 1]).then_inc(squared, 1)
                    act.wait_ge(squared, g * TT + t + 1)
            for n in range(2, 8):
                if n == 7:
                    squares(0)
                if n >= RAW:
                    act.wait_ge(m.unit_used, n0 + n - RAW + 1)
                hi(n, (rounds + n // RAW + 1) * 16)
            squares(1)
            act.wait_ge(parts_added, 1)
            A(m.rstd[:], m.ss[:], ACT.Sqrt, bias=m.eps[:, 0:1], scale=1.0 / D).then_inc(stats, 1)
            for n in range(8, 8 + RAW):
                act.wait_ge(m.unit_used, n0 + n - RAW + 1)
                hi(n, (rounds + n // RAW + 1) * 16)
            norm_stats(nc, act, m, x, scratch[:], lambda e, t: e.wait_ge(x2_ready, t + 1), stats_b)
            split_act(nc, act, m, h2T, 4, piece, transposed, bank_free, piece_lo, hi_ready, True, 24)

        @block.vector
        def _(dve):
            V = nc.vector
            for w, (gate, gain) in enumerate(((16, 1), (40, 3))):
                m.dve.then(dve, V.tensor_tensor(gcol[:, w, :], m.mod[:, gate:gate + KC], m.gains[:, gain, :],
                                                ALU.mult))
            for c in range(2 * KC):
                V.tensor_scalar(diag[:, c, :], m.ident[:], gcol[:, c // KC, c % KC:c % KC + 1], None, ALU.mult
                                ).then_inc(diag_ready, 1)

            def first_lo():
                for u in range(2):
                    unit_lo(nc, dve, m, raw, hl, u, n0 + u)
            split_dve(nc, dve, catT, piece, cat_hi, cat_lo, first_lo)
            for c in range(4):
                dve.wait_ge(row_ready, c + 1)
                m.dve.then(dve, V.tensor_copy(m.rowg[:, c // 2, (c % 2) * S:(c % 2 + 1) * S], m.psum[c][:]))
            m.dve.then(dve, V.scalar_tensor_tensor(m.scale[:], m.mod[:, 32:40], 1.0, m.gains[:, 2, :],
                                                   ALU.add, ALU.mult))

            def times_gain(g, t, bank):
                dve.wait_ge(squared, g * TT + t + 1)
                return V.tensor_tensor(y[:, t, g], bank, m.rowg[:, 0, g * S:(g + 1) * S], ALU.mult)
            row_units_dve(nc, dve, m, raw, hl, None, n0, e0, 2, None, 2, times_gain)
            V.tensor_tensor(m.ss[:], parts[:, 0], parts[:, 1], ALU.add).then_inc(parts_added, 1)
            dve.wait_ge(stats, 1)
            dve.wait_ge(x_landed, 16)
            m.dve.then(dve, V.reciprocal(m.rstd[:], m.rstd[:]))
            dve.wait_ge(m.unit_evac, e0 + 2 * TT)
            for t in range(TT):
                xt = x[:, t, :].rearrange("p (g n) -> p g n", g=2)
                V.scalar_tensor_tensor(xt, y[:, t], m.rstd[:, t:t + 1], xt, ALU.mult, ALU.add).then_inc(x2_ready, 1)
            norm_rows_dve(nc, dve, m, x, m.rows, stats_b, 1, xn_ready)
            split_dve(nc, dve, h2T, piece, hi_ready, piece_lo)

        @block.tensor
        def _(pe):
            def gain_row(c):
                pe.wait_ge(diag_ready, 4 * c + 4)
                nc.tensor.matmul(m.psum[c][:], m.ones[:], diag[:, 4 * c:4 * c + 4, :].rearrange("p c n -> p (c n)"),
                                 start=True, stop=True).then_inc(row_ready, 1)
            transpose_pe(nc, pe, m, m.rows, 4, None, cat_free, cat_tr, gain_row)
            pe.wait_ge(cat_free, KC)
            row_units_pe(nc, pe, m, hl, n0, e0, 2, cat_lo)
            pe.wait_ge(m.unit_evac, e0 + 2 * TT)
            transpose_pe(nc, pe, m, m.rows, 4, xn_ready, bank_free, transposed)
    m.units += 8
    m.evacs += 8
    m.actT = h2T



ROWS = [(a, 1 + a, TOPK // (a + 1)) for a in range(5)] + [(5, 8, 2), (8, 16, 1)]
NCAND = sum((a1 - a0) * n for a0, a1, n in ROWS)
PRE = 5
ROUNDS = (HJ + PRE * JG) // RAW
assert ROUNDS == PH + 1


def candidate_sums(eng, out, first, second):
    at = 0
    for a0, a1, n in ROWS:
        c = a1 - a0
        o = out[:, :, at:at + c * n].rearrange("p h (a b) -> p h a b", a=c)
        last = eng.tensor_tensor(o, first[:, :, a0:a1].unsqueeze(3).to_broadcast([P, TT, c, n]),
                                 second[:, :, 0:n].unsqueeze(2).to_broadcast([P, TT, c, n]), ALU.add)
        at += c * n
    return last


def stage_select(nc, a, m):
    with ExitStack() as own:
        def sb(name, shape, dt=F32):
            return m.sb(name, shape, dt, own)

        qT = sb("qT", [P, RAW, S])
        keys = sb("keys", [P, HJ * NKEY])
        raw, hl = m.raw, m.hl
        scores = sb("key_scores", [P, HJ, TT * NKEY])
        early = sb("early_acts", [P, 2, S])
        rest = sb("rest", [P, 2 * TT, NKEY])
        v = sb("v", [P, 2 * TT, TOPK])
        vi = sb("vi", [P, 2 * TT, TOPK], U32)
        vf = sb("vf", [P, 2, 2, TT, TOPK])
        cand = sb("cand", [P, TT, NCAND])
        cand2 = sb("cand2", [P, TT, NCAND])
        code = sb("code", [P, 2, TT, NCAND])
        top = sb("top", [P, TT, PH, TOPK])
        best = sb("best", [P, TT, TOPK])
        pos = sb("pos", [P, TT, TOPK], U32)
        posf = sb("posf", [P, TT, TOPK])
        hit = sb("hit", [P, 2, TT * TOPK, NCAND])
        chosen = sb("chosen", [P, TT, PH, TOPK])
        places = sb("places", [P, NCAND])
        room = m.rows[:].rearrange("p t d -> p (t d)")
        n = 3 * TT * PH * TOPK
        slots = room[:, 0:n].rearrange("p (t w n) -> p t w n", t=TT, w=3)
        slots_u = room[:, n:2 * n].bitcast(U32).rearrange("p (w t n) -> p w t n", t=TT, w=3)
        total = sb("total", [P, TT, PH])
        sem = m.sem
        keys_landed = sem("keys_landed")
        scored, scores_read = sem("scored"), sem("scores_read")
        early_stored = [sem("early_stored0"), sem("early_stored1")]
        iota_ready = sem("iota_ready")
        vf_ready, code_ready = sem("vf_ready"), sem("code_ready")
        hit_ready, hit_coded, hit_summed = sem("hit_ready"), sem("hit_coded"), sem("hit_summed")
        shifted, exps = sem("shifted"), sem("exps")
        slots_ready, slots_tr, slots_read = sem("slots_ready"), sem("slots_tr"), sem("slots_read")
        n0, e0 = m.units, m.evacs
        early_units = PRE * JG
        block = own.enter_context(nc.Block())

        @block.sync
        def _(sp):
            sp.dma_start(keys[:], a.keys).then_inc(keys_landed, 16)
            units_load(nc, sp, m, a.w_pq, raw, n0, HJ, done=RAW)

            def body(i, first):
                for u in range(RAW):
                    sp.wait_ge(m.unit_lo, i + (n0 + HJ - RAW + 1 + u))
                    sp.dma_start(raw[:, u, :], a.u[bass.ds(i + u, 1), :, :].rearrange("a p f -> p (a f)")
                                 ).then_inc(m.unit_landed[u], 16)
                    if not (first and u < 2):
                        sp.wait_ge(m.unit_evac, i + (e0 + HJ + u - 1))
                        sp.dma_start(a.early[bass.ds(i + (u - 2), 1), :, :].rearrange("a p f -> p (a f)"),
                                     early[:, u % 2, :]).then_inc(early_stored[u % 2], 16)
            body(0, True)
            with sp.Fori(1, PRE) as k:
                body(k * RAW, False)
            for u in range(2):
                sp.wait_ge(m.unit_evac, e0 + HJ + early_units - 1 + u)
                sp.dma_start(a.early[early_units - 2 + u], early[:, u, :]).then_inc(early_stored[u], 16)
            for u in range(2):
                sp.wait_ge(early_stored[u], 16 * early_units // 2)

        @block.gpsimd
        def _(pool):
            g = nc.gpsimd
            for out, pattern in ((places, [[1, NCAND]]), (m.iota, [[1, NKEY]]), (m.iota_bf, [[1, NKEY], [0, ROUND]])):
                g.iota(out[:], pattern, base=0, channel_multiplier=0,
                       allow_small_or_imprecise_dtypes=True).then_inc(iota_ready, 1)

            def codes(k, b):
                pool.wait_ge(vf_ready, k)
                candidate_sums(g, code[:, b], vf[:, b, 0], vf[:, b, 1]).then_inc(code_ready, 1)
                pool.wait_ge(code_ready, k)
                pool.wait_ge(hit_ready, k)

            def coded(b, half):
                hv = hit[:, b].rearrange("p (t k) c -> p t k c", t=TT)[:, 2 * half:2 * half + 2]
                c = code[:, b, 2 * half:2 * half + 2].unsqueeze(2).to_broadcast([P, 2, TOPK, NCAND])
                g.tensor_tensor(hv, hv, c, ALU.mult).then_inc(hit_coded, 1)

            def low(k, u):
                pool.wait_ge(m.unit_hi, k * RAW + (n0 + u + 1))
                g.tensor_tensor(hl[:, 1, u % m.split, :], raw[:, u, :], hl[:, 0, u % m.split, :].bitcast(F32),
                                ALU.subtract).then_inc(m.unit_lo, 1)

            def round_(k, b, at):
                for u in range(RAW):
                    if u == at:
                        codes(k, b)
                        coded(b, 0)
                    low(k, u)
                    if u == at:
                        coded(b, 1)
            with pool.Fori(0, (ROUNDS - 3) // 2) as r:
                for b in range(2):
                    round_(r * 2 + (b + 1), b, RAW - 1)
            round_(ROUNDS - 2, 0, RAW - 1)
            round_(ROUNDS - 1, 1, 2)

        @block.scalar
        def _(act):
            def hi(i, k, u):
                act.wait_ge(m.unit_landed[u], k * 16 + (n0 // RAW + 1) * 16)
                act.wait_ge(m.unit_used, i + (n0 - m.split + 1 + u))
                nc.scalar.activation(hl[:, 0, u % m.split, :], raw[:, u, :], ACT.Copy).then_inc(m.unit_hi, 1)

            def read_queries(i, u):
                act.wait_ge(m.unit_used, i + (n0 + u + 1))
                nc.scalar.activation(qT[:, u % RAW, :], m.psum[u % 2][:], ACT.Copy).then_inc(m.unit_evac, 1)

            def read_scores(i, u):
                act.wait_ge(scored, i + (u + 1))
                nc.scalar.activation(scores[:, bass.ds(i + u, 1), :].rearrange("p a n -> p (a n)"),
                                     m.psum[2 + u % RAW][:], ACT.Copy).then_inc(scores_read, 1)

            def queries_round(i, k, first):
                for u in range(RAW):
                    if not first:
                        hi(i, k, u)
                    if not (first and u < 1):
                        read_queries(i, u - 1)
                    if not (first and u < 2):
                        read_scores(i, u - 2)
            queries_round(0, 0, True)
            with act.Fori(1, HJ // RAW) as k:
                queries_round(k * RAW, k, False)

            def early_round(i, k, first):
                for u in range(RAW):
                    hi(i + HJ, k + HJ // RAW, u)
                    if first and u < 1:
                        read_queries(HJ, -1)
                    elif not first or u >= 1:
                        act.wait_ge(m.unit_used, i + (n0 + HJ + u))
                        if not (first and u < 3):
                            act.wait_ge(early_stored[(u - 1) % 2], k * 32 + 16 * ((u - 1) // 2))
                        nc.scalar.activation(early[:, (u - 1) % 2, :], m.psum[(u - 1) % 2][:], ACT.Gelu
                                             ).then_inc(m.unit_evac, 1)
                    if first and u < 2:
                        read_scores(HJ, u - 2)
            early_round(0, 0, True)
            with act.Fori(1, PRE - 1) as k:
                early_round(k * RAW, k, False)
            act.wait_ge(shifted, 1)
            nc.scalar.activation(top[:], top[:], ACT.Exp).then_inc(exps, 1)
            early_round((PRE - 1) * RAW, PRE - 1, False)
            act.wait_ge(m.unit_used, n0 + HJ + early_units)
            act.wait_ge(early_stored[1], 16 * (early_units // 2 - 1))
            nc.scalar.activation(early[:, 1, :], m.psum[1][:], ACT.Gelu).then_inc(m.unit_evac, 1)
            for t in range(TT):
                act.wait_ge(slots_tr, t + 1)
                nc.scalar.activation(m.slotsT[:, :, t * P:(t + 1) * P],
                                     m.psum[4 + t][:, 0:3 * P].rearrange("p (w n) -> p w n", w=3), ACT.Copy
                                     ).then_inc(slots_read, 1)
            act.wait_ge(slots_read, TT)

        @block.vector
        def _(dve):
            V = nc.vector
            st = m.dve

            def top16(values, count, replaced, largest, where):
                for r in range(count):
                    last = V.max(largest[:, r, 0:8], values[:, r, :])
                st.then(dve, last)
                for r in range(count):
                    last = V.match_replace(replaced[:, r, :], largest[:, r, 0:8], values[:, r, :], LOWEST)
                st.then(dve, last)
                for r in range(count):
                    V.max_index(where[:, r, 0:8], largest[:, r, 0:8], values[:, r, :])
                for r in range(count):
                    last = V.max(largest[:, r, 8:16], replaced[:, r, :])
                st.then(dve, last)
                for r in range(count):
                    last = V.max_index(where[:, r, 8:16], largest[:, r, 8:16], replaced[:, r, :])
                st.then(dve, last)

            def codes(h):
                dve.wait_ge(hit_coded, 2 * h + 2)
                V.tensor_reduce(chosen[:, :, h, :], hit[:, h % 2].rearrange("p (t k) c -> p t k c", t=TT), AX_X, ALU.add
                                ).then_inc(hit_summed, 1)

            dve.wait_ge(iota_ready, 1)
            for h in range(PH):
                dve.wait_ge(scores_read, 2 * h + 2)
                pair = scores[:, 2 * h:2 * h + 2, :].rearrange("p j (t n) -> p (j t) n", t=TT)
                top16(pair, 2 * TT, rest, v, vi)
                if h >= 2:
                    dve.wait_ge(hit_coded, 2 * h - 2)
                V.tensor_scalar(vf[:, h % 2, 0], vi[:, 0:TT], float(NKEY), None, ALU.mult)
                V.tensor_copy(vf[:, h % 2, 1], vi[:, TT:]).then_inc(vf_ready, 1)
                st.then(dve, candidate_sums(V, cand, v[:, 0:TT], v[:, TT:]))
                top16(cand, TT, cand2, best, pos)
                V.tensor_copy(top[:, :, h, :], best[:])
                st.then(dve, V.tensor_copy(posf[:], pos[:]))
                if h >= 2:
                    codes(h - 2)
                    dve.wait_ge(hit_summed, h - 1)
                V.tensor_tensor(hit[:, h % 2], posf[:].rearrange("p t k -> p (t k)").unsqueeze(2)
                                .to_broadcast([P, TT * TOPK, NCAND]),
                                places[:].unsqueeze(1).to_broadcast([P, TT * TOPK, NCAND]), ALU.is_equal
                                ).then_inc(hit_ready, 1)
            tops = top[:].rearrange("p t h k -> p (t h) k")
            st.then(dve, V.tensor_copy(total[:], top[:, :, :, 0]))
            V.tensor_tensor(tops, tops, total[:].rearrange("p t h -> p (t h)").unsqueeze(2)
                            .to_broadcast([P, TT * PH, TOPK]), ALU.subtract).then_inc(shifted, 1)
            dve.wait_ge(exps, 1)
            st.then(dve, V.tensor_reduce(total[:].rearrange("p t h -> p (t h)"), tops, AX_X, ALU.add))
            st.then(dve, V.reciprocal(total[:], total[:]))
            for t in range(TT):
                V.tensor_tensor(slots[:, t, 2, :].rearrange("p (h k) -> p h k", h=PH), top[:, t],
                                total[:, t].unsqueeze(2).to_broadcast([P, PH, TOPK]), ALU.mult)
            codes(PH - 2)
            codes(PH - 1)
            dve.wait_ge(hit_summed, PH)
            st.then(dve, V.tensor_copy(slots_u[:, 2], chosen[:].rearrange("p t h k -> p t (h k)")))
            V.tensor_scalar(slots_u[:, 0], slots_u[:, 2], 7, None, ALU.logical_shift_right)
            st.then(dve, V.tensor_scalar(slots_u[:, 1], slots_u[:, 2], NKEY - 1, None, ALU.bitwise_and))
            for t in range(TT):
                V.tensor_copy(slots[:, t, 0:2, :], slots_u[:, 0:2, t, :]).then_inc(slots_ready, 1)

        @block.tensor
        def _(pe):
            def unit(i, u, first):
                pe.wait_ge(m.unit_lo, i + (n0 + 1 + u))
                if not (first and u < 2):
                    pe.wait_ge(m.unit_evac, i + (e0 - 1 + u))
                bank = m.psum[u % 2]
                for kc in range(KC):
                    for j, (x, z) in enumerate(PASSES):
                        last = nc.tensor.matmul(bank[:], hl[:, x, u % m.split, kc * P:(kc + 1) * P],
                                                m.actT[:, z, kc, :], start=(kc == 0 and j == 0),
                                                stop=(kc == KC - 1 and j == 2))
                last.then_inc(m.unit_used, 1)

            def score(i, u, first):
                if first:
                    pe.wait_ge(keys_landed, 16)
                pe.wait_ge(m.unit_evac, i + (e0 + 1 + u))
                if not first:
                    pe.wait_ge(scores_read, i + (u + 1 - RAW))
                for t in range(TT):
                    last = nc.tensor.matmul(m.psum[2 + u % RAW][:, t * P:(t + 1) * P],
                                            qT[:, u % RAW, t * P:(t + 1) * P],
                                            keys[:, bass.ds((i + u) * NKEY, NKEY)], start=True, stop=True)
                last.then_inc(scored, 1)

            def queries_round(i, first):
                for u in range(RAW):
                    unit(i, u, first)
                    if not (first and u < 1):
                        score(i, u - 1, first)
            queries_round(0, True)
            with pe.Fori(1, HJ // RAW) as k:
                queries_round(k * RAW, False)
            unit(HJ, 0, False)
            score(HJ, -1, False)
            for u in range(1, RAW):
                unit(HJ, u, False)
            with pe.Fori(HJ // RAW + 1, ROUNDS) as k:
                for u in range(RAW):
                    unit(k * RAW, u, False)
            for t in range(TT):
                pe.wait_ge(slots_ready, t + 1)
                for w in range(3):
                    last = nc.tensor.transpose(m.psum[4 + t][:, w * P:(w + 1) * P], slots[:, t, w, :], m.ident[:])
                last.then_inc(slots_tr, 1)
    m.units += HJ + early_units
    m.evacs += HJ + early_units



ROUND = 8
ACT_ROWS = 2
PER = 4
CHUNKS = ROUND // PER
GATE_PAIRS = S // (2 * TB)
BUFS = 4
DROW = NKEY * S + 1024


def stage_gates(nc, a, m):
    with ExitStack() as own:
        def sb(name, shape, dt=F32):
            return m.sb(name, shape, dt, own)

        slotsT = m.slotsT
        iota, iota_bf = m.iota, m.iota_bf
        first_bf = sb("first_bf", [P, S], BF16)
        hits = sb("first_hits", [P, BUFS, NKEY, ROUND], BF16)
        gate = sb("gate_now", [P, BUFS, ROUND])
        onehot1 = sb("onehot1", [P, BUFS, ROUND, NKEY])
        onehot2 = sb("onehot2", [P, BUFS, ROUND, NKEY])
        gates = sb("gates", [P, 2, NKEY, TB])
        sem = m.sem
        hits_ready, second_ready = sem("hits_ready"), sem("second_ready")
        pool_rows, act_rows = sem("pool_rows"), sem("act_rows")
        gated, gates_read = sem("gated"), sem("gates_read")
        stored = m.stored
        pairs = GATE_PAIRS
        rounds = 2 * TB // ROUND
        pool_n = ROUND - ACT_ROWS
        block = own.enter_context(nc.Block())

        @block.gpsimd
        def _(pool):
            def body(i, first):
                for b in range(rounds):
                    pool.wait_ge(hits_ready, i * rounds + (b + 1))
                    if not (first and b < BUFS):
                        pool.wait_ge(gated, i * (rounds * CHUNKS) + (b + 1 - BUFS) * CHUNKS)
                    n = bass.ds(i * (rounds * ROUND) + b * ROUND, pool_n)
                    nc.gpsimd.tensor_tensor(
                        onehot1[:, b % BUFS, 0:pool_n, :].rearrange("p t k -> p k t"), hits[:, b % BUFS, :, 0:pool_n],
                        slotsT[:, 2, n].unsqueeze(1).to_broadcast([P, NKEY, pool_n]), ALU.mult
                        ).then_inc(pool_rows, 1)
            body(0, True)
            with pool.Fori(1, pairs) as i:
                body(i, False)

        @block.scalar
        def _(act):
            def scale_rows(i, b, first):
                act.wait_ge(hits_ready, i * rounds + (b + 1))
                if not (first and b < BUFS):
                    act.wait_ge(gated, i * (rounds * CHUNKS) + (b + 1 - BUFS) * CHUNKS)
                for u in range(pool_n, ROUND):
                    last = nc.scalar.activation(onehot1[:, b % BUFS, u, :], hits[:, b % BUFS, :, u], ACT.Copy,
                                                scale=gate[:, b % BUFS, u:u + 1])
                last.then_inc(act_rows, 1)

            def read_gates(i, b, first):
                k = b * ROUND // TB % 2
                if not first and b * ROUND % TB == 0:
                    act.wait_ge(stored[k], i * 16)
                for c in range(CHUNKS):
                    act.wait_ge(gated, i * (rounds * CHUNKS) + (b * CHUNKS + c + 1))
                    at = (b * ROUND + c * PER) % TB
                    nc.scalar.activation(gates[:, k, :, at:at + PER],
                                         m.psum[CHUNKS * (b % BUFS) + c][:].rearrange("p (t j) -> p j t", t=PER), ACT.Copy
                                         ).then_inc(gates_read, 1)

            def body(i, first):
                for b in range(rounds):
                    scale_rows(i, b, first)
                    if b >= 1:
                        read_gates(i, b - 1, first)
                    elif not first:
                        read_gates(i - 1, rounds - 1, False)
            body(0, True)
            with act.Fori(1, pairs) as i:
                body(i, False)
            read_gates(pairs - 1, rounds - 1, False)

        @block.sync
        def _(sp):
            for j in range(JG):
                sp.dma_start(m.v_raw[:, j, :], a.v[j]).then_inc(m.early_landed[j], 16)
                sp.dma_start(m.early_in[:, j, :], a.early[j]).then_inc(m.early_landed[j], 16)
            sp.dma_start(m.u_raw[:], a.u[PRE * JG:(PRE + 1) * JG].rearrange("j p d -> p j d")
                         ).then_inc(m.u_landed, 16)
            with sp.Fori(0, pairs) as p:
                for k in range(2):
                    sp.wait_ge(gates_read, p * (2 * TB // PER) + ((k + 1) * (TB // PER)))
                    dst = a.gates[:, 0:NKEY * S].rearrange("p (g n) -> p g n", n=NTB * JG * TB)
                    sp.dma_start(dst[:, 0:GROUPS, bass.ds(p * (2 * JG * TB) + k * JG * TB, JG * TB)],
                                 gates[:, k, :, :].rearrange("p (g j) t -> p g (j t)", j=JG)).then_inc(stored[k], 16)
        @block.vector
        def _(dve):
            V = nc.vector
            m.dve.then(dve, V.tensor_copy(first_bf[:], slotsT[:, 0, :]))

            def body(i, first):
                for b in range(rounds):
                    if not (first and b < BUFS):
                        dve.wait_ge(gated, i * (rounds * CHUNKS) + (b + 1 - BUFS) * CHUNKS)
                    n = bass.ds(i * (rounds * ROUND) + b * ROUND, ROUND)
                    V.tensor_copy(gate[:, b % BUFS, :], slotsT[:, 2, n])
                    V.tensor_tensor(hits[:, b % BUFS], iota_bf[:],
                                    first_bf[:, n].unsqueeze(1).to_broadcast([P, NKEY, ROUND]), ALU.is_equal
                                    ).then_inc(hits_ready, 1)
                    V.tensor_tensor(onehot2[:, b % BUFS], iota[:].unsqueeze(1).to_broadcast([P, ROUND, NKEY]),
                                    slotsT[:, 1, n].unsqueeze(2).to_broadcast([P, ROUND, NKEY]), ALU.is_equal
                                    ).then_inc(second_ready, 1)
            body(0, True)
            with dve.Fori(1, pairs) as i:
                body(i, False)

        @block.tensor
        def _(pe):
            def body(i, first):
                for b in range(rounds):
                    pe.wait_ge(pool_rows, i * rounds + (b + 1))
                    pe.wait_ge(second_ready, i * rounds + (b + 1))
                    for c in range(CHUNKS):
                        if not (first and b < BUFS):
                            pe.wait_ge(gates_read, i * (rounds * CHUNKS) + ((b - BUFS) * CHUNKS + c + 1))
                        if c == pool_n // PER:
                            pe.wait_ge(act_rows, i * rounds + (b + 1))
                        for k in range(PER):
                            u = c * PER + k
                            last = nc.tensor.matmul(m.psum[CHUNKS * (b % BUFS) + c][:, k * NKEY:(k + 1) * NKEY],
                                                    onehot1[:, b % BUFS, u, :], onehot2[:, b % BUFS, u, :],
                                                    start=True, stop=True)
                        last.then_inc(gated, 1)
            body(0, True)
            with pe.Fori(1, pairs) as i:
                body(i, False)



def stage_experts(nc, a, m):
    with ExitStack() as own:
        def sb(name, shape, dt=F32):
            return m.sb(name, shape, dt, own)

        u_raw, v_raw, early = m.u_raw, m.v_raw, m.early_in
        u = sb("u", [P, 2, JG, D], F32R)
        v = sb("v_parts", [P, 2, JG, D], F32R)
        w = sb("w", [P, 2, JG, S], F32R)
        gates = sb("group_gates", [P, NTB, JG, TB])
        act_out = sb("act_out", [P, 2, S])
        weighed = sb("weighed", [P, 2, S])
        waiting = [m.slotsT[:, j, :] for j in range(3)] + [act_out[:, 1, :]]
        y = m.rows
        sem = m.sem
        u_landed, early_landed = m.u_landed, m.early_landed
        v_landed, gates_landed = sem("v_landed"), sem("gates_landed")
        u_hi, u_lo, v_hi, v_lo = sem("u_hi"), sem("u_lo"), sem("v_hi"), sem("v_lo")
        a_done, gelus, weighed_done, w_ready = sem("a_done"), sem("gelus"), sem("weighed_done"), sem("w_ready")
        y_done, y_added = sem("y_done"), sem("y_added")
        weigh_step = sem("weigh_step")
        early_used = sem("early_used")
        squares, stats, out_ready = sem("squares5"), sem("stats5"), sem("out_ready")
        parts_added, gained = sem("parts_added5"), sem("gained")
        parts = sb("sumsq_parts5", [P, 2, TT])
        x2_landed, out_stored = sem("x2_landed"), sem("out_stored")
        pieces = 2 * TT
        block = own.enter_context(nc.Block())

        @block.sync
        def _(sp):
            def load_u(g):
                sp.dma_start(u_raw[:], a.u[bass.ds(g * JG, JG), :, :].rearrange("j p d -> p j d")).then_inc(u_landed, 16)

            def load_v(g):
                sp.dma_start(v_raw[:], a.v[bass.ds(g * JG, JG), :, :].rearrange("j p d -> p j d")).then_inc(v_landed, 16)

            def load_gates(g):
                n = NTB * JG * TB
                sp.dma_start(gates[:].rearrange("p b j t -> p (b j t)"), a.gates[:, bass.ds(g * n, n)]
                             ).then_inc(gates_landed, 16)

            for k in range(2):
                sp.wait_ge(m.stored[k], 16 * GATE_PAIRS)
            load_gates(0)
            with sp.Fori(1, PRE) as g:
                for j in range(JG):
                    sp.wait_ge(v_lo, g * JG + (j + 1 - JG))
                    sp.dma_start(v_raw[:, j, :], a.v[bass.ds(g * JG + j, 1), :, :].rearrange("a p d -> p (a d)")
                                 ).then_inc(early_landed[j], 16)
                    sp.wait_ge(weighed_done, g * JG + (j + 1 - JG))
                    sp.dma_start(early[:, j, :], a.early[bass.ds(g * JG + j, 1), :, :].rearrange("a p s -> p (a s)")
                                 ).then_inc(early_landed[j], 16)
                load_gates(g)
            sp.wait_ge(v_lo, PRE * JG)
            load_v(PRE)
            sp.wait_ge(weighed_done, PRE * JG)
            load_gates(PRE)
            sp.wait_ge(u_lo, JG)
            load_u(PRE + 1)
            with sp.Fori(PRE, GROUPS - 2) as g:
                sp.wait_ge(v_lo, g * JG + JG)
                load_v(g + 1)
                sp.wait_ge(weighed_done, g * JG + JG)
                load_gates(g + 1)
                sp.wait_ge(u_lo, g * JG + (2 - PRE) * JG)
                load_u(g + 2)
            sp.wait_ge(v_lo, (GROUPS - 1) * JG)
            load_v(GROUPS - 1)
            sp.wait_ge(weighed_done, (GROUPS - 1) * JG)
            load_gates(GROUPS - 1)
            sp.wait_ge(u_lo, (GROUPS - PRE) * JG)
            sp.dma_start(u_raw[:], a.x2).then_inc(x2_landed, 16)
            for t in range(TT):
                sp.wait_ge(out_ready, t + 1)
                sp.dma_start(a.out[t * P:(t + 1) * P, :], u_raw[:, t, :]).then_inc(out_stored, 16)
            sp.wait_ge(out_stored, 16 * TT)

        @block.scalar
        def _(act):
            def hi_of_u(g):
                act.wait_ge(u_landed, (g - PRE) * 16 + 16)
                for j in range(JG):
                    nc.scalar.activation(u[:, 0, j, :], u_raw[:, j, :], ACT.Copy).then_inc(u_hi, 1)

            def activations(g, first=False):
                act.wait_ge(v_landed, (g - PRE) * 16 + 16)
                act.wait_ge(y_added, (g - PRE) * pieces + pieces)
                for j in range(JG):
                    nc.scalar.activation(v[:, 0, j, :], v_raw[:, j, :], ACT.Copy).then_inc(v_hi, 1)
                    if first:
                        continue
                    act.wait_ge(a_done, (g - PRE) * JG + (j + 1))
                    if j >= 2:
                        act.wait_ge(weighed_done, g * JG + (j - 1))
                    nc.scalar.activation(act_out[:, j % 2, :], m.psum[j % 2][:], ACT.Gelu).then_inc(gelus, 1)

            def hi_of_v(g, first):
                for j in range(JG):
                    act.wait_ge(early_landed[j], g * 32 + 32)
                    if not first:
                        act.wait_ge(early_used, g * JG + (j + 1 - JG))
                    nc.scalar.activation(v[:, 0, j, :], v_raw[:, j, :], ACT.Copy).then_inc(v_hi, 1)
            hi_of_u(PRE)
            for k in range(2):
                act.wait_ge(m.stored[k], 16 * GATE_PAIRS)
            hi_of_v(0, True)
            for j in range(JG):
                act.wait_ge(a_done, j + 1)
                nc.scalar.activation(waiting[j], m.psum[j][:], ACT.Gelu).then_inc(gelus, 1)
            with act.Fori(1, PRE) as g:
                hi_of_v(g, False)
            for p in range(0, pieces, 2):
                t, half = p % TT, p // TT
                act.wait_ge(early_used, PRE * JG)
                nc.scalar.activation(y[:, t, half * S:(half + 1) * S], m.psum[p][:], ACT.Copy).then_inc(y_added, 1)
            activations(PRE, True)
            hi_of_u(PRE + 1)
            with act.Fori(PRE + 1, GROUPS - 1) as g:
                activations(g)
                hi_of_u(g + 1)
            activations(GROUPS - 1)
            done = (GROUPS - PRE) * pieces
            for p in range(pieces):
                t, half = p % TT, p // TT
                act.wait_ge(y_added, done + p + 1)
                nc.scalar.activation(v_raw[:, p % JG, 0:S], y[:, t, half * S:(half + 1) * S], ACT.Square,
                                     accum_out=parts[:, half, t:t + 1]).then_inc(squares, 1)
                act.wait_ge(squares, p + 1)
            act.wait_ge(parts_added, 1)
            nc.scalar.activation(m.rstd[:], m.ss[:], ACT.Sqrt, bias=m.eps[:, 0:1], scale=1.0 / D).then_inc(stats, 1)

        @block.vector
        def _(dve):
            V = nc.vector

            def lo_of_u(g):
                for j in range(JG):
                    dve.wait_ge(u_hi, (g - PRE) * JG + (j + 1))
                    V.tensor_tensor(u[:, 1, j, :], u_raw[:, j, :], u[:, 0, j, :].bitcast(F32), ALU.subtract
                                    ).then_inc(u_lo, 1)

            def weigh(g, acts, ready):
                dve.wait_ge(gates_landed, g * 16 + 16)
                for j in range(JG):
                    dve.wait_ge(v_hi, g * JG + (j + 1))
                    V.tensor_tensor(v[:, 1, j, :], v_raw[:, j, :], v[:, 0, j, :].bitcast(F32), ALU.subtract
                                    ).then_inc(v_lo, 1)
                    ready(j)
                    V.tensor_tensor(weighed[:, j % 2, :].rearrange("p (b t) -> p b t", t=TB),
                                    acts(j).rearrange("p (b t) -> p b t", t=TB), gates[:, :, j, :],
                                    ALU.mult).then_inc(weighed_done, 1)
                    dve.wait_ge(weighed_done, g * JG + (j + 1))
                    V.tensor_copy(w[:, 0, j, :], weighed[:, j % 2, :]).then_inc(weigh_step, 1)
                    dve.wait_ge(weigh_step, g * JG + (j + 1))
                    V.tensor_tensor(w[:, 1, j, :], weighed[:, j % 2, :], w[:, 0, j, :].bitcast(F32), ALU.subtract
                                    ).then_inc(w_ready, 1)

            def weigh_early(g):
                weigh(g, lambda j: early[:, j, :], lambda j: dve.wait_ge(early_landed[j], g * 32 + 32))

            def weigh_late(g):
                weigh(g, lambda j: act_out[:, j % 2, :], lambda j: dve.wait_ge(gelus, (g - PRE) * JG + (j + 1)))

            def add(g, last=False):
                for p in range(pieces):
                    t, half = p % TT, p // TT
                    dve.wait_ge(y_done, (g - PRE) * pieces + (p + 1))
                    part = y[:, t, half * S:(half + 1) * S]
                    V.tensor_tensor(part, part, m.psum[2 + p % 6][:], ALU.add).then_inc(y_added, 1)
                    if last and p >= 1:
                        times_gain(p - 1)
                if last:
                    times_gain(pieces - 1)

            def times_gain(p):
                t, half = p % TT, p // TT
                dve.wait_ge(squares, p + 1)
                part = y[:, t, half * S:(half + 1) * S]
                V.tensor_tensor(part, part, m.rowg[:, 1, half * S:(half + 1) * S], ALU.mult).then_inc(gained, 1)
            lo_of_u(PRE)
            with dve.Fori(0, PRE) as g:
                weigh_early(g)
            for p in range(1, pieces, 2):
                t, half = p % TT, p // TT
                dve.wait_ge(early_used, PRE * JG)
                V.tensor_copy(y[:, t, half * S:(half + 1) * S], m.psum[p][:]).then_inc(y_added, 1)
            dve.wait_ge(y_added, pieces)
            weigh(PRE, lambda j: waiting[j], lambda j: dve.wait_ge(gelus, j + 1))
            lo_of_u(PRE + 1)
            add(PRE)
            with dve.Fori(PRE + 1, GROUPS - 1) as g:
                weigh_late(g)
                lo_of_u(g + 1)
                add(g)
            weigh_late(GROUPS - 1)
            add(GROUPS - 1, True)
            V.tensor_tensor(m.ss[:], parts[:, 0], parts[:, 1], ALU.add).then_inc(parts_added, 1)
            dve.wait_ge(stats, 1)
            m.dve.then(dve, V.reciprocal(m.rstd[:], m.rstd[:]))
            dve.wait_ge(x2_landed, 16)
            dve.wait_ge(gained, pieces)
            for t in range(TT):
                V.scalar_tensor_tensor(u_raw[:, t, :], y[:, t, :], m.rstd[:, t:t + 1], u_raw[:, t, :], ALU.mult,
                                       ALU.add).then_inc(out_ready, 1)

        @block.tensor
        def _(pe):
            def activate(g, banks):
                for j in range(JG):
                    pe.wait_ge(u_lo, (g - PRE) * JG + (j + 1))
                    if j >= banks:
                        pe.wait_ge(gelus, (g - PRE) * JG + (j - 1))
                    for kc in range(KC):
                        for i, (p, q) in enumerate(PASSES):
                            last = nc.tensor.matmul(m.psum[j % banks][:], u[:, p, j, kc * P:(kc + 1) * P],
                                                    m.actT[:, q, kc, :], start=(kc == 0 and i == 0),
                                                    stop=(kc == KC - 1 and i == 2))
                    last.then_inc(a_done, 1)

            def early_units(g, first, final):
                for j in range(JG):
                    pe.wait_ge(v_lo, g * JG + (j + 1))
                    pe.wait_ge(w_ready, g * JG + (j + 1))
                    if first and j == 0:
                        pe.wait_ge(gelus, JG)
                    for p in range(pieces):
                        t, half = p % TT, p // TT
                        for i, (x, z) in enumerate(PASSES):
                            last = nc.tensor.matmul(m.psum[p][:], w[:, x, j, t * P:(t + 1) * P],
                                                    v[:, z, j, half * S:(half + 1) * S],
                                                    start=(first and j == 0 and i == 0),
                                                    stop=(final and j == JG - 1 and i == 2))
                    last.then_inc(early_used, 1)

            def weighed_sum(g):
                def piece(p, j):
                    t, half = p % TT, p // TT
                    for i, (x, z) in enumerate(PASSES):
                        last = nc.tensor.matmul(m.psum[2 + p % 6][:], w[:, x, j, t * P:(t + 1) * P],
                                                v[:, z, j, half * S:(half + 1) * S], start=(j == 0 and i == 0),
                                                stop=(j == JG - 1 and i == 2))
                    if j == JG - 1:
                        last.then_inc(y_done, 1)
                pe.wait_ge(y_added, (g - PRE) * pieces + pieces)
                for j in range(JG):
                    pe.wait_ge(v_lo, g * JG + (j + 1))
                    pe.wait_ge(w_ready, g * JG + (j + 1))
                    for p in range(TT):
                        piece(p, j)
                for p in range(TT, pieces):
                    if p >= 6:
                        pe.wait_ge(y_added, (g - PRE) * pieces + (pieces + p - 5))
                    for j in range(JG):
                        piece(p, j)
            activate(PRE, JG)
            early_units(0, True, False)
            with pe.Fori(1, PRE - 1) as g:
                early_units(g, False, False)
            early_units(PRE - 1, False, True)
            weighed_sum(PRE)
            with pe.Fori(PRE + 1, GROUPS) as g:
                activate(g, 2)
                weighed_sum(g)



def kernel(**inputs):
    import numpy as np
    import concourse.bacc as bacc
    from concourse.bass_utils import run_bass_kernel_spmd

    def get(name):
        return np.asarray(inputs[name])

    def columns(w):
        n = w.shape[1] // P
        return w.reshape(KC, P, n, P).transpose(2, 1, 0, 3).reshape(n, P, KC * P)

    def rows(w):
        n = w.shape[1] // S
        return w.reshape(KC // 2, 2, P, n, S).transpose(3, 0, 2, 1, 4).reshape(n * KC // 2, P, 2 * S)

    def by_partition(vec):
        return vec.reshape(-1, P).T

    w_in, w_ada = get("w_in")[0], get("w_ada")[0]
    parts = [w_in[:, i * S:(i + 1) * S] for i in range(7)]
    theta = get("lb_theta")
    arrays = {
        "x": get("x")[0],
        "c": by_partition(get("c")[0]),
        "w_ada": w_ada.reshape(KC, P, 48 // ADA, ADA, P).transpose(2, 1, 3, 0, 4),
        "b_ada": by_partition(get("b_ada")[0]),
        "gains": np.stack([by_partition(get(n)[0]) for n in ("g_pre_mix", "g_post_mix", "g_pre_ffn", "g_post_ffn")],
                          axis=1),
        "w_cols": np.concatenate([columns(parts[i]) for i in (0, 1, 3, 4)]),
        "w_rows": np.concatenate([rows(parts[i]) for i in (2, 5, 6)]),
        "small": np.concatenate([np.tile(get("lam_qk")[0].reshape(1, -1), (P, 1)), by_partition(theta[0]),
                                 by_partition(theta[1]), np.tile(get("g_diff_sub"), (P, 1)),
                                 np.tile(get("g_hgrn_out"), (P, 1))], axis=1),
        "w_out": rows(get("w_out")[0]),
        "w_pq": columns(get("w_pq")[0]),
        "keys": get("sub_keys")[0].transpose(3, 0, 1, 2).reshape(P, HJ * NKEY),
        "u": get("expert_u")[0].reshape(NKEY, NKEY, KC, P).transpose(1, 3, 2, 0).reshape(NKEY, P, D),
        "v": get("expert_v")[0].reshape(NKEY, NKEY, D).transpose(1, 0, 2),
    }
    nc = bacc.Bacc("TRN2", target_bir_lowering=False, num_devices=1)
    a = Memory()
    for name, value in arrays.items():
        arrays[name] = value = np.ascontiguousarray(value)
        a.__dict__[name] = nc.dram_tensor(f"in_{name}", value.shape, F32, kind="ExternalInput").ap()
    a.x2 = nc.dram_tensor("x2", (P, TT, D), F32).ap()
    a.early = nc.dram_tensor("early_activations", (PRE * JG, P, S), F32).ap()
    a.gates = nc.dram_tensor("expert_gates", (P, DROW), F32).ap()
    a.out = nc.dram_tensor("out", (S, D), F32, kind="ExternalOutput").ap()
    build(nc, a)
    r = run_bass_kernel_spmd(nc, [{f"in_{k}": v for k, v in arrays.items()}], core_ids=[0])
    return r.results[0]["out"].reshape(1, S, D)
```
